# Optimizing a Trainium2 kernel written in Bass

```python
import jax, jax.numpy as jnp
from jax import lax
import numpy as np

D_MODEL = 1024
BATCH = 1
SEQ = 1024
DEPTH = 1

GRID_W = 64
CTX_LEN = 256
CONV_W = 1024
RET_HEADS = 4
RET_DK = 256
RET_DV = 512
RET_QK = RET_HEADS * RET_DK
RET_V = RET_HEADS * RET_DV
RET_CHUNK = 128
ROPE_PAIRS = RET_DK // 4
ROPE_BASE = 10000.0
D_FF = 2816
N_MOD = 6
EPS = 1e-6

OFF_CX = 0
OFF_CB = OFF_CX + CONV_W
OFF_CC = OFF_CB + CONV_W
OFF_Q = OFF_CC + CONV_W
OFF_K = OFF_Q + RET_QK
OFF_V = OFF_K + RET_QK
OFF_G = OFF_V + RET_V
OFF_GA = OFF_G + RET_V
OFF_GB = OFF_GA + D_MODEL
IN_COLS = OFF_GB + D_MODEL

kernel_name = 'hybrid_conv_retention_diffusion_block'

def rms_norm(x, gain):
    xf = x.astype(jnp.float32)
    y = xf * lax.rsqrt(jnp.mean(xf * xf, axis=-1, keepdims=True) + EPS)
    return y.astype(x.dtype) * gain

def dwconv3(x, w, b, axis):
    n = x.shape[axis]
    pad = [(0, 0)] * x.ndim
    pad[axis] = (1, 1)
    xp = jnp.pad(x, pad)
    return (w[0] * lax.slice_in_dim(xp, 0, n, axis=axis)
            + w[1] * lax.slice_in_dim(xp, 1, n + 1, axis=axis)
            + w[2] * lax.slice_in_dim(xp, 2, n + 2, axis=axis) + b)

def grid_conv(x, w, b, axis):
    bsz, n, ch = x.shape
    rows = n // GRID_W
    xg = x.reshape(bsz, rows, GRID_W, ch)
    return dwconv3(xg, w, b, axis).reshape(bsz, n, ch)

def conv_along_rows(x, w, b):
    return grid_conv(x, w, b, 2)

def conv_along_cols(x, w, b):
    return grid_conv(x, w, b, 1)

def conv_along_seq(x, w, b):
    return dwconv3(x, w, b, 1)

def rotary_tables(n):
    t = jnp.arange(n)
    row = (t // GRID_W).astype(jnp.float32)
    col = (t % GRID_W).astype(jnp.float32)
    inv = ROPE_BASE ** (-jnp.arange(ROPE_PAIRS, dtype=jnp.float32) / ROPE_PAIRS)
    ang = jnp.concatenate([row[:, None] * inv, col[:, None] * inv], axis=-1)
    return jnp.cos(ang), jnp.sin(ang)

def apply_rotary(t, cos, sin):
    half = RET_DK // 2
    t1, t2 = t[..., :half], t[..., half:]
    return jnp.concatenate([t1 * cos - t2 * sin, t2 * cos + t1 * sin], axis=-1)

def to_heads(t, dh):
    bsz, n, _ = t.shape
    return t.reshape(bsz, n, RET_HEADS, dh).transpose(0, 2, 1, 3).astype(jnp.float32)

def flip_seq(t):
    return jnp.flip(t, axis=2)

def retention_scan(q, k, v, log_gamma, s0, strict):
    bsz, nh, n, dk = q.shape
    nc = n // RET_CHUNK
    idx = jnp.arange(RET_CHUNK, dtype=jnp.float32)
    diff = idx[:, None] - idx[None, :]
    mask = diff > 0 if strict else diff >= 0
    dmat = jnp.where(mask, jnp.exp(jnp.where(mask, diff, 0.0)[None] * log_gamma[:, None, None]), 0.0)
    xi = jnp.exp((idx + 1.0)[None, :] * log_gamma[:, None])
    zeta = jnp.exp((RET_CHUNK - 1.0 - idx)[None, :] * log_gamma[:, None])
    chunk_decay = jnp.exp(RET_CHUNK * log_gamma)

    def to_chunks(t):
        return jnp.moveaxis(t.reshape(bsz, nh, nc, RET_CHUNK, t.shape[-1]), 2, 0)

    def step(s, qkv):
        qc, kc, vc = qkv
        scores = jnp.einsum('bhnd,bhmd->bhnm', qc, kc) * dmat
        o = (jnp.einsum('bhnm,bhmv->bhnv', scores, vc)
             + jnp.einsum('bhnd,bhdv->bhnv', qc * xi[..., None], s))
        s = chunk_decay[:, None, None] * s + jnp.einsum('bhmd,bhmv->bhdv', kc * zeta[..., None], vc)
        return s, o

    s_final, o = lax.scan(step, s0, (to_chunks(q), to_chunks(k), to_chunks(v)))
    o = jnp.moveaxis(o, 0, 2).reshape(bsz, nh, n, v.shape[-1])
    return o, s_final

def context_states(kc, vc, lg_fw, lg_bw):
    lc = kc.shape[2]
    m = jnp.arange(lc, dtype=jnp.float32)
    w_fw = jnp.exp((lc - 1.0 - m)[None, :] * lg_fw[:, None])
    w_bw = jnp.exp(m[None, :] * lg_bw[:, None])
    s_fw = jnp.einsum('bhmd,hm,bhmv->bhdv', kc, w_fw, vc)
    s_bw = jnp.einsum('bhmd,hm,bhmv->bhdv', kc, w_bw, vc)
    return s_fw, s_bw

def mixer_branches(p, q, k, v, s_fw, s_bw, lg_fw, lg_bw, conv_w, conv_b, w_conv_out, w_ret_out, w_o, conv_fn):
    y_conv = (p[..., OFF_CB:OFF_CC]
              * conv_fn(p[..., OFF_CC:OFF_Q] * p[..., OFF_CX:OFF_CB], conv_w, conv_b)) @ w_conv_out
    o_fw, _ = retention_scan(q, k, v, lg_fw, s_fw, False)
    o_bw, _ = retention_scan(flip_seq(q), flip_seq(k), flip_seq(v), lg_bw, s_bw, True)
    o = o_fw + flip_seq(o_bw)
    o = o * lax.rsqrt(jnp.mean(o * o, axis=-1, keepdims=True) + EPS)
    bsz, _, n, _ = o.shape
    o = o.transpose(0, 2, 1, 3).reshape(bsz, n, RET_V).astype(p.dtype)
    y_ret = (jax.nn.silu(p[..., OFF_G:OFF_GA]) * o) @ w_ret_out
    merged = (jax.nn.sigmoid(p[..., OFF_GA:OFF_GB]) * y_conv
              + jax.nn.sigmoid(p[..., OFF_GB:IN_COLS]) * y_ret)
    return merged @ w_o

def conv_ffn(h, w_up, conv_w, conv_b, w_down, conv_fn):
    u = conv_fn(h @ w_up, conv_w, conv_b)
    return (jax.nn.silu(u[..., :D_FF]) * u[..., D_FF:]) @ w_down

def setup_inputs(seed: int = 0) -> dict:
    key = jax.random.key(seed)
    ks = jax.random.split(key, 22)

    def nrm(k, shape, scale):
        return jax.random.normal(k, shape, jnp.float32) * scale

    L = DEPTH
    D = D_MODEL
    theta0 = jnp.log(2.0 ** (5.0 + jnp.arange(RET_HEADS, dtype=jnp.float32)) - 1.0)
    return {
        'x': nrm(ks[0], (BATCH, SEQ, D), 1.0),
        'c': nrm(ks[1], (BATCH, D), 1.0),
        'ctx': nrm(ks[2], (BATCH, CTX_LEN, D), 1.0),
        'c_ctx': nrm(ks[3], (D,), 1.0),
        'w_ada': nrm(ks[4], (L, D, N_MOD * D), D ** -0.5),
        'b_ada': nrm(ks[5], (L, N_MOD * D), 0.01),
        'norm_mix_pre': 1.0 + nrm(ks[6], (L, D), 0.02),
        'norm_mix_post': 1.0 + nrm(ks[7], (L, D), 0.02),
        'w_in': nrm(ks[8], (L, D, IN_COLS), D ** -0.5),
        'conv_w': nrm(ks[9], (L, 3, CONV_W), 3 ** -0.5),
        'conv_b': nrm(ks[10], (L, CONV_W), 0.01),
        'w_conv_out': nrm(ks[11], (L, CONV_W, D), CONV_W ** -0.5),
        'ret_decay_fw': theta0 + nrm(ks[12], (L, RET_HEADS), 0.05),
        'ret_decay_bw': theta0 + nrm(ks[13], (L, RET_HEADS), 0.05),
        'w_ret_out': nrm(ks[14], (L, RET_V, D), RET_V ** -0.5),
        'w_o': nrm(ks[15], (L, D, D), D ** -0.5),
        'norm_ffn_pre': 1.0 + nrm(ks[16], (L, D), 0.02),
        'norm_ffn_post': 1.0 + nrm(ks[17], (L, D), 0.02),
        'w_ffn_up': nrm(ks[18], (L, D, 2 * D_FF), D ** -0.5),
        'ffn_conv_w': nrm(ks[19], (L, 3, 2 * D_FF), 3 ** -0.5),
        'ffn_conv_b': nrm(ks[20], (L, 2 * D_FF), 0.01),
        'w_ffn_down': nrm(ks[21], (L, D_FF, D), D_FF ** -0.5),
    }

def reference(x, c, ctx, c_ctx, w_ada, b_ada, norm_mix_pre, norm_mix_post, w_in, conv_w, conv_b,
              w_conv_out, ret_decay_fw, ret_decay_bw, w_ret_out, w_o, norm_ffn_pre, norm_ffn_post,
              w_ffn_up, ffn_conv_w, ffn_conv_b, w_ffn_down):
    bsz, n, _ = x.shape
    rows = n // GRID_W
    cos, sin = rotary_tables(rows * GRID_W)
    xc = ctx
    for layer in range(DEPTH):
        update_ctx = layer + 1 < DEPTH
        mod = (jax.nn.silu(c) @ w_ada[layer] + b_ada[layer]).reshape(bsz, N_MOD, 1, D_MODEL)
        mod_c = (jax.nn.silu(c_ctx) @ w_ada[layer] + b_ada[layer]).reshape(N_MOD, D_MODEL)
        lg_fw = jax.nn.log_sigmoid(ret_decay_fw[layer].astype(jnp.float32))
        lg_bw = jax.nn.log_sigmoid(ret_decay_bw[layer].astype(jnp.float32))

        h = rms_norm(x, norm_mix_pre[layer]) * (1.0 + mod[:, 1]) + mod[:, 0]
        hc = rms_norm(xc, norm_mix_pre[layer]) * (1.0 + mod_c[1]) + mod_c[0]
        if update_ctx:
            pc = hc @ w_in[layer]
            pc_kv = pc[..., OFF_K:OFF_G]
        else:
            pc_kv = hc @ w_in[layer][:, OFF_K:OFF_G]
        kc = to_heads(pc_kv[..., :RET_QK], RET_DK) * RET_DK ** -0.5
        vc = to_heads(pc_kv[..., RET_QK:], RET_DV)
        s_fw, s_bw = context_states(kc, vc, lg_fw, lg_bw)

        p = h @ w_in[layer]
        q = apply_rotary(to_heads(p[..., OFF_Q:OFF_K], RET_DK), cos, sin)
        k = apply_rotary(to_heads(p[..., OFF_K:OFF_V], RET_DK), cos, sin) * RET_DK ** -0.5
        v = to_heads(p[..., OFF_V:OFF_G], RET_DV)
        y = mixer_branches(p, q, k, v, s_fw, s_bw, lg_fw, lg_bw, conv_w[layer], conv_b[layer],
                           w_conv_out[layer], w_ret_out[layer], w_o[layer], conv_along_rows)
        if update_ctx:
            zero_state = jnp.zeros_like(s_fw)
            qc = to_heads(pc[..., OFF_Q:OFF_K], RET_DK)
            yc = mixer_branches(pc, qc, kc, vc, zero_state, zero_state, lg_fw, lg_bw, conv_w[layer],
                                conv_b[layer], w_conv_out[layer], w_ret_out[layer], w_o[layer],
                                conv_along_seq)
            xc = xc + mod_c[2] * rms_norm(yc, norm_mix_post[layer])
        x = x + mod[:, 2] * rms_norm(y, norm_mix_post[layer])

        h = rms_norm(x, norm_ffn_pre[layer]) * (1.0 + mod[:, 4]) + mod[:, 3]
        f = conv_ffn(h, w_ffn_up[layer], ffn_conv_w[layer], ffn_conv_b[layer], w_ffn_down[layer],
                     conv_along_cols)
        x = x + mod[:, 5] * rms_norm(f, norm_ffn_post[layer])
        if update_ctx:
            hc = rms_norm(xc, norm_ffn_pre[layer]) * (1.0 + mod_c[4]) + mod_c[3]
            fc = conv_ffn(hc, w_ffn_up[layer], ffn_conv_w[layer], ffn_conv_b[layer],
                          w_ffn_down[layer], conv_along_seq)
            xc = xc + mod_c[5] * rms_norm(fc, norm_ffn_post[layer])
    return x


_drawn_inputs = setup_inputs


def setup_inputs(seed=0):
    import zlib

    import numpy as np

    out = dict(_drawn_inputs(seed))
    spreads = {}
    factors = {'ctx': 12.987,
     'b_ada': 3.014,
     'norm_mix_pre': 2.994,
     'norm_mix_post': 5.039,
     'conv_b': 59.705,
     'norm_ffn_pre': 13.175,
     'norm_ffn_post': 21.914,
     'ffn_conv_b': 28.979,
     'c_ctx': 5.859}
    for name, (base, spread) in spreads.items():
        noise = np.random.default_rng([zlib.crc32(name.encode()), seed]).standard_normal(out[name].shape)
        drawn = base * np.exp(spread * noise) if base else spread * noise
        out[name] = __import__('jax').numpy.asarray(drawn.astype(out[name].dtype))
    for name, factor in factors.items():
        out[name] = (out[name] * factor).astype(out[name].dtype)
    return out
```

```python
import math

import numpy as np

import concourse.bass as bass
from concourse import mybir

F32 = mybir.dt.float32
F32R = mybir.dt.float32r
ACT = mybir.ActivationFunctionType
ALU = mybir.AluOpType

START = 256

P = 128
D = 1024
T = 1024
CTX = 256
GRID = 64
KT = D // P
NCH = T // P
NCX = CTX // P
HALF = 512
HEADS = 4
DK, DV = 256, 512
FF = 2816
FT = FF // P
EPS = 1e-6
K_SCALE = 1.0 / math.sqrt(DK)

V_C, V_CC, V_BADA = 0, 8, 16
V_GMIX, V_GPOST, V_GFFN, V_GFPOST = 64, 72, 80, 88
V_CW, V_CB = 96, 120
V_FW, V_FB = 128, 260
V_DEC = 304
V_N = 312

C_ID, C_DPOS, C_DNEG, C_GE, C_LT, C_RF, C_RB = 0, 128, 256, 384, 512, 640, 768
C_COLF, C_COLB = 896, 900
C_N = 904

H_D, H_XF, H_XB, H_F, H_B = 0, 128, 256, 384, 388
H_N = 392

R_CTX = 0
R_QK = R_CTX + 24
R_VG = R_QK + 16
R_CONV = R_VG + 32
R_GATE = R_CONV + 24
R_CO = R_GATE + 16
R_A = R_CO + 8
R_B = R_A + 16
R_C = R_B + 16
R_WO = R_C + 8
R_UP = R_WO + 8
R_END = R_UP + 2 * FT

P_CTX = 0
P_QK = P_CTX + 6 * 5
P_VG = P_QK + 16
P_CONV = P_VG + 8 * 11
P_GATE = P_CONV + 24
P_A = P_GATE + 16
P_B = P_A + 8
P_C = P_B + 8
P_UP = P_C + 8

ST_KVC = 0
ST_QK = ST_KVC + 6
ST_VG = ST_QK + 2 * HEADS
ST_CO = ST_VG + 8 * NCH
ST_GATE = ST_CO + KT
ST_GO = ST_GATE + 2 * KT
ST_X1 = ST_GO + HEADS * NCH
ST_A = ST_X1 + NCH

ADA_RING = 4
CONV_PAIR = (0, 1, 2, 3, 0, 1)
N_DOWN = FT - 1 + NCH

N_U = 4 + 2 * 2 * (NCH - 1)
KZ_B, KZ_END = [], []
for _m in range(NCH):
    _n = KZ_END[-1] if KZ_END else 0
    KZ_B.append(_n + 1)
    KZ_END.append(_n + (_m < NCH - 1) + (_m > 0))
N_KZ = KZ_END[-1]

Y_COUNT = {}
for _c in range(NCH + 1):
    for _step, _of in (("inv1", _c), ("z", _c), ("scale", _c - 1), ("shift", _c - 1), ("inv2", _c)):
        if 0 <= _of < NCH:
            Y_COUNT[_step, _of] = len(Y_COUNT) + 1

DC_T, DC_AZ, DC_U, DC_W, DC_LN, DC_CORR, DC_RW, DC_LG = range(8)


def build(nc, io):
    ps = nc.alloc_psum_tensor("ps", [P, 8, HALF], F32)

    def pair(n):
        return ps[:, 2 * n:2 * n + 2, :].rearrange("p b c -> p (b c)")

    kb = 1024
    PERS = 16640
    RING = PERS + 12 * kb
    X0 = RING + 24 * kb
    X1 = X0 + 64 * kb
    REST = X1 + 64 * kb
    end = nc.sbuf_usable_end
    top = [0]

    def sb(name, shape, at, dt=F32):
        size = 4 * int(np.prod(shape[1:]))
        assert at + size <= end, (name, at + size, end)
        top[0] = at + size
        return nc.alloc_sbuf_tensor_at(name, shape, dt, offset=at)

    def after(align=32):
        return -(-top[0] // align) * align

    vec = sb("vec", [P, V_N], PERS)
    ident = sb("ident", [P, P], after())
    ones = sb("ones", [P, P], after())
    silu_c = sb("silu_c", [P, KT, 2], after())
    mod_a = sb("mod_a", [P, 16, 2], after())
    mod_b = sb("mod_b", [P, 32], after())
    scale_x = sb("scale_x", [P, KT, 2], after())
    scale_h = sb("scale_h", [P, KT], after())
    gain_y = sb("gain_y", [P, KT], after())
    gain_f = sb("gain_f", [P, KT], after())
    head_tab = sb("head_tab", [P, HEADS, H_N], after())
    ssum = sb("ssum", [P, 10], after())
    root = sb("root", [P, 10], after())
    rinv = sb("rinv", [P, 10], after())
    dec = sb("dec", [P, 8, 8], after())
    onum = sb("onum", [P, 2, 4], after())
    eps = sb("eps", [P, 1], after())
    st1 = sb("st1", [P, 8, 4], after())
    st2 = sb("st2", [P, 8, 4], after())
    assert top[0] <= RING, top[0] - RING

    raw = [sb(f"raw{n}", [P, 1024], RING + 4096 * n) for n in range(2)]
    w_hi = [sb(f"w_hi{n}", [P, 1024], RING + 8192 + 4096 * n, F32R) for n in range(2)]
    w_lo = [sb(f"w_lo{n}", [P, 1024], RING + 16384 + 4096 * n, F32R) for n in range(2)]

    x0_hi = sb("x0_hi", [P, KT, T], X0, F32R)
    x0_lo = sb("x0_lo", [P, KT, T], X0 + 32 * kb, F32R)
    x1_hi = sb("x1_hi", [P, KT, T], X1, F32R)
    x1_lo = sb("x1_lo", [P, KT, T], X1 + 32 * kb, F32R)

    hc_hi = sb("hc_hi", [P, KT, CTX], X1, F32R)
    hc_lo = sb("hc_lo", [P, KT, CTX], after(), F32R)
    x_in = sb("x_in", [P, 10, D], after())
    xn = [sb(f"xn{n}", [P, D], REST + 4096 * n) for n in range(2)]
    aff = [sb(f"aff{n}", [P, D], REST + 8192 + 4096 * n) for n in range(2)]
    junk = sb("junk", [P, D], REST + 16384)
    const = sb("const", [P, C_N], REST + 20480)
    ada_raw = [sb(f"ada_raw{n}", [P, 1024], REST + 24576 + 4096 * n) for n in range(4)]
    dtmp = sb("dtmp", [P, HEADS, P], after())
    ctx_out = [sb(f"ctx_out{n}", [P, NCX, HALF], X1 + 56 * kb + 4096 * n) for n in range(2)]

    cos = sb("cos", [P, T], X1)
    sin = sb("sin", [P, T], X1 + 4 * kb)
    rot_a = [sb(f"rot_a{n}", [P, 2, T], X1 + (8 + 8 * n) * kb) for n in range(2)]
    rot_b = [sb(f"rot_b{n}", [P, 2, T], X1 + (24 + 8 * n) * kb) for n in range(2)]
    rot_o = [sb(f"rot_o{n}", [P, 2, T], X1 + (40 + 8 * n) * kb) for n in range(2)]
    vg_out = [sb(f"vg_out{n}", [P, HALF], REST + 2048 * n) for n in range(8)]
    cx = [sb(f"cx{n}", [P, T], X1 + (0 + 16 * n) * kb) for n in range(2)]
    cprod = [sb(f"cprod{n}", [P, T], X1 + (4 + 16 * n) * kb) for n in range(2)]
    cy = [sb(f"cy{n}", [P, T], X1 + (8 + 16 * n) * kb) for n in range(2)]
    co = [sb(f"co{n}", [P, T], X1 + (12 + 16 * n) * kb) for n in range(2)]
    gate_o = [sb(f"gate_o{n}", [P, T], X1 + (32 + 4 * n) * kb) for n in range(2)]

    at = X0
    q_t = [sb(f"q_t{n}", [P, 2, T], at + n * 8 * kb) for n in range(2)]
    at += 16 * kb
    k_t = [sb(f"k_t{n}", [P, 2, T], at + n * 8 * kb) for n in range(2)]
    at += 16 * kb
    v_n = [sb(f"v_n{n}", [P, NCH, DV], at + n * 16 * kb) for n in range(2)]
    at += 32 * kb
    kc_n = [sb(f"kc_n{n}", [P, NCX, DK], at + n * 2 * kb) for n in range(2)]
    at += 4 * kb
    vc_n = [sb(f"vc_n{n}", [P, NCX, DV], at + n * 4 * kb) for n in range(2)]
    at += 8 * kb
    s_bw = sb("s_bw", [P, NCH, 2, DV], at)
    at += 32 * kb
    s_fw = sb("s_fw", [P, 2, 2, DV], at)
    at += 8 * kb
    kz_f = sb("kz_f", [P, NCH, DK], at)
    at += 8 * kb
    kz_b = sb("kz_b", [P, 2, DK], at)
    at += 2 * kb
    q_f = sb("q_f", [P, 2, T], at)
    at += 8 * kb
    q_b = sb("q_b", [P, 2, T], at)
    at += 8 * kb
    kcw_f = sb("kcw_f", [P, NCX, DK], at)
    kcw_b = sb("kcw_b", [P, NCX, DK], at + 2 * kb)
    at += 4 * kb
    s_sc = sb("s_sc", [P, 2, P], at)
    at += kb
    g_in = [sb(f"g_in{n}", [P, DV], at + n * 2 * kb) for n in range(2)]
    at += 4 * kb
    og = [sb(f"og{n}", [P, DV], at + n * 2 * kb) for n in range(2)]
    at += 4 * kb
    og_t = [sb(f"og_t{n}", [P, 4, P], at + n * 2 * kb) for n in range(2)]
    at += 4 * kb
    sq_j = sb("sq_j", [P, DV], at)
    at += 2 * kb
    hd = [sb(f"hd{n}", [P, H_N], at + n * 1600) for n in range(2)]
    ada_ret = raw

    merged = sb("merged", [P, KT, T], REST)
    gate_in = [sb(f"gate_in{n}", [P, T], REST + (32 + 4 * n) * kb) for n in range(2)]
    mtmp = sb("mtmp", [P, HALF], REST + 40 * kb)
    gain_row = sb("gain_row", [P, D], REST)
    diag = sb("diag", [P, KT, P], REST + 4 * kb)
    xr = [sb(f"xr{n}", [P, D], REST + (8 + 4 * n) * kb) for n in range(2)]
    x1n = [sb(f"x1n{n}", [P, D], REST + (16 + 4 * n) * kb) for n in range(2)]
    hn = [sb(f"hn{n}", [P, D], REST + (24 + 4 * n) * kb) for n in range(2)]
    haff = sb("haff", [P, D], REST + 32 * kb)
    junk2 = sb("junk2", [P, D], REST + 36 * kb)
    uy = [[sb(f"uy{n}{m}", [P, T], X1 + (12 * n + 4 * m) * kb) for m in range(2)] for n in range(2)]
    ua = [sb(f"ua{n}", [P, T], X1 + (12 * n + 8) * kb) for n in range(2)]
    a_raw = [sb(f"a_raw{n}", [P, T], X1 + (24 + 4 * n) * kb) for n in range(2)]
    d_raw = [sb(f"d_raw{n}", [P, HALF], X1 + (32 + 2 * n) * kb) for n in range(2)]
    d_hi = [sb(f"d_hi{n}", [P, HALF], X1 + (36 + 2 * n) * kb, F32R) for n in range(2)]
    d_lo = [sb(f"d_lo{n}", [P, HALF], X1 + (40 + 2 * n) * kb, F32R) for n in range(2)]
    a_hi = [sb(f"a_hi{n}", [P, T], X1 + (44 + 4 * n) * kb, F32R) for n in range(2)]
    a_lo = [sb(f"a_lo{n}", [P, T], X1 + (52 + 4 * n) * kb, F32R) for n in range(2)]
    f0 = sb("f0", [P, NCH, HALF], X0)
    x1all = sb("x1all", [P, NCH, D], X0 + 16 * kb)
    gain_row2 = sb("gain_row2", [P, D], X0 + 48 * kb)
    fo = [sb(f"fo{n}", [P, D], X0 + (52 + 4 * n) * kb) for n in range(2)]
    diag2 = sb("diag2", [P, KT, P], REST)
    junk3 = sb("junk3", [P, HALF], REST + 4 * kb)
    fsum = sb("fsum", [P, 8, 8], REST + 8 * kb)

    def dram(name, shape):
        return nc.dram_tensor(name, shape, F32).ap()

    kvc_d = dram("kvc_d", [6, P, NCX, HALF])
    qk_d = dram("qk_d", [2 * HEADS, P, 2, T])
    vg_d = dram("vg_d", [2 * HEADS, NCH, P, DV])
    co_d = dram("co_d", [KT, P, T])
    gate_d = dram("gate_d", [2 * KT, P, T])
    go_d = dram("go_d", [HEADS * 4, P, T])
    x1_d = dram("x1_d", [NCH, P, D])
    a_d = dram("a_d", [FT, P, T])

    def sem(name):
        return nc.alloc_semaphore(name)

    vec_in, ident_in, const_in, ctx_ready = sem("vec_in"), sem("ident_in"), sem("const_in"), sem("ctx_ready")
    x_ready = [sem(f"x_ready{c}") for c in range(NCH)]
    ada_in = [sem(f"ada_in{n}") for n in range(ADA_RING)]
    silu_ok, ada_done, mod_ok = sem("silu_ok"), sem("ada_done"), sem("mod_ok")
    act0, dve0 = sem("act0"), sem("dve0")
    sq_ok, root_ok, rinv_ok, xn_ok, xt_ok, aff_ok, h_hi, h_lo = (
        sem(n) for n in ("sq_ok", "root_ok", "rinv_ok", "xn_ok", "xt_ok", "aff_ok", "h_hi", "h_lo"))
    setup_ok = sem("setup_ok")
    raw_in = [sem("raw_in0"), sem("raw_in1")]
    hi_done, lo_done, pe_done = sem("hi_done"), sem("lo_done"), sem("pe_done")
    kvc_st, qk_st, vg_st, co_st, gate_st, go_st, x1_st, a_st = (
        sem(n) for n in ("kvc_st", "qk_st", "vg_st", "co_st", "gate_st", "go_st", "x1_st", "a_st"))
    out_st = [sem("out_st0"), sem("out_st1")]
    landed = sem("landed")
    ctx_ev, trig_in, rot_mul, rot_add, vg_ev = (sem(n) for n in ("ctx_ev", "trig_in", "rot_mul", "rot_add", "vg_ev"))
    cv_x, cv_p, cv_b, cv_y, cv_s = (sem(n) for n in ("cv_x", "cv_p", "cv_b", "cv_y", "cv_s"))
    gate_ev = sem("gate_ev")
    ret_in, g_ld = [sem("ret_in0"), sem("ret_in1")], [sem("g_ld0"), sem("g_ld1")]
    (hd_ok, q_ok, kcw_ok, kt_ok, kz_ok, u_ok, st_ok, sc_ok, ms_ok, o_ok, osq_ok, ort_ok,
     oinv_ok, og_ok, ogt_ok, ogc_ok) = (sem(n) for n in (
         "hd_ok", "q_ok", "kcw_ok", "kt_ok", "kz_ok", "u_ok", "st_ok", "sc_ok", "ms_ok", "o_ok", "osq_ok",
         "ort_ok", "oinv_ok", "og_ok", "ogt_ok", "ogc_ok"))
    adb_in, adb_done = [sem("adb_in0"), sem("adb_in1")], sem("adb_done")
    gt_in, mg_mul, mg_add = [sem("gt_in0"), sem("gt_in1")], sem("mg_mul"), sem("mg_add")
    m_hi, m_lo = sem("m_hi"), sem("m_lo")
    dg_ok, row_mm, row_ok = sem("dg_ok"), sem("row_mm"), sem("row_ok")
    xr_in, y_done, y_sq, y_act, y_dve, y_x1, y_hn, y_t, y_hi, y_lo = (
        [sem("xr_in0"), sem("xr_in1")], *(sem(n) for n in (
            "y_done", "y_sq", "y_act", "y_dve", "y_x1", "y_hn", "y_t", "y_hi", "y_lo")))
    up_b, up_c, up_s, up_a = (sem(n) for n in ("up_b", "up_c", "up_s", "up_a"))
    dn_in, dn_hi, dn_lo, dn_pe, dn_ev, dn_sq, dn_add, dn_dve, dn_rt, x1_in, out_ok = (
        [sem("dn_in0"), sem("dn_in1")], *(sem(n) for n in (
            "dn_hi", "dn_lo", "dn_pe", "dn_ev", "dn_sq", "dn_add", "dn_dve", "dn_rt", "x1_in", "out_ok")))

    with nc.Block() as block:

        @block.sync
        def _(sp):
            def load(base, i, per, src):
                sp.wait_ge(lo_done, START + base - 1 + i * per)
                sp.dma_start(raw[base % 2][:, :], src).then_inc(raw_in[base % 2], 16)

            sp.dma_start(vec[:, :], io["vecs"]).then_inc(vec_in, 16)
            sp.dma_start(ident[:, :], io["consts"][:, C_ID:C_ID + P]).then_inc(ident_in, 16)
            sp.dma_start(x_in[:, 8:10, :], io["ctx"].rearrange("(c p) d -> p c d", p=P)).then_inc(ctx_ready, 16)
            for n in range(ADA_RING):
                sp.dma_start(ada_raw[n][:, :], io["w_ada_t"][n]).then_inc(ada_in[n], 16)
            sp.dma_start(const[:, :], io["consts"]).then_inc(const_in, 16)
            for c in range(NCH):
                sp.dma_start(x_in[:, c, :], io["x"][c * P:(c + 1) * P, :]).then_inc(x_ready[c], 16)
            with sp.Fori(1, 16 // ADA_RING) as i:
                for n in range(ADA_RING):
                    sp.wait_ge(ada_done, i * ADA_RING + (n - ADA_RING + 1))
                    sp.dma_start(ada_raw[n][:, :], io["w_ada_t"][i * ADA_RING + n]).then_inc(ada_in[n], 16)
            with sp.Fori(0, 6) as b:
                for u in range(4):
                    load(R_CTX + u, b, 4, io["w_n"][b, u])
            for u in range(2):
                load(R_QK + u, 0, 0, io["w_t"][u])
            sp.wait_ge(pe_done, START + P_QK)
            sp.wait_ge(h_lo, START + 10)
            sp.dma_start(cos[:, :], io["trig"][0]).then_inc(trig_in, 16)
            sp.dma_start(sin[:, :], io["trig"][1]).then_inc(trig_in, 16)
            for u in range(2, 4):
                load(R_QK + u, 0, 0, io["w_t"][u])
            with sp.Fori(1, 4) as i:
                for u in range(4):
                    load(R_QK + u, i, 4, io["w_t"][i * 4 + u])
            with sp.Fori(0, 8) as b:
                for u in range(4):
                    load(R_VG + u, b, 4, io["w_n"][b + 2, u])
            with sp.Fori(0, 4) as i:
                for u in range(6):
                    load(R_CONV + u, i, 6, io["w_t"][i * 6 + (16 + u)])
            with sp.Fori(0, 8) as i:
                for u in range(2):
                    load(R_GATE + u, i, 2, io["w_t"][i * 2 + (40 + u)])

            sp.wait_ge(pe_done, START + P_A)
            sp.wait_ge(gate_st, START + 16)
            sp.wait_ge(co_st, START + 8)
            sp.wait_ge(vg_st, START + 64)
            sp.wait_ge(qk_st, START + 8)

            def head_loads(h):
                p = h % 2
                sp.dma_start(q_t[p][:, :, :], qk_d[h]).then_inc(ret_in[p], 16)
                sp.dma_start(k_t[p][:, :, :], qk_d[h + HEADS]).then_inc(ret_in[p], 16)
                sp.dma_start(v_n[p][:, :, :], vg_d[h].rearrange("c p d -> p c d")).then_inc(ret_in[p], 16)
                sp.dma_start(kc_n[p][:, :, :], kvc_d[h // 2, :, :, p * DK:(p + 1) * DK]).then_inc(ret_in[p], 16)
                sp.dma_start(vc_n[p][:, :, :], kvc_d[h + 2]).then_inc(ret_in[p], 16)

            head_loads(0)
            head_loads(1)
            for h in range(HEADS):
                with sp.Fori(0, NCH // 2) as i:
                    for e in range(2):
                        n = h * NCH + e
                        sp.wait_ge(og_ok, START + n - 1 + i * 2)
                        sp.dma_start(g_in[e][:, :], vg_d[h + HEADS, i * 2 + e]).then_inc(g_ld[e], 16)
                        sp.wait_ge(adb_done, START + n - 1 + i * 2)
                        sp.dma_start(ada_ret[e][:, :], io["w_ada_t"][i * 2 + (16 + n)]).then_inc(adb_in[e], 16)
                if h + 2 < HEADS:
                    sp.wait_ge(ogt_ok, START + NCH * (h + 1))
                    sp.wait_ge(q_ok, START + 2 * (h + 1))
                    head_loads(h + 2)

            sp.wait_ge(go_st, START + HEADS * NCH)

            def gate_load(stage, j, i, src):
                sp.wait_ge(mg_mul, START + 2 * (8 * stage + j - 1) + i * 4)
                sp.dma_start(gate_in[j % 2][:, :], src).then_inc(gt_in[j % 2], 16)

            with sp.Fori(0, 4) as i:
                for j in range(2):
                    load(R_CO + j, i, 2, co_d[i * 2 + j])
            for stage, (base, gate_row) in enumerate(((R_A, 0), (R_B, 8))):
                with sp.Fori(0, 4) as i:
                    for j in range(2):
                        load(base + 2 * j, i, 4, io["w_m"][i * 2 + (8 * stage + j)])
                        load(base + 2 * j + 1, i, 4, go_d[i * 2 + (8 * stage + j)])
                        gate_load(stage, j, i, gate_d[i * 2 + (gate_row + j)])
            with sp.Fori(0, 4) as i:
                for j in range(2):
                    load(R_C + j, i, 2, io["w_m"][i * 2 + (16 + j)])
                    gate_load(2, j, i, gate_d[i * 2 + (8 + j)])
            with sp.Fori(0, 4) as i:
                for j in range(2):
                    load(R_WO + j, i, 2, io["w_o_t"][i * 2 + j])
            load(R_UP, 0, 0, io["w_up_t"][0])
            load(R_UP + 1, 0, 0, io["w_up_t"][1])
            sp.wait_ge(m_lo, START + KT)
            for c in range(NCH):
                sp.wait_ge(y_x1, START + c - 1)
                sp.dma_start(xr[c % 2][:, :], io["x"][c * P:(c + 1) * P, :]).then_inc(xr_in[c % 2], 16)

            for u in range(2, 4):
                load(R_UP + u, 0, 0, io["w_up_t"][u])
            with sp.Fori(1, FT // 2) as i:
                for u in range(4):
                    load(R_UP + u, i, 4, io["w_up_t"][i * 4 + u])
            sp.wait_ge(pe_done, START + P_UP + 2 * FT)
            sp.wait_ge(x1_st, START + NCH)
            sp.dma_start(x1all[:, :, :], x1_d.rearrange("c p d -> p c d")).then_inc(x1_in, 16)
            sp.wait_ge(a_st, START + FT)

            for half in range(2):
                with sp.Fori(0, FT // 2) as i:
                    for u in range(2):
                        sp.wait_ge(dn_lo, START + 2 * (half * FT + u - 1) + i * 4)
                        sp.dma_start(a_raw[u][:, :], a_d[i * 2 + u]).then_inc(dn_in[u], 16)
                        sp.dma_start(d_raw[u][:, :], io["w_dn_t"][i * 2 + u, :, half * HALF:(half + 1) * HALF])\
                          .then_inc(dn_in[u], 16)
            for c in range(NCH):
                sp.wait_ge(out_ok, START + c + 1)
                sp.dma_start(io["out"][c * P:(c + 1) * P, :], fo[c % 2][:, :]).then_inc(out_st[c % 2], 16)
            for n in range(2):
                sp.wait_ge(out_st[n], 16 * NCH // 2)

        @block.gpsimd
        def _(pool):
            for s in (kvc_st, qk_st, vg_st, co_st, gate_st, go_st, x1_st, a_st, q_ok, out_ok):
                pool.sem_inc(s, START)

            def store(dst, src, n, stored):
                pool.dma_start(dst, src).then_inc(landed, 16)
                pool.wait_ge(landed, 16 * (n + 1) if isinstance(n, int) else n * 16 + 16)
                pool.sem_inc(stored, 1)

            pool.memset(ones[:, :], 1.0).then_inc(setup_ok, 1)
            pool.memset(eps[:, :], EPS).then_inc(setup_ok, 1)
            with pool.Fori(0, 3) as i:
                for e in range(2):
                    pool.wait_ge(ctx_ev, START + 2 * (e + 1) + i * 4)
                    store(kvc_d[i * 2 + e], ctx_out[e][:, :, :], i * 2 + (ST_KVC + e), kvc_st)
            with pool.Fori(0, 4) as i:
                for d in range(2):
                    pool.wait_ge(rot_add, START + 2 * (d + 1) + i * 4)
                    store(qk_d[i * 2 + d], rot_o[d][:, :, :], i * 2 + (ST_QK + d), qk_st)
            with pool.Fori(0, 8) as b:
                for c in range(NCH):
                    pool.wait_ge(vg_ev, START + c + 1 + b * 8)
                    store(vg_d[b, c], vg_out[c][:, :], b * 8 + (ST_VG + c), vg_st)
            with pool.Fori(0, 4) as i:
                for j in range(2):
                    pool.wait_ge(cv_s, START + j + 1 + i * 2)
                    store(co_d[i * 2 + j], co[j][:, :], i * 2 + (ST_CO + j), co_st)
            with pool.Fori(0, 8) as i:
                for j in range(2):
                    pool.wait_ge(gate_ev, START + j + 1 + i * 2)
                    store(gate_d[i * 2 + j], gate_o[j][:, :], i * 2 + (ST_GATE + j), gate_st)

            with pool.Fori(0, 2) as i:
                for p in range(2):
                    pool.wait_ge(ret_in[p], 80 + i * 80)
                    pool.wait_ge(hd_ok, START + p + 1 + i * 2)
                    pool.wait_ge(o_ok, START + NCH * p + i * 16)
                    for dst, col in ((q_f, H_XF), (q_b, H_XB)):
                        rows = hd[p][:, col:col + P].unsqueeze(1).broadcast_to([P, 2 * NCH, P])
                        pool.tensor_tensor(dst[:, :, :].rearrange("p k (c t) -> p (k c) t", t=P),
                                           q_t[p][:, :, :].rearrange("p k (c t) -> p (k c) t", t=P),
                                           rows, ALU.mult).then_inc(q_ok, 1)
                    for c in range(NCH):
                        pool.wait_ge(ogc_ok, START + NCH * p + c + 1 + i * 16)
                        store(go_d[bass.ds(i * 8 + 4 * p, 4), :, c * P:(c + 1) * P].rearrange("k p t -> p k t"),
                              og_t[c % 2][:, :, :], i * 16 + (ST_GO + NCH * p + c), go_st)
            for c in range(NCH):
                pool.wait_ge(y_x1, START + c + 1)
                store(x1_d[c], x1n[c % 2][:, :], ST_X1 + c, x1_st)
            with pool.Fori(0, FT // 2) as i:
                for j in range(2):
                    pool.wait_ge(up_a, START + j + 1 + i * 2)
                    store(a_d[i * 2 + j], ua[j][:, :], i * 2 + (ST_A + j), a_st)
            pool.wait_ge(x1_in, 16)
            for c in range(NCH):
                pool.wait_ge(dn_dve, START + 3 * (c + 1))
                pool.tensor_tensor(fo[c % 2][:, :], fo[c % 2][:, :], x1all[:, c, :], ALU.add).then_inc(out_ok, 1)

        @block.scalar
        def _(act):
            for s in (hi_done, sq_ok, xn_ok, h_hi, ctx_ev, vg_ev, cv_x, cv_b, gate_ev, kcw_ok, kz_ok,
                      osq_ok, ort_ok, ogc_ok, m_hi, y_sq, y_act, y_hn, y_hi, up_b, up_s, dn_hi, dn_sq, dn_rt):
                act.sem_inc(s, START)

            def split_hi(base, i, per, dst):
                act.wait_ge(raw_in[base % 2], 16 * (base // 2 + 1) + i * (8 * per))
                act.activation(dst, raw[base % 2][:, :], ACT.Copy).then_inc(hi_done, 1)

            act.wait_ge(vec_in, 16)
            act.activation(silu_c[:, :, :].rearrange("p k v -> p v k"),
                           vec[:, V_C:V_C + 16].rearrange("p (v k) -> p v k", v=2), ACT.Silu).then_inc(silu_ok, 1)
            act.wait_ge(setup_ok, 2)
            act.wait_ge(ctx_ready, 16)
            for n, c in enumerate((8, 9)):
                act.wait_ge(sq_ok, START + n)
                act.activation(junk[:, :], x_in[:, c, :], ACT.Square, accum_out=ssum[:, c:c + 1]).then_inc(sq_ok, 1)
            act.wait_ge(sq_ok, START + 2)
            act.activation(root[:, 8:10], ssum[:, 8:10], ACT.Sqrt, bias=eps[:, :], scale=1.0 / D).then_inc(root_ok, 1)
            for c in range(NCH):
                act.wait_ge(x_ready[c], 16)
                act.wait_ge(sq_ok, START + 2 + c)
                act.activation(junk[:, :], x_in[:, c, :], ACT.Square, accum_out=ssum[:, c:c + 1]).then_inc(sq_ok, 1)
            act.wait_ge(sq_ok, START + 10)
            act.activation(root[:, 0:8], ssum[:, 0:8], ACT.Sqrt, bias=eps[:, :], scale=1.0 / D).then_inc(root_ok, 1)
            def norm_chunk(n, c):
                act.wait_ge(xt_ok, START + n - 1)
                act.activation(xn[n % 2][:, :], x_in[:, c, :], ACT.Copy, scale=rinv[:, c:c + 1]).then_inc(xn_ok, 1)

            def h_high(n, dst):
                act.wait_ge(aff_ok, START + 2 * n + 2)
                act.activation(dst, aff[n % 2][:, :].rearrange("p (k t) -> p k t", t=P), ACT.Copy).then_inc(h_hi, 1)

            order = (8, 9) + tuple(range(NCH))
            act.wait_ge(rinv_ok, 1)
            norm_chunk(0, 8)
            norm_chunk(1, 9)
            act.wait_ge(rinv_ok, 2)
            for n in range(10):
                if n >= 1 and n + 1 < 10:
                    norm_chunk(n + 1, order[n + 1])
                h_high(n, hc_hi[:, :, n * P:(n + 1) * P] if n < 2 else x0_hi[:, :, (n - 2) * P:(n - 1) * P])

            split_hi(R_CTX, 0, 0, w_hi[0][:, :])
            with act.Fori(0, 3) as i:
                for e in range(2):
                    for u in range(4):
                        r = 4 * e + u
                        act.wait_ge(pe_done, START + 5 * e + u + i * 10)
                        split_hi(R_CTX + r + 1, i, 8, w_hi[(r + 1) % 2][:, :])
                    act.wait_ge(kvc_st, START + e - 1 + i * 2)
                    for c in range(NCX):
                        act.wait_ge(pe_done, START + 5 * e + 3 + c + 1 + i * 10)
                        act.activation(ctx_out[e][:, c, :], ps[:, 2 * e + c, :], ACT.Copy).then_inc(ctx_ev, 1)

            act.wait_ge(dve0, 2)
            act.activation(dec[:, DC_U, :], dec[:, DC_AZ, :], ACT.Exp, scale=-1.0).then_inc(act0, 1)
            act.wait_ge(dve0, 3)
            act.activation(dec[:, DC_LN, :], dec[:, DC_W, :], ACT.Ln).then_inc(act0, 1)
            act.wait_ge(dve0, 8)
            act.wait_ge(const_in, 16)
            for h in range(HEADS):
                fw, bw = dec[:, DC_LG, h:h + 1], dec[:, DC_LG, HEADS + h:HEADS + h + 1]
                for dst, src, scale in ((head_tab[:, h, H_D:H_D + P], const[:, C_DPOS:C_DPOS + P], fw),
                                        (dtmp[:, h, :], const[:, C_DNEG:C_DNEG + P], bw),
                                        (head_tab[:, h, H_XF:H_XF + P], const[:, C_RF:C_RF + P], fw),
                                        (head_tab[:, h, H_XB:H_XB + P], const[:, C_RB:C_RB + P], bw),
                                        (head_tab[:, h, H_F:H_F + 4], const[:, C_COLF:C_COLF + 4], fw),
                                        (head_tab[:, h, H_B:H_B + 4], const[:, C_COLB:C_COLB + 4], bw)):
                    act.activation(dst, src, ACT.Exp, scale=scale).then_inc(act0, 1)

            with act.Fori(0, 4) as i:
                for u in range(4):
                    act.wait_ge(pe_done, START + P_QK + u + i * 4)
                    split_hi(R_QK + u + 1, i, 4, w_hi[(u + 1) % 2][:, :])

            for base, func in ((0, ACT.Copy), (4, ACT.Silu)):
                with act.Fori(0, 4) as b:
                    for u in range(4):
                        act.wait_ge(pe_done, START + P_VG + 11 * base + u + b * 11)
                        split_hi(R_VG + 4 * base + u + 1, b, 4, w_hi[(u + 1) % 2][:, :])
                    for c in range(NCH):
                        act.wait_ge(vg_st, START + 8 * base + c - 7 + b * 8)
                        act.wait_ge(pe_done, START + P_VG + 11 * base + 4 + c + b * 11)
                        act.activation(vg_out[c][:, :], ps[:, c, :], func).then_inc(vg_ev, 1)

            with act.Fori(0, 4) as i:
                for j in range(2):
                    for m in range(3):
                        u = 3 * j + m
                        act.wait_ge(pe_done, START + P_CONV + u + i * 6)
                        split_hi(R_CONV + u + 1, i, 6, w_hi[(u + 1) % 2][:, :])
                        if m == 0:
                            act.wait_ge(cv_p, START + j - 1 + i * 2)
                            act.wait_ge(pe_done, START + P_CONV + u + 1 + i * 6)
                            act.activation(cx[j][:, :], pair(CONV_PAIR[u]), ACT.Copy).then_inc(cv_x, 1)
                        if m == 1:
                            act.wait_ge(cv_p, START + j + 1 + i * 2)
                            act.wait_ge(cv_s, START + j - 1 + i * 2)
                            act.activation(cy[j][:, :], cprod[j][:, :], ACT.Identity,
                                           scale=vec[:, bass.ds(i * 2 + (V_CW + 8 + j), 1)],
                                           bias=vec[:, bass.ds(i * 2 + (V_CB + j), 1)]).then_inc(cv_b, 1)

            def gates(i, last):
                for u in range(2):
                    act.wait_ge(pe_done, START + P_GATE + u + i * 2)
                    if not (last and u == 1):
                        split_hi(R_GATE + u + 1, i, 2, w_hi[(u + 1) % 2][:, :])
                    act.wait_ge(gate_st, START + u - 1 + i * 2)
                    act.wait_ge(pe_done, START + P_GATE + u + 1 + i * 2)
                    act.activation(gate_o[u][:, :], pair(2 + u), ACT.Sigmoid).then_inc(gate_ev, 1)

            with act.Fori(0, 7) as i:
                gates(i, False)
            gates(7, True)

            with act.Fori(0, 2) as i:
                for p in range(2):
                    act.wait_ge(ret_in[p], 80 + i * 80)
                    act.wait_ge(hd_ok, START + p + 1 + i * 2)
                    act.wait_ge(u_ok, START + N_U * (p - 1) + 4 + i * 2 * N_U)
                    for dst, col in ((kcw_b, H_B), (kcw_f, H_F)):
                        for m in range(NCX):
                            act.activation(dst[:, m, :], kc_n[p][:, m, :], ACT.Copy,
                                           scale=hd[p][:, col + 1 + m:col + 2 + m]).then_inc(kcw_ok, 1)
                    for m in range(NCH):
                        c = NCH - 1 - m
                        act.wait_ge(kt_ok, START + NCH * p + m + 1 + i * 16)
                        act.wait_ge(u_ok, START + N_U * p + 2 * m + 2 + i * 2 * N_U)
                        if c > 0:
                            act.activation(kz_b[:, m % 2, :], ps[:, m % 2, 0:DK], ACT.Copy,
                                           scale=hd[p][:, H_B:H_B + 1]).then_inc(kz_ok, 1)
                        if c < NCH - 1:
                            act.activation(kz_f[:, c, :], ps[:, m % 2, 0:DK], ACT.Copy,
                                           scale=hd[p][:, H_F:H_F + 1]).then_inc(kz_ok, 1)
                    def gated_out(c):
                        act.wait_ge(go_st, START + NCH * p + c - 1 + i * 16)
                        act.wait_ge(ogt_ok, START + NCH * p + c + 1 + i * 16)
                        act.activation(og_t[c % 2][:, :, :].rearrange("p k t -> p (k t)"), ps[:, 6, :],
                                       ACT.Copy).then_inc(ogc_ok, 1)

                    for c in range(NCH):
                        n = NCH * p + c
                        act.wait_ge(o_ok, START + n + 1 + i * 16)
                        act.wait_ge(osq_ok, START + n + i * 16)
                        act.activation(sq_j[:, :], ps[:, 2 + c % 2, :], ACT.Square,
                                       accum_out=onum[:, c % 2, 0:1]).then_inc(osq_ok, 1)
                        act.wait_ge(osq_ok, START + n + 1 + i * 16)
                        act.wait_ge(oinv_ok, START + n - 1 + i * 16)
                        act.activation(onum[:, c % 2, 1:2], onum[:, c % 2, 0:1], ACT.Sqrt,
                                       bias=eps[:, :], scale=1.0 / DV).then_inc(ort_ok, 1)
                        if c > 0:
                            gated_out(c - 1)
                    gated_out(NCH - 1)

            with act.Fori(0, 4) as i:
                for j in range(2):
                    split_hi(R_CO + j, i, 2, x1_hi[:, bass.ds(i * 2 + j, 1), :].rearrange("p k t -> p (k t)"))
            split_hi(R_A, 0, 0, w_hi[0][:, :])
            for base, count, dst in ((R_A, P_A, x0_hi), (R_B, P_B, x1_hi)):
                with act.Fori(0, 4) as i:
                    for j in range(2):
                        act.wait_ge(pe_done, START + count + j + i * 2)
                        split_hi(base + 2 * j + 1, i, 4, dst[:, bass.ds(i * 2 + j, 1), :].rearrange("p k t -> p (k t)"))
                        split_hi(base + 2 * j + 2, i, 4, w_hi[(j + 1) % 2][:, :])

            def last_stage(i, last):
                for j in range(2):
                    act.wait_ge(pe_done, START + P_C + j + i * 2)
                    if not (last and j == 1):
                        split_hi(R_C + j + 1, i, 2, w_hi[(j + 1) % 2][:, :])
                    act.wait_ge(mg_add, START + 16 + 2 * (j + 1) + i * 4)
                    act.activation(x0_hi[:, bass.ds(i * 2 + j, 1), :], merged[:, bass.ds(i * 2 + j, 1), :],
                                   ACT.Copy).then_inc(m_hi, 1)

            with act.Fori(0, 3) as i:
                last_stage(i, False)
            last_stage(3, True)
            act.wait_ge(pe_done, START + P_UP)
            with act.Fori(0, 4) as i:
                for j in range(2):
                    split_hi(R_WO + j, i, 2, x1_hi[:, bass.ds(i * 2 + j, 1), :].rearrange("p k t -> p (k t)"))
            split_hi(R_UP, 0, 0, w_hi[0][:, :])

            act.wait_ge(row_mm, 1)
            act.activation(gain_row[:, :], pair(2), ACT.Copy).then_inc(row_ok, 1)
            for c in range(NCH + 1):
                if c < NCH:
                    act.wait_ge(y_done, START + c + 1)
                    act.wait_ge(y_sq, START + 2 * c)
                    act.activation(junk2[:, :], pair(c % 2), ACT.Square, accum_out=st1[:, c, 0:1]).then_inc(y_sq, 1)
                    act.wait_ge(y_sq, START + 2 * c + 1)
                    act.activation(st1[:, c, 1:2], st1[:, c, 0:1], ACT.Sqrt, bias=eps[:, :], scale=1.0 / D).then_inc(y_act, 1)
                    act.wait_ge(y_x1, START + c + 1)
                    act.wait_ge(y_sq, START + 2 * c + 1)
                    act.activation(junk2[:, :], x1n[c % 2][:, :], ACT.Square, accum_out=st2[:, c, 0:1]).then_inc(y_sq, 1)
                    act.wait_ge(y_sq, START + 2 * c + 2)
                    act.activation(st2[:, c, 1:2], st2[:, c, 0:1], ACT.Sqrt, bias=eps[:, :], scale=1.0 / D).then_inc(y_act, 1)
                if c > 0:
                    act.wait_ge(y_dve, START + Y_COUNT["shift", c - 1])
                    act.activation(x0_hi[:, :, (c - 1) * P:c * P], haff[:, :].rearrange("p (k t) -> p k t", t=P),
                                   ACT.Copy).then_inc(y_hi, 1)
                if c < NCH:
                    act.wait_ge(y_dve, START + Y_COUNT["inv2", c])
                    act.activation(hn[c % 2][:, :], x1n[c % 2][:, :], ACT.Copy, scale=st2[:, c, 2:3]).then_inc(y_hn, 1)

            def up(i, last):
                for j in range(2):
                    for m in range(2):
                        u = 2 * j + m
                        act.wait_ge(pe_done, START + P_UP + u + i * 4)
                        if not (last and u == 3):
                            split_hi(R_UP + u + 1, i, 4, w_hi[(u + 1) % 2][:, :])
                        act.wait_ge(up_a, START + j - 1 + i * 2)
                        act.wait_ge(pe_done, START + P_UP + u + 1 + i * 4)
                        tile = FT * m + j
                        act.activation(uy[j][m][:, :], pair(u), ACT.Identity,
                                       scale=vec[:, bass.ds(i * 6 + (V_FW + 3 * tile + 1), 1)],
                                       bias=vec[:, bass.ds(i * 2 + (V_FB + tile), 1)]).then_inc(up_b, 1)
                    act.wait_ge(up_c, START + 4 * j + 2 + i * 8)
                    act.activation(uy[j][0][:, :], uy[j][0][:, :], ACT.Silu).then_inc(up_s, 1)

            with act.Fori(0, FT // 2 - 1) as i:
                up(i, False)
            up(FT // 2 - 1, True)

            act.wait_ge(row_mm, 2)
            act.activation(gain_row2[:, :], pair(3), ACT.Copy).then_inc(row_ok, 1)

            def down_hi(n, i, u):
                act.wait_ge(dn_in[u], 32 * (n // 2 + 1) + i * 32)
                act.activation(a_hi[u][:, :], a_raw[u][:, :], ACT.Copy).then_inc(dn_hi, 1)
                act.activation(d_hi[u][:, :], d_raw[u][:, :], ACT.Copy).then_inc(dn_hi, 1)

            def down(half, i, last):
                for u in range(2):
                    act.wait_ge(dn_pe, START + N_DOWN * half + u + i * 2)
                    if not (last and half == 1 and u == 1):
                        down_hi(FT * half + u + 1, i, (u + 1) % 2)

            down_hi(0, 0, 0)
            for half in range(2):
                with act.Fori(0, FT // 2 - 1) as i:
                    down(half, i, False)
                down(half, FT // 2 - 1, True)
                for c in range(NCH):
                    act.wait_ge(dn_pe, START + N_DOWN * half + FT + c)
                    act.wait_ge(dn_sq, START + NCH * half + c)
                    act.activation(junk3[:, :], ps[:, c, :], ACT.Square, accum_out=fsum[:, c, half:half + 1]).then_inc(dn_sq, 1)
                    if half == 1:
                        act.wait_ge(dn_add, START + c + 1)
                        act.activation(fsum[:, c, 3:4], fsum[:, c, 2:3], ACT.Sqrt, bias=eps[:, :], scale=1.0 / D).then_inc(dn_rt, 1)

        @block.vector
        def _(dve):
            for s in (lo_done, aff_ok, h_lo, rot_mul, rot_add, cv_p, cv_y, cv_s, hd_ok, st_ok, ms_ok, oinv_ok, og_ok,
                      mg_mul, mg_add, m_lo, y_dve, y_x1, y_lo, up_c, up_a, dn_lo, dn_ev, dn_add, dn_dve):
                dve.sem_inc(s, START)

            def split_lo(base, i, per, dst, hi):
                dve.wait_ge(hi_done, START + base + 1 + i * per)
                dve.tensor_tensor(dst, raw[base % 2][:, :], hi.bitcast(F32), ALU.subtract).then_inc(lo_done, 1)

            def ring_lo(base, i, per):
                split_lo(base, i, per, w_lo[base % 2][:, :], w_hi[base % 2][:, :])

            def flat(t, i, j):
                return t[:, bass.ds(i * 2 + j, 1), :].rearrange("p k t -> p (k t)")

            def by_tile(v):
                return v.unsqueeze(2).broadcast_to([P, KT, P])

            dve.wait_ge(root_ok, 1)
            dve.reciprocal(rinv[:, 8:10], root[:, 8:10]).then_inc(rinv_ok, 1)
            dve.wait_ge(root_ok, 2)
            dve.reciprocal(rinv[:, 0:8], root[:, 0:8]).then_inc(rinv_ok, 1)
            dve.wait_ge(ada_done, 16)
            dve.tensor_tensor(mod_a[:, :, :], ps[:, 7, 0:32].rearrange("p (t v) -> p t v", v=2),
                              vec[:, V_BADA:V_BADA + 16].unsqueeze(2).broadcast_to([P, 16, 2]), ALU.add).then_inc(mod_ok, 1)
            dve.wait_ge(mod_ok, 1)
            dve.scalar_tensor_tensor(scale_x[:, :, :], mod_a[:, KT:16, :], 1.0,
                                     vec[:, V_GMIX:V_GMIX + KT].unsqueeze(2).broadcast_to([P, KT, 2]),
                                     ALU.add, ALU.mult).then_inc(mod_ok, 1)
            dve.wait_ge(mod_ok, 2)
            for n in range(10):
                who = 1 if n < 2 else 0
                tile = aff[n % 2][:, :].rearrange("p (k t) -> p k t", t=P)
                dve.wait_ge(xt_ok, START + n + 1)
                dve.tensor_tensor(tile, pair(n % 2).rearrange("p (k t) -> p k t", t=P), by_tile(scale_x[:, :, who]),
                                  ALU.mult).then_inc(aff_ok, 1)
                dve.wait_ge(aff_ok, START + 2 * n + 1)
                dve.tensor_tensor(tile, tile, by_tile(mod_a[:, 0:KT, who]), ALU.add).then_inc(aff_ok, 1)
                hi, lo = (hc_hi, hc_lo) if n < 2 else (x0_hi, x0_lo)
                cols = slice(n * P, (n + 1) * P) if n < 2 else slice((n - 2) * P, (n - 1) * P)
                dve.wait_ge(h_hi, START + n + 1)
                dve.tensor_tensor(lo[:, :, cols], tile, hi[:, :, cols].bitcast(F32), ALU.subtract).then_inc(h_lo, 1)

            ring_lo(R_CTX, 0, 0)
            with dve.Fori(0, 3) as i:
                for r in range(8):
                    ring_lo(R_CTX + r + 1, i, 8)

            z = vec[:, V_DEC:V_DEC + 8]
            dve.tensor_scalar(dec[:, DC_T, :], z, -1.0, None, ALU.mult).then_inc(dve0, 1)
            dve.wait_ge(dve0, 1)
            dve.tensor_tensor(dec[:, DC_AZ, :], z, dec[:, DC_T, :], ALU.max).then_inc(dve0, 1)
            dve.wait_ge(act0, 1)
            dve.tensor_scalar(dec[:, DC_W, :], dec[:, DC_U, :], 1.0, None, ALU.add).then_inc(dve0, 1)
            dve.wait_ge(dve0, 3)
            dve.scalar_tensor_tensor(dec[:, DC_CORR, :], dec[:, DC_W, :], 1.0, dec[:, DC_U, :],
                                     ALU.subtract, ALU.subtract).then_inc(dve0, 1)
            dve.reciprocal(dec[:, DC_RW, :], dec[:, DC_W, :]).then_inc(dve0, 1)
            dve.wait_ge(dve0, 5)
            dve.tensor_tensor(dec[:, DC_CORR, :], dec[:, DC_CORR, :], dec[:, DC_RW, :], ALU.mult).then_inc(dve0, 1)
            dve.wait_ge(dve0, 6)
            dve.wait_ge(act0, 2)
            dve.tensor_tensor(dec[:, DC_LN, :], dec[:, DC_LN, :], dec[:, DC_CORR, :], ALU.subtract).then_inc(dve0, 1)
            dve.wait_ge(dve0, 7)
            dve.scalar_tensor_tensor(dec[:, DC_LG, :], z, 0.0, dec[:, DC_LN, :], ALU.min, ALU.subtract).then_inc(dve0, 1)
            dve.wait_ge(act0, 2 + 6 * HEADS)
            mask = head_tab[:, :, H_D:H_D + P]
            dve.tensor_tensor(mask, mask, const[:, C_GE:C_GE + P].unsqueeze(1).broadcast_to([P, HEADS, P]),
                              ALU.mult).then_inc(dve0, 1)
            dve.tensor_tensor(dtmp[:, :, :], dtmp[:, :, :], const[:, C_LT:C_LT + P].unsqueeze(1).broadcast_to([P, HEADS, P]),
                              ALU.mult).then_inc(dve0, 1)
            for col in (H_F, H_B):
                dve.tensor_scalar(head_tab[:, :, col:col + 3], head_tab[:, :, col:col + 3], K_SCALE, None,
                                  ALU.mult).then_inc(dve0, 1)
            dve.wait_ge(dve0, 12)
            dve.tensor_tensor(mask, mask, dtmp[:, :, :], ALU.add).then_inc(dve0, 1)

            dve.wait_ge(trig_in, 32)
            with dve.Fori(0, 4) as i:
                for d in range(2):
                    for m in range(2):
                        u = 2 * d + m
                        ring_lo(R_QK + u + 1, i, 4)
                        dve.wait_ge(pe_done, START + P_QK + u + 1 + i * 4)
                        dve.tensor_tensor(rot_a[d][:, m, :], pair(u), cos[:, :], ALU.mult).then_inc(rot_mul, 1)
                        dve.tensor_tensor(rot_b[d][:, 1 - m, :], pair(u), sin[:, :], ALU.mult).then_inc(rot_mul, 1)
                    dve.wait_ge(rot_mul, START + 4 * (d + 1) + i * 8)
                    dve.wait_ge(qk_st, START + d - 1 + i * 2)
                    dve.tensor_tensor(rot_o[d][:, 0, :], rot_a[d][:, 0, :], rot_b[d][:, 0, :], ALU.subtract).then_inc(rot_add, 1)
                    dve.tensor_tensor(rot_o[d][:, 1, :], rot_a[d][:, 1, :], rot_b[d][:, 1, :], ALU.add).then_inc(rot_add, 1)

            with dve.Fori(0, 8) as b:
                for u in range(4):
                    ring_lo(R_VG + u + 1, b, 4)

            with dve.Fori(0, 4) as i:
                for j in range(2):
                    rows_p = cprod[j][:, :].rearrange("p (r t) -> p r t", t=GRID)
                    rows_y = cy[j][:, :].rearrange("p (r t) -> p r t", t=GRID)
                    for m in range(3):
                        u = 3 * j + m
                        ring_lo(R_CONV + u + 1, i, 6)
                        if m == 1:
                            dve.wait_ge(pe_done, START + P_CONV + u + 1 + i * 6)
                            dve.wait_ge(cv_x, START + j + 1 + i * 2)
                            dve.tensor_tensor(cprod[j][:, :], pair(CONV_PAIR[u]), cx[j][:, :], ALU.mult).then_inc(cv_p, 1)
                            dve.wait_ge(cv_b, START + j + 1 + i * 2)
                            dve.scalar_tensor_tensor(rows_y[:, :, 1:GRID], rows_p[:, :, 0:GRID - 1],
                                                     vec[:, bass.ds(i * 2 + (V_CW + j), 1)], rows_y[:, :, 1:GRID],
                                                     ALU.mult, ALU.add).then_inc(cv_y, 1)
                            dve.wait_ge(cv_y, START + 2 * j + 1 + i * 4)
                            dve.scalar_tensor_tensor(rows_y[:, :, 0:GRID - 1], rows_p[:, :, 1:GRID],
                                                     vec[:, bass.ds(i * 2 + (V_CW + 2 * KT + j), 1)], rows_y[:, :, 0:GRID - 1],
                                                     ALU.mult, ALU.add).then_inc(cv_y, 1)
                        if m == 2:
                            dve.wait_ge(cv_y, START + 2 * j + 2 + i * 4)
                            dve.wait_ge(co_st, START + j - 1 + i * 2)
                            dve.wait_ge(pe_done, START + P_CONV + u + 1 + i * 6)
                            dve.tensor_tensor(co[j][:, :], cy[j][:, :], pair(CONV_PAIR[u]), ALU.mult).then_inc(cv_s, 1)

            with dve.Fori(0, 7) as i:
                for u in range(2):
                    ring_lo(R_GATE + u + 1, i, 2)
            ring_lo(R_GATE + 15, 0, 0)

            with dve.Fori(0, 2) as i:
                for p in range(2):
                    dve.wait_ge(q_ok, START + 2 * (p - 1) + i * 4)
                    dve.wait_ge(kz_ok, START + N_KZ * (p - 1) + i * 2 * N_KZ)
                    dve.wait_ge(ret_in[p], 80 + i * 80)
                    dve.tensor_copy(hd[p][:, :], head_tab[:, bass.ds(i * 2 + p, 1), :].rearrange("p h n -> p (h n)"))\
                       .then_inc(hd_ok, 1)
                    u0 = N_U * p

                    def state(n, dst, old, decay):
                        dve.wait_ge(u_ok, START + u0 + n + 1 + i * 2 * N_U)
                        if old is None:
                            dve.tensor_copy(dst, ps[:, 4 + n % 2, :]).then_inc(st_ok, 1)
                        else:
                            dve.wait_ge(st_ok, START + u0 + n - 1 + i * 2 * N_U)
                            dve.scalar_tensor_tensor(dst, old, decay, ps[:, 4 + n % 2, :], ALU.mult, ALU.add).then_inc(st_ok, 1)

                    dve.wait_ge(o_ok, START + NCH * p + i * 16)
                    for t in range(2):
                        state(t, s_bw[:, NCH - 1, t, :], None, None)
                    for t in range(2):
                        state(2 + t, s_fw[:, 0, t, :], None, None)
                    dve.wait_ge(hd_ok, START + p + 1 + i * 2)
                    for m in range(NCH - 1):
                        c = NCH - 1 - m
                        for t in range(2):
                            state(4 + 2 * m + t, s_bw[:, c - 1, t, :], s_bw[:, c, t, :], hd[p][:, H_B + 3:H_B + 4])

                    def mask_scores(c):
                        n = NCH * p + c
                        dve.wait_ge(o_ok, START + n - 1 + i * 16)
                        dve.wait_ge(sc_ok, START + n + 1 + i * 16)
                        dve.tensor_tensor(s_sc[:, c % 2, :], ps[:, c % 2, 0:P], hd[p][:, H_D:H_D + P], ALU.mult).then_inc(ms_ok, 1)

                    def forward(c, t):
                        if t == 0:
                            dve.wait_ge(o_ok, START + NCH * p + c + i * 16)
                        state(18 + 2 * c + t, s_fw[:, (c + 1) % 2, t, :], s_fw[:, c % 2, t, :], hd[p][:, H_F + 3:H_F + 4])

                    mask_scores(0)
                    for c in range(NCH):
                        n = NCH * p + c
                        if c + 1 < NCH:
                            mask_scores(c + 1)
                            forward(c, 0)
                        dve.wait_ge(ort_ok, START + n + 1 + i * 16)
                        dve.reciprocal(onum[:, c % 2, 2:3], onum[:, c % 2, 1:2]).then_inc(oinv_ok, 1)
                        if c + 1 < NCH:
                            forward(c, 1)
                        dve.wait_ge(oinv_ok, START + n + 1 + i * 16)
                        dve.wait_ge(g_ld[c % 2], 16 * (NCH // 2 * p + c // 2 + 1) + i * 128)
                        dve.wait_ge(ogt_ok, START + n - 1 + i * 16)
                        dve.scalar_tensor_tensor(og[c % 2][:, :], ps[:, 2 + c % 2, :], onum[:, c % 2, 2:3], g_in[c % 2][:, :],
                                                 ALU.mult, ALU.mult).then_inc(og_ok, 1)
            dve.wait_ge(adb_done, START + 32)
            dve.tensor_tensor(mod_b[:, :], ps[:, 7, 0:32], vec[:, V_BADA + 16:V_BADA + 48], ALU.add).then_inc(mod_ok, 1)
            dve.wait_ge(mod_ok, 3)
            dve.scalar_tensor_tensor(scale_h[:, :], mod_b[:, 16:24], 1.0, vec[:, V_GFFN:V_GFFN + KT], ALU.add, ALU.mult).then_inc(mod_ok, 1)
            dve.tensor_tensor(gain_y[:, :], mod_b[:, 0:8], vec[:, V_GPOST:V_GPOST + KT], ALU.mult).then_inc(mod_ok, 1)
            dve.tensor_tensor(gain_f[:, :], mod_b[:, 24:32], vec[:, V_GFPOST:V_GFPOST + KT], ALU.mult).then_inc(mod_ok, 1)

            with dve.Fori(0, 4) as i:
                for j in range(2):
                    split_lo(R_CO + j, i, 2, flat(x1_lo, i, j), flat(x1_hi, i, j))
            ring_lo(R_A, 0, 0)

            def merge(stage, count, i, j):
                dve.wait_ge(gt_in[j], 16 * (4 * stage + 1) + i * 16)
                dve.wait_ge(pe_done, START + count + j + 1 + i * 2)
                for n in range(2):
                    cols = slice(n * HALF, (n + 1) * HALF)
                    out = merged[:, bass.ds(i * 2 + j, 1), cols].rearrange("p k t -> p (k t)")
                    made = START + 16 * stage + 2 * j + n + 1
                    if stage == 0:
                        dve.tensor_tensor(out, ps[:, 2 * j + n, :], gate_in[j][:, cols], ALU.mult).then_inc(mg_mul, 1)
                    else:
                        dve.wait_ge(mg_add, made - 17 + i * 4)
                        dve.tensor_tensor(mtmp[:, :], ps[:, 2 * j + n, :], gate_in[j][:, cols], ALU.mult).then_inc(mg_mul, 1)
                        dve.wait_ge(mg_mul, made + i * 4)
                        dve.tensor_tensor(out, out, mtmp[:, :], ALU.add).then_inc(mg_add, 1)

            for stage, (base, count, hi, lo) in enumerate(((R_A, P_A, x0_hi, x0_lo), (R_B, P_B, x1_hi, x1_lo))):
                with dve.Fori(0, 4) as i:
                    for j in range(2):
                        split_lo(base + 2 * j + 1, i, 4, flat(lo, i, j), flat(hi, i, j))
                        split_lo(base + 2 * j + 2, i, 4, w_lo[(j + 1) % 2][:, :], w_hi[(j + 1) % 2][:, :])
                        merge(stage, count, i, j)

            def last_stage(i, last):
                for j in range(2):
                    if not (last and j == 1):
                        ring_lo(R_C + j + 1, i, 2)
                    merge(2, P_C, i, j)
                    dve.wait_ge(m_hi, START + j + 1 + i * 2)
                    dve.tensor_tensor(flat(x0_lo, i, j), flat(merged, i, j), flat(x0_hi, i, j).bitcast(F32),
                                      ALU.subtract).then_inc(m_lo, 1)

            with dve.Fori(0, 3) as i:
                last_stage(i, False)
            last_stage(3, True)
            dve.wait_ge(mod_ok, 6)
            dve.wait_ge(m_lo, START + KT)
            dve.tensor_tensor(diag[:, :, :], ident[:, :].unsqueeze(1).broadcast_to([P, KT, P]), by_tile(gain_y[:, :]),
                              ALU.mult).then_inc(dg_ok, 1)
            with dve.Fori(0, 4) as i:
                for j in range(2):
                    split_lo(R_WO + j, i, 2, flat(x1_lo, i, j), flat(x1_hi, i, j))
            ring_lo(R_UP, 0, 0)

            dve.wait_ge(row_ok, 1)
            tile = haff[:, :].rearrange("p (k t) -> p k t", t=P)
            for c in range(NCH + 1):
                if c < NCH:
                    dve.wait_ge(y_act, START + 2 * c + 1)
                    dve.reciprocal(st1[:, c, 2:3], st1[:, c, 1:2]).then_inc(y_dve, 1)
                    dve.wait_ge(y_dve, START + Y_COUNT["inv1", c])
                    dve.wait_ge(y_hn, START + c - 1)
                    dve.wait_ge(y_t, START + c - 1)
                    dve.scalar_tensor_tensor(hn[c % 2][:, :], pair(c % 2), st1[:, c, 2:3], gain_row[:, :],
                                             ALU.mult, ALU.mult).then_inc(y_dve, 1)
                    dve.wait_ge(y_dve, START + Y_COUNT["z", c])
                    dve.wait_ge(xr_in[c % 2], 16 * (c // 2 + 1))
                    dve.wait_ge(x1_st, START + c - 1)
                    dve.tensor_tensor(x1n[c % 2][:, :], hn[c % 2][:, :], xr[c % 2][:, :], ALU.add).then_inc(y_x1, 1)
                if c > 0:
                    dve.wait_ge(y_t, START + c)
                    dve.wait_ge(y_lo, START + c - 1)
                    dve.tensor_tensor(tile, pair(2 + (c - 1) % 2).rearrange("p (k t) -> p k t", t=P), by_tile(scale_h[:, :]),
                                      ALU.mult).then_inc(y_dve, 1)
                    dve.wait_ge(y_dve, START + Y_COUNT["scale", c - 1])
                    dve.tensor_tensor(tile, tile, by_tile(mod_b[:, 8:16]), ALU.add).then_inc(y_dve, 1)
                if c < NCH:
                    dve.wait_ge(y_act, START + 2 * c + 2)
                    dve.reciprocal(st2[:, c, 2:3], st2[:, c, 1:2]).then_inc(y_dve, 1)
                if c > 0:
                    dve.wait_ge(y_hi, START + c)
                    cols = slice((c - 1) * P, c * P)
                    dve.tensor_tensor(x0_lo[:, :, cols], tile, x0_hi[:, :, cols].bitcast(F32), ALU.subtract).then_inc(y_lo, 1)

            def up(i, last):
                for j in range(2):
                    for m in range(2):
                        u = 2 * j + m
                        tile = FT * m + j
                        if not (last and u == 3):
                            ring_lo(R_UP + u + 1, i, 4)
                        dve.wait_ge(up_b, START + u + 1 + i * 4)
                        y = uy[j][m]
                        dve.scalar_tensor_tensor(y[:, GRID:T], pair(u)[:, 0:T - GRID],
                                                 vec[:, bass.ds(i * 6 + (V_FW + 3 * tile), 1)], y[:, GRID:T],
                                                 ALU.mult, ALU.add).then_inc(up_c, 1)
                        dve.wait_ge(up_c, START + 2 * u + 1 + i * 8)
                        dve.scalar_tensor_tensor(y[:, 0:T - GRID], pair(u)[:, GRID:T],
                                                 vec[:, bass.ds(i * 6 + (V_FW + 3 * tile + 2), 1)], y[:, 0:T - GRID],
                                                 ALU.mult, ALU.add).then_inc(up_c, 1)
                    dve.wait_ge(up_s, START + j + 1 + i * 2)
                    dve.wait_ge(up_c, START + 4 * (j + 1) + i * 8)
                    dve.wait_ge(a_st, START + j - 1 + i * 2)
                    dve.tensor_tensor(ua[j][:, :], uy[j][0][:, :], uy[j][1][:, :], ALU.mult).then_inc(up_a, 1)

            with dve.Fori(0, FT // 2 - 1) as i:
                up(i, False)
            up(FT // 2 - 1, True)

            dve.wait_ge(y_lo, START + NCH)
            dve.tensor_tensor(diag2[:, :, :], ident[:, :].unsqueeze(1).broadcast_to([P, KT, P]), by_tile(gain_f[:, :]),
                              ALU.mult).then_inc(dg_ok, 1)

            def down_lo(n, i, u):
                dve.wait_ge(dn_hi, START + 2 * (n + 1) + i * 4)
                dve.tensor_tensor(a_lo[u][:, :], a_raw[u][:, :], a_hi[u][:, :].bitcast(F32), ALU.subtract).then_inc(dn_lo, 1)
                dve.tensor_tensor(d_lo[u][:, :], d_raw[u][:, :], d_hi[u][:, :].bitcast(F32), ALU.subtract).then_inc(dn_lo, 1)

            def down(half, i, last):
                for u in range(2):
                    if not (last and half == 1 and u == 1):
                        down_lo(FT * half + u + 1, i, (u + 1) % 2)

            down_lo(0, 0, 0)
            for half in range(2):
                with dve.Fori(0, FT // 2 - 1) as i:
                    down(half, i, False)
                down(half, FT // 2 - 1, True)
                if half == 0:
                    for c in range(NCH):
                        dve.wait_ge(dn_sq, START + c + 1)
                        dve.tensor_copy(f0[:, c, :], ps[:, c, :]).then_inc(dn_ev, 1)
            dve.wait_ge(row_ok, 2)
            dve.wait_ge(dn_ev, START + NCH)
            for c in range(NCH):
                dve.wait_ge(dn_sq, START + NCH + c + 1)
                dve.tensor_tensor(fsum[:, c, 2:3], fsum[:, c, 0:1], fsum[:, c, 1:2], ALU.add).then_inc(dn_add, 1)
                dve.wait_ge(dn_rt, START + c + 1)
                dve.reciprocal(fsum[:, c, 4:5], fsum[:, c, 3:4]).then_inc(dn_dve, 1)
                dve.wait_ge(dn_dve, START + 3 * c + 1)
                if c > 1:
                    dve.wait_ge(out_st[c % 2], 16 * (c // 2))
                for n, part in ((0, f0[:, c, :]), (1, ps[:, c, :])):
                    cols = slice(n * HALF, (n + 1) * HALF)
                    dve.scalar_tensor_tensor(fo[c % 2][:, cols], part, fsum[:, c, 4:5], gain_row2[:, cols],
                                             ALU.mult, ALU.mult).then_inc(dn_dve, 1)

        @block.tensor
        def _(pe):
            for s in (pe_done, xt_ok, kt_ok, u_ok, sc_ok, o_ok, ogt_ok, adb_done, y_done, y_t, dn_pe):
                pe.sem_inc(s, START)

            def product(out, a, b, first, last):
                (ah, al), (bh, bl) = a, b
                pe.matmul(out, ah, bh, start=first, stop=False)
                pe.matmul(out, ah, bl, start=False, stop=False)
                return pe.matmul(out, al, bh, start=False, stop=last)

            def by_width(slot, x, out):
                for n in range(2):
                    for k in range(KT):
                        w = tuple(t[slot][:, k * P:(k + 1) * P] for t in (w_hi, w_lo))
                        xs = tuple(t[:, k, n * HALF:(n + 1) * HALF] for t in x)
                        done = product(out[:, n * HALF:(n + 1) * HALF], w, xs, k == 0, k == KT - 1)
                return done

            def by_tokens(slot, k, r, x, c, bank, first, last):
                xs = tuple(t[:, k, c * P:(c + 1) * P] for t in x)
                w = tuple(t[slot][:, r * HALF:(r + 1) * HALF] for t in (w_hi, w_lo))
                return product(ps[:, bank, :], xs, w, first, last)

            def transpose(out, tile):
                return pe.transpose(out, tile, ident[:, :])

            pe.wait_ge(vec_in, 16)
            pe.wait_ge(silu_ok, 1)
            with pe.Fori(0, 16 // ADA_RING) as i:
                for n in range(ADA_RING):
                    pe.wait_ge(ada_in[n], 16 + i * 16)
                    for k in range(KT):
                        done = pe.matmul(ps[:, 7, bass.ds(i * 2 * ADA_RING + 2 * n, 2)], ada_raw[n][:, k * P:(k + 1) * P],
                                         silu_c[:, k, :], start=(k == 0), stop=(k == KT - 1))
                    done.then_inc(ada_done, 1)
            pe.wait_ge(ident_in, 16)
            for n in range(10):
                pe.wait_ge(xn_ok, START + n + 1)
                if n >= 2:
                    pe.wait_ge(aff_ok, START + 2 * (n - 2) + 1)
                for k in range(KT):
                    done = transpose(pair(n % 2)[:, k * P:(k + 1) * P], xn[n % 2][:, k * P:(k + 1) * P])
                done.then_inc(xt_ok, 1)

            pe.wait_ge(h_lo, START + 2)
            pe.wait_ge(aff_ok, START + 20)
            with pe.Fori(0, 3) as i:
                for e in range(2):
                    for u in range(4):
                        pe.wait_ge(lo_done, START + R_CTX + 4 * e + u + 1 + i * 8)
                        for r in range(2):
                            k = 2 * u + r
                            for c in range(NCX):
                                if k == 0:
                                    pe.wait_ge(ctx_ev, START + 2 * (e - 2) + c + 1 + i * 4)
                                done = by_tokens(u % 2, k, r, (hc_hi, hc_lo), c, 2 * e + c, k == 0, k == KT - 1)
                                if k == KT - 1:
                                    done.then_inc(pe_done, 1)
                        if u < 3:
                            done.then_inc(pe_done, 1)

            pe.wait_ge(h_lo, START + 10)
            pe.wait_ge(ctx_ev, START + 12)
            with pe.Fori(0, 4) as i:
                for u in range(4):
                    pe.wait_ge(lo_done, START + R_QK + u + 1 + i * 4)
                    pe.wait_ge(rot_mul, START + 2 * (u + 1) - 8 + i * 8)
                    by_width(u % 2, (x0_hi, x0_lo), pair(u)).then_inc(pe_done, 1)

            pe.wait_ge(rot_mul, START + 32)
            with pe.Fori(0, 8) as b:
                for u in range(4):
                    pe.wait_ge(lo_done, START + R_VG + u + 1 + b * 4)
                    for r in range(2):
                        k = 2 * u + r
                        for c in range(NCH):
                            if k == 0:
                                pe.wait_ge(vg_ev, START + c - 7 + b * 8)
                            done = by_tokens(u % 2, k, r, (x0_hi, x0_lo), c, c, k == 0, k == KT - 1)
                            if k == KT - 1:
                                done.then_inc(pe_done, 1)
                    if u < 3:
                        done.then_inc(pe_done, 1)

            pe.wait_ge(vg_ev, START + 64)
            frees = ((cv_p, 0), (cv_s, 0), (cv_s, -1), (cv_x, 0), (cv_x, 1), (cv_p, 1))
            with pe.Fori(0, 4) as i:
                for u in range(6):
                    freed, n = frees[u]
                    pe.wait_ge(lo_done, START + R_CONV + u + 1 + i * 6)
                    pe.wait_ge(freed, START + n + i * 2)
                    by_width(u % 2, (x0_hi, x0_lo), pair(CONV_PAIR[u])).then_inc(pe_done, 1)

            pe.wait_ge(cv_s, START + 7)
            pe.wait_ge(cv_x, START + 8)
            with pe.Fori(0, 8) as i:
                for u in range(2):
                    pe.wait_ge(lo_done, START + R_GATE + u + 1 + i * 2)
                    pe.wait_ge(gate_ev, START + u - 1 + i * 2)
                    by_width(u % 2, (x0_hi, x0_lo), pair(2 + u)).then_inc(pe_done, 1)

            pe.wait_ge(cv_s, START + 8)
            pe.wait_ge(gate_ev, START + 16)
            with pe.Fori(0, 2) as i:
                for p in range(2):
                    u0 = N_U * p
                    z0 = N_KZ * p

                    def state(n, terms):
                        pe.wait_ge(st_ok, START + u0 + n - 1 + i * 2 * N_U)
                        for m, (a, b) in enumerate(terms):
                            done = pe.matmul(ps[:, 4 + n % 2, :], a, b, start=(m == 0), stop=(m == len(terms) - 1))
                        done.then_inc(u_ok, 1)

                    def transpose_k(m):
                        c = NCH - 1 - m
                        pe.wait_ge(kz_ok, START + z0 + (KZ_END[m - 2] if m > 1 else 0) + i * 2 * N_KZ)
                        if m < 2:
                            pe.wait_ge(ms_ok, START + NCH * p + i * 16)
                        for k in range(2):
                            done = transpose(ps[:, m % 2, k * P:(k + 1) * P], k_t[p][:, k, c * P:(c + 1) * P])
                        done.then_inc(kt_ok, 1)

                    pe.wait_ge(ret_in[p], 80 + i * 80)
                    transpose_k(0)
                    transpose_k(1)
                    for d, kcw in enumerate((kcw_b, kcw_f)):
                        pe.wait_ge(kcw_ok, START + 4 * p + 2 * (d + 1) + i * 8)
                        for t in range(2):
                            state(2 * d + t, [(kcw[:, m, t * P:(t + 1) * P], vc_n[p][:, m, :]) for m in range(NCX)])
                    for m in range(NCH - 1):
                        c = NCH - 1 - m
                        pe.wait_ge(kz_ok, START + z0 + KZ_B[m] + i * 2 * N_KZ)
                        for t in range(2):
                            state(4 + 2 * m + t, [(kz_b[:, m % 2, t * P:(t + 1) * P], v_n[p][:, c, :])])
                        if m + 2 < NCH:
                            transpose_k(m + 2)
                    pe.wait_ge(kz_ok, START + z0 + N_KZ + i * 2 * N_KZ)

                    def scores(c):
                        pe.wait_ge(ms_ok, START + NCH * p + c - 1 + i * 16)
                        for k in range(2):
                            done = pe.matmul(ps[:, c % 2, 0:P], k_t[p][:, k, c * P:(c + 1) * P],
                                             q_t[p][:, k, c * P:(c + 1) * P], start=(k == 0), stop=(k == 1))
                        done.then_inc(sc_ok, 1)

                    def transpose_out(c):
                        n = NCH * p + c
                        pe.wait_ge(og_ok, START + n + 1 + i * 16)
                        pe.wait_ge(ogc_ok, START + n + i * 16)
                        for t in range(4):
                            done = transpose(ps[:, 6, t * P:(t + 1) * P], og[c % 2][:, t * P:(t + 1) * P])
                        done.then_inc(ogt_ok, 1)

                    scores(0)
                    pe.wait_ge(q_ok, START + 2 * (p + 1) + i * 4)
                    for c in range(NCH):
                        n = NCH * p + c
                        if c + 1 < NCH:
                            scores(c + 1)
                        pe.wait_ge(og_ok, START + n - 1 + i * 16)
                        pe.wait_ge(ms_ok, START + n + 1 + i * 16)
                        out = ps[:, 2 + c % 2, :]
                        pe.matmul(out, s_sc[:, c % 2, :], v_n[p][:, c, :], start=True, stop=False)
                        pe.wait_ge(st_ok, START + u0 + 18 + 2 * c + i * 2 * N_U)
                        for k in range(2):
                            pe.matmul(out, q_b[:, k, c * P:(c + 1) * P], s_bw[:, c, k, :], start=False, stop=False)
                        for k in range(2):
                            done = pe.matmul(out, q_f[:, k, c * P:(c + 1) * P], s_fw[:, c % 2, k, :], start=False, stop=(k == 1))
                        done.then_inc(o_ok, 1)
                        if c + 1 < NCH:
                            for t in range(2):
                                state(18 + 2 * c + t, [(kz_f[:, c, t * P:(t + 1) * P], v_n[p][:, c, :])])
                        pe.wait_ge(adb_in[c % 2], 16 * (NCH // 2 * p + c // 2 + 1) + i * 128)
                        for k in range(KT):
                            done = pe.matmul(ps[:, 7, bass.ds(i * 16 + n, 1)], ada_ret[c % 2][:, k * P:(k + 1) * P],
                                             silu_c[:, k, 0:1], start=(k == 0), stop=(k == KT - 1))
                        done.then_inc(adb_done, 1)
                        if c > 0:
                            transpose_out(c - 1)
                    transpose_out(NCH - 1)

            pe.wait_ge(lo_done, START + R_A)
            for stage, (base, count, x, per) in enumerate(((R_A, P_A, (x1_hi, x1_lo), 4), (R_B, P_B, (x0_hi, x0_lo), 4),
                                                           (R_C, P_C, (x1_hi, x1_lo), 2))):
                with pe.Fori(0, 4) as i:
                    for j in range(2):
                        pe.wait_ge(lo_done, START + base + per // 2 * j + 1 + i * per)
                        pe.wait_ge(mg_mul, START + 16 * stage + 2 * j - 2 + i * 4)
                        by_width(j, x, pair(j)).then_inc(pe_done, 1)

            def gain(n, d):
                pe.wait_ge(dg_ok, n)
                for h in range(2):
                    done = pe.matmul(pair(1 + n)[:, h * HALF:(h + 1) * HALF], ones[:, :],
                                     d[:, 4 * h:4 * h + 4, :].rearrange("p k t -> p (k t)"), start=True, stop=True)
                done.then_inc(row_mm, 1)

            gain(1, diag)
            pe.wait_ge(mg_mul, START + 48)
            pe.wait_ge(m_lo, START + KT)
            pe.wait_ge(lo_done, START + R_UP)
            pe.wait_ge(row_ok, 1)
            for c in range(NCH + 1):
                if c < NCH:
                    if c > 1:
                        pe.wait_ge(y_dve, START + Y_COUNT["z", c - 2])
                    for h in range(2):
                        for k in range(KT):
                            xs = tuple(t[:, k, c * P:(c + 1) * P] for t in (x0_hi, x0_lo))
                            w = tuple(t[:, k, h * HALF:(h + 1) * HALF] for t in (x1_hi, x1_lo))
                            done = product(pair(c % 2)[:, h * HALF:(h + 1) * HALF], xs, w, k == 0, k == KT - 1)
                    done.then_inc(y_done, 1)
                if c > 0:
                    pe.wait_ge(y_hn, START + c)
                    if c > 2:
                        pe.wait_ge(y_dve, START + Y_COUNT["scale", c - 3])
                    for k in range(KT):
                        done = transpose(pair(2 + (c - 1) % 2)[:, k * P:(k + 1) * P], hn[(c - 1) % 2][:, k * P:(k + 1) * P])
                    done.then_inc(y_t, 1)

            pe.wait_ge(y_lo, START + NCH)
            with pe.Fori(0, FT // 2) as i:
                for u in range(4):
                    pe.wait_ge(lo_done, START + R_UP + u + 1 + i * 4)
                    pe.wait_ge(up_c, START + 2 * (u + 1) - 8 + i * 8)
                    by_width(u % 2, (x0_hi, x0_lo), pair(u)).then_inc(pe_done, 1)

            pe.wait_ge(up_c, START + 4 * FT)
            gain(2, diag2)
            pe.wait_ge(row_ok, 2)

            def down(half, i, u, first, last):
                pe.wait_ge(dn_lo, START + 2 * (FT * half + u + 1) + i * 4)
                for c in range(NCH):
                    if first and half == 1:
                        pe.wait_ge(dn_ev, START + c + 1)
                    done = product(ps[:, c, :], tuple(t[u][:, c * P:(c + 1) * P] for t in (a_hi, a_lo)),
                                   tuple(t[u][:, :] for t in (d_hi, d_lo)), first, last)
                    if last:
                        done.then_inc(dn_pe, 1)
                if not last:
                    done.then_inc(dn_pe, 1)

            for half in range(2):
                down(half, 0, 0, True, False)
                down(half, 0, 1, False, False)
                with pe.Fori(1, FT // 2 - 1) as i:
                    for u in range(2):
                        down(half, i, u, False, False)
                down(half, FT // 2 - 1, 0, False, False)
                down(half, FT // 2 - 1, 1, False, True)


def kernel(**inputs):
    import concourse.bacc as bacc
    from concourse.bass_utils import run_bass_kernel_spmd

    a = {k: np.asarray(v) for k, v in inputs.items()}

    def cols(v):
        return np.ascontiguousarray(v.reshape(-1, P).T)

    def by_column_tile(w):
        k, n = w.shape
        return np.ascontiguousarray(w.reshape(k // P, P, n // P, P).transpose(2, 1, 0, 3)).reshape(n // P, P, k)

    def by_column_block(w):
        k, n = w.shape
        return np.ascontiguousarray(w.reshape(k // 256, 2, P, n // HALF, HALF).transpose(3, 0, 2, 1, 4))\
            .reshape(n // HALF, k // 256, P, 1024)

    w_in = a["w_in"][0]
    cx_, cb_, cc_, q_, k_, v_, g_, ga_, gb_ = np.split(w_in, np.cumsum([D, D, D, D, D, 2 * D, 2 * D, D]), axis=1)
    conv_tiles = np.stack([by_column_tile(cx_), by_column_tile(cc_), by_column_tile(cb_)], axis=1).reshape(24, P, D)
    ret = a["w_ret_out"][0]
    up = by_column_tile(a["w_ffn_up"][0])
    fw = a["ffn_conv_w"][0].reshape(3, 2 * FT, P).transpose(2, 1, 0).reshape(P, 6 * FT)
    decay = np.concatenate([a["ret_decay_fw"][0], a["ret_decay_bw"][0]])
    vecs = np.concatenate(
        [cols(a["c"][0]), cols(a["c_ctx"]), cols(a["b_ada"][0]), cols(a["norm_mix_pre"][0]), cols(a["norm_mix_post"][0]),
         cols(a["norm_ffn_pre"][0]), cols(a["norm_ffn_post"][0]), cols(a["conv_w"][0]), cols(a["conv_b"][0]), fw,
         cols(a["ffn_conv_b"][0]), np.repeat(decay[None], P, axis=0)], axis=1)
    assert vecs.shape == (P, V_N)

    m, n = np.arange(P)[:, None], np.arange(P)[None, :]
    consts = np.zeros((P, C_N), np.float32)
    consts[:, C_ID:C_ID + P] = np.eye(P)
    consts[:, C_DPOS:C_DPOS + P] = np.maximum(n - m, 0)
    consts[:, C_DNEG:C_DNEG + P] = np.maximum(m - n, 0)
    consts[:, C_GE:C_GE + P] = (n >= m) * K_SCALE
    consts[:, C_LT:C_LT + P] = (n < m) * K_SCALE
    consts[:, C_RF:C_RF + P] = n + 1
    consts[:, C_RB:C_RB + P] = P - n
    consts[:, C_COLF:C_COLF + 4] = np.concatenate([P - 1 - m, CTX - 1 - m, P - 1 - m, 0 * m + P], axis=1)
    consts[:, C_COLB:C_COLB + 4] = np.concatenate([m, m, P + m, 0 * m + P], axis=1)

    pairs = DK // 4
    inv = np.float32(10000.0) ** (-np.arange(pairs, dtype=np.float32) / np.float32(pairs))
    t = np.arange(T)
    ang = np.concatenate([(t // GRID).astype(np.float32)[:, None] * inv, (t % GRID).astype(np.float32)[:, None] * inv], axis=1)
    trig = np.stack([np.cos(ang).T, np.sin(ang).T]).astype(np.float32)

    arrays = {
        "x": a["x"][0],
        "ctx": a["ctx"][0],
        "vecs": vecs,
        "consts": consts,
        "trig": np.ascontiguousarray(trig),
        "w_ada_t": by_column_tile(a["w_ada"][0]),
        "w_n": np.concatenate([by_column_block(k_), by_column_block(v_), by_column_block(g_)]),
        "w_t": np.concatenate([by_column_tile(q_), by_column_tile(k_), conv_tiles, by_column_tile(ga_), by_column_tile(gb_)]),
        "w_m": np.concatenate([by_column_tile(a["w_conv_out"][0]), by_column_tile(ret[:D]), by_column_tile(ret[D:])]),
        "w_o_t": a["w_o"][0].reshape(KT, P, D),
        "w_up_t": np.stack([up[:FT], up[FT:]], axis=1).reshape(2 * FT, P, D),
        "w_dn_t": a["w_ffn_down"][0].reshape(FT, P, D),
    }
    nc = bacc.Bacc("TRN2", target_bir_lowering=False, num_devices=1)
    io = {}
    for name, v in arrays.items():
        arrays[name] = np.ascontiguousarray(v)
        io[name] = nc.dram_tensor(name, arrays[name].shape, mybir.dt.from_np(v.dtype), kind="ExternalInput").ap()
    io["out"] = nc.dram_tensor("out", (T, D), F32, kind="ExternalOutput").ap()
    build(nc, io)
    r = run_bass_kernel_spmd(nc, [arrays], core_ids=[0])
    return r.results[0]["out"].reshape(1, T, D)
```

```python
import math

import numpy as np

import concourse.bass as bass
from concourse import mybir

F32 = mybir.dt.float32
F32R = mybir.dt.float32r
ACT = mybir.ActivationFunctionType
ALU = mybir.AluOpType

START = 256

P = 128
D = 1024
T = 1024
CTX = 256
GRID = 64
KT = D // P
NCH = T // P
NCX = CTX // P
HALF = 512
HEADS = 4
DK, DV = 256, 512
FF = 2816
FT = FF // P
EPS = 1e-6
K_SCALE = 1.0 / math.sqrt(DK)

V_C, V_CC, V_BADA = 0, 8, 16
V_GMIX, V_GPOST, V_GFFN, V_GFPOST = 64, 72, 80, 88
V_CW, V_CB = 96, 120
V_FW, V_FB = 128, 260
V_DEC = 304
V_N = 312

C_ID, C_DPOS, C_DNEG, C_GE, C_LT, C_RF, C_RB = 0, 128, 256, 384, 512, 640, 768
C_COLF, C_COLB = 896, 900
C_N = 904

H_D, H_XF, H_XB, H_F, H_B = 0, 128, 256, 384, 388
H_N = 392

R_CTX = 0
R_QK = R_CTX + 24
R_VG = R_QK + 16
R_CONV = R_VG + 32
R_GATE = R_CONV + 24
R_CO = R_GATE + 16
R_A = R_CO + 8
R_B = R_A + 16
R_C = R_B + 16
R_WO = R_C + 8
R_UP = R_WO + 8
R_END = R_UP + 2 * FT

P_CTX = 0
P_QK = P_CTX + 6 * 5
P_VG = P_QK + 16
P_CONV = P_VG + 8 * 11
P_GATE = P_CONV + 24
P_A = P_GATE + 16
P_B = P_A + 8
P_C = P_B + 8
P_UP = P_C + 8

ST_KVC = 0
ST_QK = ST_KVC + 6
ST_VG = ST_QK + 2 * HEADS
ST_CO = ST_VG + 8 * NCH
ST_GATE = ST_CO + KT
ST_GO = ST_GATE + 2 * KT
ST_X1 = ST_GO + HEADS * NCH
ST_A = ST_X1 + NCH

ADA = 2 * D
CONV_PAIR = (0, 1, 2, 3, 0, 1)
N_DOWN = FT - 1 + NCH

N_U = 4 + 2 * 2 * (NCH - 1)
KZ_B, KZ_END = [], []
for _m in range(NCH):
    _n = KZ_END[-1] if KZ_END else 0
    KZ_B.append(_n + 1)
    KZ_END.append(_n + (_m < NCH - 1) + (_m > 0))
N_KZ = KZ_END[-1]

Y_COUNT = {}
for _c in range(NCH + 1):
    for _step, _of in (("inv1", _c), ("z", _c), ("scale", _c - 1), ("shift", _c - 1), ("inv2", _c)):
        if 0 <= _of < NCH:
            Y_COUNT[_step, _of] = len(Y_COUNT) + 1

DC_T, DC_AZ, DC_U, DC_W, DC_LN, DC_CORR, DC_RW, DC_LG = range(8)


def build(nc, io):
    ps = nc.alloc_psum_tensor("ps", [P, 8, HALF], F32)

    def pair(n):
        return ps[:, 2 * n:2 * n + 2, :].rearrange("p b c -> p (b c)")

    kb = 1024
    PERS = 16640
    RING = PERS + 12 * kb
    X0 = RING + 24 * kb
    X1 = X0 + 64 * kb
    REST = X1 + 64 * kb
    end = nc.sbuf_usable_end
    top = [0]

    def sb(name, shape, at, dt=F32):
        size = 4 * int(np.prod(shape[1:]))
        assert at + size <= end, (name, at + size, end)
        top[0] = at + size
        return nc.alloc_sbuf_tensor_at(name, shape, dt, offset=at)

    def after(align=32):
        return -(-top[0] // align) * align

    vec = sb("vec", [P, V_N], PERS)
    ident = sb("ident", [P, P], after())
    ones = sb("ones", [P, P], after())
    silu_c = sb("silu_c", [P, KT, 2], after())
    mod_a = sb("mod_a", [P, 16, 2], after())
    mod_b = sb("mod_b", [P, 32], after())
    scale_x = sb("scale_x", [P, KT, 2], after())
    scale_h = sb("scale_h", [P, KT], after())
    gain_y = sb("gain_y", [P, KT], after())
    gain_f = sb("gain_f", [P, KT], after())
    head_tab = sb("head_tab", [P, HEADS, H_N], after())
    dec = sb("dec", [P, 8, 8], after())
    onum = sb("onum", [P, 2, 4], after())
    eps = sb("eps", [P, 1], after())
    st1 = sb("st1", [P, 8, 4], after())
    st2 = sb("st2", [P, 8, 4], after())
    assert top[0] <= RING, top[0] - RING

    raw = [sb(f"raw{n}", [P, 1024], RING + 4096 * n) for n in range(2)]
    w_hi = [sb(f"w_hi{n}", [P, 1024], RING + 8192 + 4096 * n, F32R) for n in range(2)]
    w_lo = [sb(f"w_lo{n}", [P, 1024], RING + 16384 + 4096 * n, F32R) for n in range(2)]

    x0_hi = sb("x0_hi", [P, KT, T], X0, F32R)
    x0_lo = sb("x0_lo", [P, KT, T], X0 + 32 * kb, F32R)
    x1_hi = sb("x1_hi", [P, KT, T], X1, F32R)
    x1_lo = sb("x1_lo", [P, KT, T], X1 + 32 * kb, F32R)

    hc_hi = sb("hc_hi", [P, KT, CTX], X1, F32R)
    hc_lo = sb("hc_lo", [P, KT, CTX], after(), F32R)
    x_in = sb("x_in", [P, KT, T], after())
    ctx_in = sb("ctx_in", [P, KT, CTX], after())
    ctx_h = sb("ctx_h", [P, KT, CTX], after())
    x_sq = [sb(f"x_sq{n}", [P, T], REST + 4096 * n) for n in range(2)]
    x_sum = sb("x_sum", [P, T], REST + 8192)
    inv_x = sb("inv_x", [P, T], REST + 12288)
    aff = [sb(f"aff{n}", [P, T], REST + 16384 + 4096 * n) for n in range(2)]
    ctx_out = [sb(f"ctx_out{n}", [P, NCX, HALF], REST + 24576 + 4096 * n) for n in range(2)]
    const = sb("const", [P, C_N], after())
    dtmp = sb("dtmp", [P, HEADS, P], after())
    inv_c = sb("inv_c", [P, CTX], after())
    ada_raw = sb("ada_raw", [P, KT, ADA], X0)
    mod_row = sb("mod_row", [2, 4, HALF], REST + 16384)

    cos = sb("cos", [P, T], X1)
    sin = sb("sin", [P, T], X1 + 4 * kb)
    rot_a = [sb(f"rot_a{n}", [P, 2, T], X1 + (8 + 8 * n) * kb) for n in range(2)]
    rot_b = [sb(f"rot_b{n}", [P, 2, T], X1 + (24 + 8 * n) * kb) for n in range(2)]
    rot_o = [sb(f"rot_o{n}", [P, 2, T], X1 + (40 + 8 * n) * kb) for n in range(2)]
    vg_out = [sb(f"vg_out{n}", [P, HALF], REST + 2048 * n) for n in range(8)]
    cx = [sb(f"cx{n}", [P, T], X1 + (0 + 16 * n) * kb) for n in range(2)]
    cprod = [sb(f"cprod{n}", [P, T], X1 + (4 + 16 * n) * kb) for n in range(2)]
    cy = [sb(f"cy{n}", [P, T], X1 + (8 + 16 * n) * kb) for n in range(2)]
    co = [sb(f"co{n}", [P, T], X1 + (12 + 16 * n) * kb) for n in range(2)]
    gate_o = [sb(f"gate_o{n}", [P, T], X1 + (32 + 4 * n) * kb) for n in range(2)]

    at = X0
    q_t = [sb(f"q_t{n}", [P, 2, T], at + n * 8 * kb) for n in range(2)]
    at += 16 * kb
    k_t = [sb(f"k_t{n}", [P, 2, T], at + n * 8 * kb) for n in range(2)]
    at += 16 * kb
    v_n = [sb(f"v_n{n}", [P, NCH, DV], at + n * 16 * kb) for n in range(2)]
    at += 32 * kb
    kc_n = [sb(f"kc_n{n}", [P, NCX, DK], at + n * 2 * kb) for n in range(2)]
    at += 4 * kb
    vc_n = [sb(f"vc_n{n}", [P, NCX, DV], at + n * 4 * kb) for n in range(2)]
    at += 8 * kb
    s_bw = sb("s_bw", [P, NCH, 2, DV], at)
    at += 32 * kb
    s_fw = sb("s_fw", [P, 2, 2, DV], at)
    at += 8 * kb
    kz_f = sb("kz_f", [P, NCH, DK], at)
    at += 8 * kb
    kz_b = sb("kz_b", [P, 2, DK], at)
    at += 2 * kb
    q_f = sb("q_f", [P, 2, T], at)
    at += 8 * kb
    q_b = sb("q_b", [P, 2, T], at)
    at += 8 * kb
    kcw_f = sb("kcw_f", [P, NCX, DK], at)
    kcw_b = sb("kcw_b", [P, NCX, DK], at + 2 * kb)
    at += 4 * kb
    s_sc = sb("s_sc", [P, 2, P], at)
    at += kb
    g_in = [sb(f"g_in{n}", [P, DV], at + n * 2 * kb) for n in range(2)]
    at += 4 * kb
    og = [sb(f"og{n}", [P, DV], at + n * 2 * kb) for n in range(2)]
    at += 4 * kb
    og_t = [sb(f"og_t{n}", [P, 4, P], at + n * 2 * kb) for n in range(2)]
    at += 4 * kb
    sq_j = sb("sq_j", [P, DV], at)
    at += 2 * kb
    hd = [sb(f"hd{n}", [P, H_N], at + n * 1600) for n in range(2)]
    at += 3200
    ada_acc = sb("ada_acc", [P, D], at)
    ada_ret = raw

    merged = sb("merged", [P, KT, T], REST)
    gate_in = [sb(f"gate_in{n}", [P, T], REST + (32 + 4 * n) * kb) for n in range(2)]
    mtmp = sb("mtmp", [P, HALF], REST + 40 * kb)
    gain_row = sb("gain_row", [P, D], REST)
    diag = sb("diag", [P, KT, P], REST + 4 * kb)
    xr = [sb(f"xr{n}", [P, D], REST + (8 + 4 * n) * kb) for n in range(2)]
    x1n = [sb(f"x1n{n}", [P, D], REST + (16 + 4 * n) * kb) for n in range(2)]
    hn = [sb(f"hn{n}", [P, D], REST + (24 + 4 * n) * kb) for n in range(2)]
    haff = sb("haff", [P, D], REST + 32 * kb)
    junk2 = sb("junk2", [P, D], REST + 36 * kb)
    uy = [[sb(f"uy{n}{m}", [P, T], X1 + (12 * n + 4 * m) * kb) for m in range(2)] for n in range(2)]
    ua = [sb(f"ua{n}", [P, T], X1 + (12 * n + 8) * kb) for n in range(2)]
    a_raw = [sb(f"a_raw{n}", [P, T], X1 + (24 + 4 * n) * kb) for n in range(2)]
    d_raw = [sb(f"d_raw{n}", [P, HALF], X1 + (32 + 2 * n) * kb) for n in range(2)]
    d_hi = [sb(f"d_hi{n}", [P, HALF], X1 + (36 + 2 * n) * kb, F32R) for n in range(2)]
    d_lo = [sb(f"d_lo{n}", [P, HALF], X1 + (40 + 2 * n) * kb, F32R) for n in range(2)]
    a_hi = [sb(f"a_hi{n}", [P, T], X1 + (44 + 4 * n) * kb, F32R) for n in range(2)]
    a_lo = [sb(f"a_lo{n}", [P, T], X1 + (52 + 4 * n) * kb, F32R) for n in range(2)]
    f0 = sb("f0", [P, NCH, HALF], X0)
    x1all = sb("x1all", [P, NCH, D], X0 + 16 * kb)
    fo = [sb(f"fo{n}", [P, D], X0 + (48 + 4 * n) * kb) for n in range(2)]
    junk3 = sb("junk3", [P, HALF], REST + 4 * kb)
    fsum = sb("fsum", [P, 8, 8], REST + 8 * kb)

    def dram(name, shape):
        return nc.dram_tensor(name, shape, F32).ap()

    kvc_d = dram("kvc_d", [6, P, NCX, HALF])
    qk_d = dram("qk_d", [2 * HEADS, P, 2, T])
    vg_d = dram("vg_d", [2 * HEADS, NCH, P, DV])
    co_d = dram("co_d", [KT, P, T])
    gate_d = dram("gate_d", [2 * KT, P, T])
    go_d = dram("go_d", [HEADS * 4, P, T])
    x1_d = dram("x1_d", [NCH, P, D])
    a_d = dram("a_d", [FT, P, T])

    def sem(name):
        return nc.alloc_semaphore(name)

    vec_in, ident_in, const_in, ctx_ready = sem("vec_in"), sem("ident_in"), sem("const_in"), sem("ctx_ready")
    x_ready = [sem(f"x_ready{n}") for n in range(4)]
    ada_in = [sem(f"ada_in{n}") for n in range(KT)]
    row_sum, row_act, row_dve = sem("row_sum"), sem("row_act"), sem("row_dve")
    silu_ok, ada_done, mod_ok = sem("silu_ok"), sem("ada_done"), sem("mod_ok")
    act0, dve0 = sem("act0"), sem("dve0")
    csq_ok, xsq_ok, csum_ok, xsum_ok, sum_mm, root_ok, inv_ok, z_ok, ca_ok, cb_ok, aff_ok, hc_hi_ok, hc_lo_ok, h_hi, h_lo = (
        sem(n) for n in ("csq_ok", "xsq_ok", "csum_ok", "xsum_ok", "sum_mm", "root_ok", "inv_ok", "z_ok", "ca_ok", "cb_ok",
                         "aff_ok", "hc_hi_ok", "hc_lo_ok", "h_hi", "h_lo"))
    setup_ok = sem("setup_ok")
    raw_in = [sem("raw_in0"), sem("raw_in1")]
    hi_done, lo_done, pe_done = sem("hi_done"), sem("lo_done"), sem("pe_done")
    kvc_st, qk_st, vg_st, co_st, gate_st, go_st, x1_st, a_st = (
        sem(n) for n in ("kvc_st", "qk_st", "vg_st", "co_st", "gate_st", "go_st", "x1_st", "a_st"))
    out_st = [sem("out_st0"), sem("out_st1")]
    landed = sem("landed")
    ctx_ev, trig_in, rot_mul, rot_add, vg_ev = (sem(n) for n in ("ctx_ev", "trig_in", "rot_mul", "rot_add", "vg_ev"))
    cv_x, cv_p, cv_b, cv_y, cv_s = (sem(n) for n in ("cv_x", "cv_p", "cv_b", "cv_y", "cv_s"))
    gate_ev = sem("gate_ev")
    ret_in, g_ld = [sem("ret_in0"), sem("ret_in1")], [sem("g_ld0"), sem("g_ld1")]
    (hd_ok, q_ok, kcw_ok, kt_ok, kz_ok, u_ok, st_ok, sc_ok, ms_ok, o_ok, osq_ok, ort_ok,
     oinv_ok, og_ok, ogt_ok, ogc_ok) = (sem(n) for n in (
         "hd_ok", "q_ok", "kcw_ok", "kt_ok", "kz_ok", "u_ok", "st_ok", "sc_ok", "ms_ok", "o_ok", "osq_ok",
         "ort_ok", "oinv_ok", "og_ok", "ogt_ok", "ogc_ok"))
    adb_in, adb_mul, adb_done = [sem("adb_in0"), sem("adb_in1")], sem("adb_mul"), sem("adb_done")
    gt_in, mg_mul, mg_add = [sem("gt_in0"), sem("gt_in1")], sem("mg_mul"), sem("mg_add")
    m_hi, m_lo = sem("m_hi"), sem("m_lo")
    dg_ok, row_mm, row_ok = sem("dg_ok"), sem("row_mm"), sem("row_ok")
    xr_in, y_done, y_sq, y_act, y_dve, y_x1, y_hn, y_t, y_hi, y_lo = (
        [sem("xr_in0"), sem("xr_in1")], *(sem(n) for n in (
            "y_done", "y_sq", "y_act", "y_dve", "y_x1", "y_hn", "y_t", "y_hi", "y_lo")))
    up_b, up_c, up_s, up_a = (sem(n) for n in ("up_b", "up_c", "up_s", "up_a"))
    dn_in, dn_hi, dn_lo, dn_pe, dn_ev, dn_sq, dn_add, dn_dve, dn_rt, x1_in, out_ok = (
        [sem("dn_in0"), sem("dn_in1")], *(sem(n) for n in (
            "dn_hi", "dn_lo", "dn_pe", "dn_ev", "dn_sq", "dn_add", "dn_dve", "dn_rt", "x1_in", "out_ok")))

    with nc.Block() as block:

        @block.sync
        def _(sp):
            def load(base, i, per, src):
                sp.wait_ge(lo_done, START + base - 1 + i * per)
                sp.dma_start(raw[base % 2][:, :], src).then_inc(raw_in[base % 2], 16)

            sp.dma_start(vec[:, :], io["vecs"]).then_inc(vec_in, 16)
            sp.dma_start(ident[:, :], io["consts"][:, C_ID:C_ID + P]).then_inc(ident_in, 16)
            sp.dma_start(ctx_in[:, :, :], io["ctx_t"]).then_inc(ctx_ready, 16)
            for k in range(KT):
                sp.dma_start(ada_raw[:, k, :], io["w_ada_a"][k]).then_inc(ada_in[k], 16)
            for u in range(2):
                load(R_CTX + u, 0, 0, io["w_n"][0, u])
            for n in range(4):
                sp.dma_start(x_in[:, 2 * n:2 * n + 2, :],
                             io["x_t"][2 * n:2 * n + 2].rearrange("n p d -> p n d")).then_inc(x_ready[n], 16)
            for u in range(2, 4):
                load(R_CTX + u, 0, 0, io["w_n"][0, u])
            sp.dma_start(const[:, :], io["consts"]).then_inc(const_in, 16)
            with sp.Fori(1, 6) as b:
                for u in range(4):
                    load(R_CTX + u, b, 4, io["w_n"][b, u])
            for u in range(2):
                load(R_QK + u, 0, 0, io["w_t"][u])
            sp.wait_ge(pe_done, START + P_QK)
            sp.dma_start(cos[:, :], io["trig"][0]).then_inc(trig_in, 16)
            sp.dma_start(sin[:, :], io["trig"][1]).then_inc(trig_in, 16)
            for u in range(2, 4):
                load(R_QK + u, 0, 0, io["w_t"][u])
            with sp.Fori(1, 4) as i:
                for u in range(4):
                    load(R_QK + u, i, 4, io["w_t"][i * 4 + u])
            with sp.Fori(0, 8) as b:
                for u in range(4):
                    load(R_VG + u, b, 4, io["w_n"][b + 2, u])
            with sp.Fori(0, 4) as i:
                for u in range(6):
                    load(R_CONV + u, i, 6, io["w_t"][i * 6 + (16 + u)])
            with sp.Fori(0, 8) as i:
                for u in range(2):
                    load(R_GATE + u, i, 2, io["w_t"][i * 2 + (40 + u)])

            sp.wait_ge(pe_done, START + P_A)
            sp.wait_ge(gate_st, START + 16)
            sp.wait_ge(co_st, START + 8)
            sp.wait_ge(vg_st, START + 64)
            sp.wait_ge(qk_st, START + 8)

            def head_loads(h):
                p = h % 2
                sp.dma_start(q_t[p][:, :, :], qk_d[h]).then_inc(ret_in[p], 16)
                sp.dma_start(k_t[p][:, :, :], qk_d[h + HEADS]).then_inc(ret_in[p], 16)
                sp.dma_start(v_n[p][:, :, :], vg_d[h].rearrange("c p d -> p c d")).then_inc(ret_in[p], 16)
                sp.dma_start(kc_n[p][:, :, :], kvc_d[h // 2, :, :, p * DK:(p + 1) * DK]).then_inc(ret_in[p], 16)
                sp.dma_start(vc_n[p][:, :, :], kvc_d[h + 2]).then_inc(ret_in[p], 16)

            head_loads(0)
            head_loads(1)
            for h in range(HEADS):
                with sp.Fori(0, NCH // 2) as i:
                    for e in range(2):
                        n = h * NCH + e
                        sp.wait_ge(og_ok, START + n - 1 + i * 2)
                        sp.dma_start(g_in[e][:, :], vg_d[h + HEADS, i * 2 + e]).then_inc(g_ld[e], 16)
                        sp.wait_ge(adb_mul, START + n - 1 + i * 2)
                        sp.dma_start(ada_ret[e][:, :], io["w_ada_b"][h, i * 2 + e]).then_inc(adb_in[e], 16)
                if h + 2 < HEADS:
                    sp.wait_ge(ogt_ok, START + NCH * (h + 1))
                    sp.wait_ge(q_ok, START + 2 * (h + 1))
                    head_loads(h + 2)

            sp.wait_ge(go_st, START + HEADS * NCH)

            def gate_load(stage, j, i, src):
                sp.wait_ge(mg_mul, START + 2 * (8 * stage + j - 1) + i * 4)
                sp.dma_start(gate_in[j % 2][:, :], src).then_inc(gt_in[j % 2], 16)

            with sp.Fori(0, 4) as i:
                for j in range(2):
                    load(R_CO + j, i, 2, co_d[i * 2 + j])
            for stage, (base, gate_row) in enumerate(((R_A, 0), (R_B, 8))):
                with sp.Fori(0, 4) as i:
                    for j in range(2):
                        load(base + 2 * j, i, 4, io["w_m"][i * 2 + (8 * stage + j)])
                        load(base + 2 * j + 1, i, 4, go_d[i * 2 + (8 * stage + j)])
                        gate_load(stage, j, i, gate_d[i * 2 + (gate_row + j)])
            with sp.Fori(0, 4) as i:
                for j in range(2):
                    load(R_C + j, i, 2, io["w_m"][i * 2 + (16 + j)])
                    gate_load(2, j, i, gate_d[i * 2 + (8 + j)])
            with sp.Fori(0, 4) as i:
                for j in range(2):
                    load(R_WO + j, i, 2, io["w_o_t"][i * 2 + j])
            load(R_UP, 0, 0, io["w_up_t"][0])
            load(R_UP + 1, 0, 0, io["w_up_t"][1])
            sp.wait_ge(m_lo, START + KT)
            for c in range(NCH):
                sp.wait_ge(y_x1, START + c - 1)
                sp.dma_start(xr[c % 2][:, :], io["x"][c * P:(c + 1) * P, :]).then_inc(xr_in[c % 2], 16)

            for u in range(2, 4):
                load(R_UP + u, 0, 0, io["w_up_t"][u])
            with sp.Fori(1, FT // 2 - 1) as i:
                for u in range(4):
                    load(R_UP + u, i, 4, io["w_up_t"][i * 4 + u])

            def down_load(half, u, i):
                sp.wait_ge(dn_lo, START + 2 * (half * FT + u - 1) + i * 4)
                sp.dma_start(d_raw[u][:, :], io["w_dn_t"][i * 2 + u, :, half * HALF:(half + 1) * HALF])\
                  .then_inc(dn_in[u], 16)
                if half == 0:
                    sp.wait_ge(a_st, START + u + 1 + i * 2)
                sp.dma_start(a_raw[u][:, :], a_d[i * 2 + u]).then_inc(dn_in[u], 16)

            down_load(0, 0, 0)
            down_load(0, 1, 0)
            for u in range(4):
                load(R_UP + 2 * FT - 4 + u, 0, 0, io["w_up_t"][2 * FT - 4 + u])

            for half in range(2):
                with sp.Fori(1 - half, FT // 2) as i:
                    for u in range(2):
                        down_load(half, u, i)
                if half == 0:
                    sp.wait_ge(pe_done, START + P_UP + 2 * FT)
                    sp.wait_ge(x1_st, START + NCH)
                    sp.dma_start(x1all[:, :, :], x1_d.rearrange("c p d -> p c d")).then_inc(x1_in, 16)
            for c in range(NCH):
                sp.wait_ge(out_ok, START + c + 1)
                sp.dma_start(io["out"][c * P:(c + 1) * P, :], fo[c % 2][:, :]).then_inc(out_st[c % 2], 16)
            for n in range(2):
                sp.wait_ge(out_st[n], 16 * NCH // 2)

        @block.gpsimd
        def _(pool):
            for s in (kvc_st, qk_st, vg_st, co_st, gate_st, go_st, x1_st, a_st, xsum_ok, q_ok, out_ok):
                pool.sem_inc(s, START)

            def store(dst, src, n, stored):
                pool.dma_start(dst, src).then_inc(landed, 16)
                pool.wait_ge(landed, 16 * (n + 1) if isinstance(n, int) else n * 16 + 16)
                pool.sem_inc(stored, 1)

            pool.memset(ones[:, :], 1.0).then_inc(setup_ok, 1)
            pool.memset(eps[:, :], EPS).then_inc(setup_ok, 1)
            for k in range(1, KT):
                pool.wait_ge(xsq_ok, START + k + 1)
                pool.wait_ge(xsum_ok, START + k - 1)
                pool.tensor_tensor(x_sum[:, :], x_sum[:, :], x_sq[k % 2][:, :], ALU.add).then_inc(xsum_ok, 1)
            with pool.Fori(0, 3) as i:
                for e in range(2):
                    pool.wait_ge(ctx_ev, START + 2 * (e + 1) + i * 4)
                    store(kvc_d[i * 2 + e], ctx_out[e][:, :, :], i * 2 + (ST_KVC + e), kvc_st)
            with pool.Fori(0, 4) as i:
                for d in range(2):
                    pool.wait_ge(rot_add, START + 2 * (d + 1) + i * 4)
                    store(qk_d[i * 2 + d], rot_o[d][:, :, :], i * 2 + (ST_QK + d), qk_st)
            with pool.Fori(0, 8) as b:
                for c in range(NCH):
                    pool.wait_ge(vg_ev, START + c + 1 + b * 8)
                    store(vg_d[b, c], vg_out[c][:, :], b * 8 + (ST_VG + c), vg_st)
            with pool.Fori(0, 4) as i:
                for j in range(2):
                    pool.wait_ge(cv_s, START + j + 1 + i * 2)
                    store(co_d[i * 2 + j], co[j][:, :], i * 2 + (ST_CO + j), co_st)
            with pool.Fori(0, 8) as i:
                for j in range(2):
                    pool.wait_ge(gate_ev, START + j + 1 + i * 2)
                    store(gate_d[i * 2 + j], gate_o[j][:, :], i * 2 + (ST_GATE + j), gate_st)

            with pool.Fori(0, 2) as i:
                for p in range(2):
                    pool.wait_ge(ret_in[p], 80 + i * 80)
                    pool.wait_ge(hd_ok, START + p + 1 + i * 2)
                    pool.wait_ge(o_ok, START + NCH * p + i * 16)
                    for dst, col in ((q_f, H_XF), (q_b, H_XB)):
                        rows = hd[p][:, col:col + P].unsqueeze(1).broadcast_to([P, 2 * NCH, P])
                        pool.tensor_tensor(dst[:, :, :].rearrange("p k (c t) -> p (k c) t", t=P),
                                           q_t[p][:, :, :].rearrange("p k (c t) -> p (k c) t", t=P),
                                           rows, ALU.mult).then_inc(q_ok, 1)
                    for c in range(NCH):
                        pool.wait_ge(ogc_ok, START + NCH * p + c + 1 + i * 16)
                        store(go_d[bass.ds(i * 8 + 4 * p, 4), :, c * P:(c + 1) * P].rearrange("k p t -> p k t"),
                              og_t[c % 2][:, :, :], i * 16 + (ST_GO + NCH * p + c), go_st)
            for c in range(NCH):
                pool.wait_ge(y_x1, START + c + 1)
                store(x1_d[c], x1n[c % 2][:, :], ST_X1 + c, x1_st)
            with pool.Fori(0, FT // 2) as i:
                for j in range(2):
                    pool.wait_ge(up_a, START + j + 1 + i * 2)
                    store(a_d[i * 2 + j], ua[j][:, :], i * 2 + (ST_A + j), a_st)
            pool.wait_ge(x1_in, 16)
            for c in range(NCH):
                pool.wait_ge(dn_dve, START + 3 * (c + 1))
                pool.tensor_tensor(fo[c % 2][:, :], fo[c % 2][:, :], x1all[:, c, :], ALU.add).then_inc(out_ok, 1)

        @block.scalar
        def _(act):
            for s in (hi_done, xsq_ok, aff_ok, h_hi, ctx_ev, vg_ev, cv_x, cv_b, gate_ev, kcw_ok, kz_ok,
                      osq_ok, ort_ok, ogc_ok, m_hi, y_sq, y_act, y_hn, y_hi, up_b, up_s, dn_hi, dn_sq, dn_rt):
                act.sem_inc(s, START)

            def split_hi(base, i, per, dst):
                act.wait_ge(raw_in[base % 2], 16 * (base // 2 + 1) + i * (8 * per))
                act.activation(dst, raw[base % 2][:, :], ACT.Copy).then_inc(hi_done, 1)

            act.wait_ge(vec_in, 16)
            act.activation(silu_c[:, :, :].rearrange("p k v -> p v k"),
                           vec[:, V_C:V_C + 16].rearrange("p (v k) -> p v k", v=2), ACT.Silu).then_inc(silu_ok, 1)
            act.wait_ge(setup_ok, 2)
            act.wait_ge(ctx_ready, 16)
            act.activation(ctx_h[:, :, :], ctx_in[:, :, :], ACT.Square).then_inc(csq_ok, 1)
            act.wait_ge(sum_mm, 1)
            act.activation(inv_c[:, :], ps[:, 6, 0:CTX], ACT.Sqrt, bias=eps[:, :], scale=1.0 / D).then_inc(root_ok, 1)
            split_hi(R_CTX, 0, 0, w_hi[0][:, :])
            split_hi(R_CTX + 1, 0, 0, w_hi[1][:, :])
            act.wait_ge(row_sum, 1)
            act.activation(mod_row[:, 0:2, :], ps[0:2, 0:2, :], ACT.Copy).then_inc(row_act, 1)
            act.wait_ge(mod_ok, 2)
            act.wait_ge(z_ok, START + 1)
            for k in range(KT // 2):
                act.activation(ctx_h[:, k, :], ctx_in[:, k, :], ACT.Identity, scale=scale_x[:, k, 1:2],
                               bias=mod_a[:, k, 1:2]).then_inc(ca_ok, 1)
            act.wait_ge(ca_ok, KT // 2)
            act.activation(hc_hi[:, 0:4, :], ctx_h[:, 0:4, :], ACT.Copy).then_inc(hc_hi_ok, 1)
            act.wait_ge(cb_ok, 2)
            act.activation(hc_hi[:, 4:8, :], ctx_h[:, 4:8, :], ACT.Copy).then_inc(hc_hi_ok, 1)

            def context_unit(e, u, i):
                act.wait_ge(pe_done, START + 5 * e + u + i * 10)
                split_hi(R_CTX + 4 * e + u + 1, i, 8, w_hi[(u + 1) % 2][:, :])

            def context_out(e, i):
                act.wait_ge(kvc_st, START + e - 1 + i * 2)
                for c in range(NCX):
                    act.wait_ge(pe_done, START + 5 * e + 3 + c + 1 + i * 10)
                    act.activation(ctx_out[e % 2][:, c, :], ps[:, 2 * (e % 2) + c, :], ACT.Copy).then_inc(ctx_ev, 1)

            for e in range(2):
                for u in range(4):
                    if e > 0 or u > 0:
                        context_unit(e, u, 0)
                    for k in ((2 * u, 2 * u + 1) if e == 0 else ()):
                        act.wait_ge(x_ready[u], 16)
                        if k == 0:
                            dst = x_sum[:, :]
                        else:
                            dst = x_sq[k % 2][:, :]
                            act.wait_ge(xsum_ok, START + k - 2 if k > 2 else START)
                        act.activation(dst, x_in[:, k, :], ACT.Square).then_inc(xsq_ok, 1)
                context_out(e, 0)
            act.wait_ge(sum_mm, 2)
            act.activation(inv_x[:, :], pair(2), ACT.Sqrt, bias=eps[:, :], scale=1.0 / D).then_inc(root_ok, 1)
            with act.Fori(1, 3) as i:
                for e in range(2):
                    for u in range(4):
                        context_unit(e, u, i)
                        if u % 2 == 1:
                            n = 2 * e + u // 2 - 4
                            k = i * 4 + n
                            act.wait_ge(z_ok, START + n + 2 + i * 4)
                            act.wait_ge(h_lo, START + n - 1 + i * 4)
                            act.activation(aff[n % 2][:, :], x_in[:, bass.ds(k, 1), :].rearrange("p k t -> p (k t)"),
                                           ACT.Identity, scale=scale_x[:, bass.ds(k, 1), 0], bias=mod_a[:, bass.ds(k, 1), 0])\
                               .then_inc(aff_ok, 1)
                            act.wait_ge(aff_ok, START + n + 1 + i * 4)
                            act.activation(x0_hi[:, bass.ds(k, 1), :].rearrange("p k t -> p (k t)"), aff[n % 2][:, :],
                                           ACT.Copy).then_inc(h_hi, 1)
                    context_out(e, i)

            act.wait_ge(dve0, 2)
            act.activation(dec[:, DC_U, :], dec[:, DC_AZ, :], ACT.Exp, scale=-1.0).then_inc(act0, 1)
            act.wait_ge(dve0, 3)
            act.activation(dec[:, DC_LN, :], dec[:, DC_W, :], ACT.Ln).then_inc(act0, 1)
            act.wait_ge(dve0, 8)
            act.wait_ge(const_in, 16)
            for h in range(HEADS):
                fw, bw = dec[:, DC_LG, h:h + 1], dec[:, DC_LG, HEADS + h:HEADS + h + 1]
                for dst, src, scale in ((head_tab[:, h, H_D:H_D + P], const[:, C_DPOS:C_DPOS + P], fw),
                                        (dtmp[:, h, :], const[:, C_DNEG:C_DNEG + P], bw),
                                        (head_tab[:, h, H_XF:H_XF + P], const[:, C_RF:C_RF + P], fw),
                                        (head_tab[:, h, H_XB:H_XB + P], const[:, C_RB:C_RB + P], bw),
                                        (head_tab[:, h, H_F:H_F + 4], const[:, C_COLF:C_COLF + 4], fw),
                                        (head_tab[:, h, H_B:H_B + 4], const[:, C_COLB:C_COLB + 4], bw)):
                    act.activation(dst, src, ACT.Exp, scale=scale).then_inc(act0, 1)

            with act.Fori(0, 4) as i:
                for u in range(4):
                    act.wait_ge(pe_done, START + P_QK + u + i * 4)
                    split_hi(R_QK + u + 1, i, 4, w_hi[(u + 1) % 2][:, :])

            for base, func in ((0, ACT.Copy), (4, ACT.Silu)):
                with act.Fori(0, 4) as b:
                    for u in range(4):
                        act.wait_ge(pe_done, START + P_VG + 11 * base + u + b * 11)
                        split_hi(R_VG + 4 * base + u + 1, b, 4, w_hi[(u + 1) % 2][:, :])
                    for c in range(NCH):
                        act.wait_ge(vg_st, START + 8 * base + c - 7 + b * 8)
                        act.wait_ge(pe_done, START + P_VG + 11 * base + 4 + c + b * 11)
                        act.activation(vg_out[c][:, :], ps[:, c, :], func).then_inc(vg_ev, 1)

            with act.Fori(0, 4) as i:
                for j in range(2):
                    for m in range(3):
                        u = 3 * j + m
                        act.wait_ge(pe_done, START + P_CONV + u + i * 6)
                        split_hi(R_CONV + u + 1, i, 6, w_hi[(u + 1) % 2][:, :])
                        if m == 0:
                            act.wait_ge(cv_p, START + j - 1 + i * 2)
                            act.wait_ge(pe_done, START + P_CONV + u + 1 + i * 6)
                            act.activation(cx[j][:, :], pair(CONV_PAIR[u]), ACT.Copy).then_inc(cv_x, 1)
                        if m == 1:
                            act.wait_ge(cv_p, START + j + 1 + i * 2)
                            act.wait_ge(cv_s, START + j - 1 + i * 2)
                            act.activation(cy[j][:, :], cprod[j][:, :], ACT.Identity,
                                           scale=vec[:, bass.ds(i * 2 + (V_CW + 8 + j), 1)],
                                           bias=vec[:, bass.ds(i * 2 + (V_CB + j), 1)]).then_inc(cv_b, 1)

            def gates(i, last):
                for u in range(2):
                    act.wait_ge(pe_done, START + P_GATE + u + i * 2)
                    if not (last and u == 1):
                        split_hi(R_GATE + u + 1, i, 2, w_hi[(u + 1) % 2][:, :])
                    act.wait_ge(gate_st, START + u - 1 + i * 2)
                    act.wait_ge(pe_done, START + P_GATE + u + 1 + i * 2)
                    act.activation(gate_o[u][:, :], pair(2 + u), ACT.Sigmoid).then_inc(gate_ev, 1)

            with act.Fori(0, 7) as i:
                gates(i, False)
            gates(7, True)

            with act.Fori(0, 2) as i:
                for p in range(2):
                    act.wait_ge(ret_in[p], 80 + i * 80)
                    act.wait_ge(hd_ok, START + p + 1 + i * 2)
                    act.wait_ge(u_ok, START + N_U * (p - 1) + 4 + i * 2 * N_U)
                    for dst, col in ((kcw_b, H_B), (kcw_f, H_F)):
                        for m in range(NCX):
                            act.activation(dst[:, m, :], kc_n[p][:, m, :], ACT.Copy,
                                           scale=hd[p][:, col + 1 + m:col + 2 + m]).then_inc(kcw_ok, 1)
                    for m in range(NCH):
                        c = NCH - 1 - m
                        act.wait_ge(kt_ok, START + NCH * p + m + 1 + i * 16)
                        act.wait_ge(u_ok, START + N_U * p + 2 * m + 2 + i * 2 * N_U)
                        if c > 0:
                            act.activation(kz_b[:, m % 2, :], ps[:, m % 2, 0:DK], ACT.Copy,
                                           scale=hd[p][:, H_B:H_B + 1]).then_inc(kz_ok, 1)
                        if c < NCH - 1:
                            act.activation(kz_f[:, c, :], ps[:, m % 2, 0:DK], ACT.Copy,
                                           scale=hd[p][:, H_F:H_F + 1]).then_inc(kz_ok, 1)
                    def gated_out(c):
                        act.wait_ge(go_st, START + NCH * p + c - 1 + i * 16)
                        act.wait_ge(ogt_ok, START + NCH * p + c + 1 + i * 16)
                        act.activation(og_t[c % 2][:, :, :].rearrange("p k t -> p (k t)"), ps[:, 6, :],
                                       ACT.Copy).then_inc(ogc_ok, 1)

                    for c in range(NCH):
                        n = NCH * p + c
                        act.wait_ge(o_ok, START + n + 1 + i * 16)
                        act.wait_ge(osq_ok, START + n + i * 16)
                        act.activation(sq_j[:, :], ps[:, 2 + c % 2, :], ACT.Square,
                                       accum_out=onum[:, c % 2, 0:1]).then_inc(osq_ok, 1)
                        act.wait_ge(osq_ok, START + n + 1 + i * 16)
                        act.wait_ge(oinv_ok, START + n - 1 + i * 16)
                        act.activation(onum[:, c % 2, 1:2], onum[:, c % 2, 0:1], ACT.Sqrt,
                                       bias=eps[:, :], scale=1.0 / DV).then_inc(ort_ok, 1)
                        if c > 0:
                            gated_out(c - 1)
                    gated_out(NCH - 1)

            with act.Fori(0, 4) as i:
                for j in range(2):
                    split_hi(R_CO + j, i, 2, x1_hi[:, bass.ds(i * 2 + j, 1), :].rearrange("p k t -> p (k t)"))
            split_hi(R_A, 0, 0, w_hi[0][:, :])
            for base, count, dst in ((R_A, P_A, x0_hi), (R_B, P_B, x1_hi)):
                with act.Fori(0, 4) as i:
                    for j in range(2):
                        act.wait_ge(pe_done, START + count + j + i * 2)
                        split_hi(base + 2 * j + 1, i, 4, dst[:, bass.ds(i * 2 + j, 1), :].rearrange("p k t -> p (k t)"))
                        split_hi(base + 2 * j + 2, i, 4, w_hi[(j + 1) % 2][:, :])

            def last_stage(i, last):
                for j in range(2):
                    act.wait_ge(pe_done, START + P_C + j + i * 2)
                    if not (last and j == 1):
                        split_hi(R_C + j + 1, i, 2, w_hi[(j + 1) % 2][:, :])
                    act.wait_ge(mg_add, START + 16 + 2 * (j + 1) + i * 4)
                    act.activation(x0_hi[:, bass.ds(i * 2 + j, 1), :], merged[:, bass.ds(i * 2 + j, 1), :],
                                   ACT.Copy).then_inc(m_hi, 1)

            with act.Fori(0, 3) as i:
                last_stage(i, False)
            last_stage(3, True)
            act.wait_ge(pe_done, START + P_UP)
            with act.Fori(0, 4) as i:
                for j in range(2):
                    split_hi(R_WO + j, i, 2, x1_hi[:, bass.ds(i * 2 + j, 1), :].rearrange("p k t -> p (k t)"))
            split_hi(R_UP, 0, 0, w_hi[0][:, :])
            split_hi(R_UP + 1, 0, 0, w_hi[1][:, :])

            act.wait_ge(row_mm, 1)
            act.activation(gain_row[:, :], pair(2), ACT.Copy).then_inc(row_ok, 1)
            for c in range(NCH + 1):
                if c < NCH:
                    act.wait_ge(y_done, START + c + 1)
                    act.wait_ge(y_sq, START + 2 * c)
                    act.activation(junk2[:, :], pair(c % 2), ACT.Square, accum_out=st1[:, c, 0:1]).then_inc(y_sq, 1)
                    act.wait_ge(y_sq, START + 2 * c + 1)
                    act.activation(st1[:, c, 1:2], st1[:, c, 0:1], ACT.Sqrt, bias=eps[:, :], scale=1.0 / D).then_inc(y_act, 1)
                    act.wait_ge(y_x1, START + c + 1)
                    act.wait_ge(y_sq, START + 2 * c + 1)
                    act.activation(junk2[:, :], x1n[c % 2][:, :], ACT.Square, accum_out=st2[:, c, 0:1]).then_inc(y_sq, 1)
                    act.wait_ge(y_sq, START + 2 * c + 2)
                    act.activation(st2[:, c, 1:2], st2[:, c, 0:1], ACT.Sqrt, bias=eps[:, :], scale=1.0 / D).then_inc(y_act, 1)
                if c > 0:
                    act.wait_ge(y_dve, START + Y_COUNT["shift", c - 1])
                    act.activation(x0_hi[:, :, (c - 1) * P:c * P], haff[:, :].rearrange("p (k t) -> p k t", t=P),
                                   ACT.Copy).then_inc(y_hi, 1)
                if c < NCH:
                    act.wait_ge(y_dve, START + Y_COUNT["inv2", c])
                    act.activation(hn[c % 2][:, :], x1n[c % 2][:, :], ACT.Copy, scale=st2[:, c, 2:3]).then_inc(y_hn, 1)

            act.wait_ge(row_mm, 2)
            act.wait_ge(y_dve, START + Y_COUNT["z", NCH - 1])
            act.activation(gain_row[:, :], pair(2), ACT.Copy).then_inc(row_ok, 1)

            def up(i, first, last):
                for j in range(2):
                    for m in range(2):
                        u = 2 * j + m
                        act.wait_ge(pe_done, START + P_UP + u + i * 4)
                        if not (last and u == 3 or first and u == 0):
                            split_hi(R_UP + u + 1, i, 4, w_hi[(u + 1) % 2][:, :])
                        act.wait_ge(up_a, START + j - 1 + i * 2)
                        act.wait_ge(pe_done, START + P_UP + u + 1 + i * 4)
                        tile = FT * m + j
                        act.activation(uy[j][m][:, :], pair(u), ACT.Identity,
                                       scale=vec[:, bass.ds(i * 6 + (V_FW + 3 * tile + 1), 1)],
                                       bias=vec[:, bass.ds(i * 2 + (V_FB + tile), 1)]).then_inc(up_b, 1)
                    act.wait_ge(up_c, START + 4 * j + 2 + i * 8)
                    act.activation(uy[j][0][:, :], uy[j][0][:, :], ACT.Silu).then_inc(up_s, 1)


            def down_hi(n, i, u):
                act.wait_ge(dn_in[u], 32 * (n // 2 + 1) + i * 32)
                act.activation(a_hi[u][:, :], a_raw[u][:, :], ACT.Copy).then_inc(dn_hi, 1)
                act.activation(d_hi[u][:, :], d_raw[u][:, :], ACT.Copy).then_inc(dn_hi, 1)

            def down(half, i, last):
                for u in range(2):
                    act.wait_ge(dn_pe, START + N_DOWN * half + u + i * 2)
                    if not (last and half == 1 and u == 1):
                        down_hi(FT * half + u + 1, i, (u + 1) % 2)

            up(0, True, False)
            with act.Fori(1, FT // 2 - 1) as i:
                up(i, False, False)
            down_hi(0, 0, 0)
            up(FT // 2 - 1, False, True)

            for half in range(2):
                with act.Fori(0, FT // 2 - 1) as i:
                    down(half, i, False)
                down(half, FT // 2 - 1, True)
                for c in range(NCH):
                    act.wait_ge(dn_pe, START + N_DOWN * half + FT + c)
                    act.wait_ge(dn_sq, START + NCH * half + c)
                    act.activation(junk3[:, :], ps[:, c, :], ACT.Square, accum_out=fsum[:, c, half:half + 1]).then_inc(dn_sq, 1)
                    if half == 1:
                        act.wait_ge(dn_add, START + c + 1)
                        act.activation(fsum[:, c, 3:4], fsum[:, c, 2:3], ACT.Sqrt, bias=eps[:, :], scale=1.0 / D).then_inc(dn_rt, 1)

        @block.vector
        def _(dve):
            for s in (lo_done, z_ok, h_lo, rot_mul, rot_add, cv_p, cv_y, cv_s, hd_ok, st_ok, ms_ok, oinv_ok, og_ok, adb_mul,
                      mg_mul, mg_add, m_lo, y_dve, y_x1, y_lo, up_c, up_a, dn_lo, dn_ev, dn_add, dn_dve):
                dve.sem_inc(s, START)

            def split_lo(base, i, per, dst, hi):
                dve.wait_ge(hi_done, START + base + 1 + i * per)
                dve.tensor_tensor(dst, raw[base % 2][:, :], hi.bitcast(F32), ALU.subtract).then_inc(lo_done, 1)

            def ring_lo(base, i, per):
                split_lo(base, i, per, w_lo[base % 2][:, :], w_hi[base % 2][:, :])

            def flat(t, i, j):
                return t[:, bass.ds(i * 2 + j, 1), :].rearrange("p k t -> p (k t)")

            def by_tile(v):
                return v.unsqueeze(2).broadcast_to([P, KT, P])

            dve.wait_ge(csq_ok, 1)
            for n, k in enumerate((4, 2, 1)):
                if n > 0:
                    dve.wait_ge(csum_ok, n)
                dve.tensor_tensor(ctx_h[:, 0:k, :], ctx_h[:, 0:k, :], ctx_h[:, k:2 * k, :], ALU.add).then_inc(csum_ok, 1)
            dve.wait_ge(root_ok, 1)
            dve.reciprocal(inv_c[:, :], inv_c[:, :]).then_inc(inv_ok, 1)
            dve.wait_ge(inv_ok, 1)
            dve.tensor_tensor(ctx_in[:, :, :], ctx_in[:, :, :], inv_c[:, :].unsqueeze(1).broadcast_to([P, KT, CTX]),
                              ALU.mult).then_inc(z_ok, 1)
            ring_lo(R_CTX, 0, 0)
            ring_lo(R_CTX + 1, 0, 0)
            dve.wait_ge(row_sum, 1)
            dve.tensor_copy(mod_row[:, 2:4, :], ps[0:2, 2:4, :]).then_inc(row_dve, 1)
            dve.wait_ge(ada_done, 1)
            dve.tensor_tensor(mod_a[:, :, :], ps[:, 7, 0:32].rearrange("p (t v) -> p t v", v=2),
                              vec[:, V_BADA:V_BADA + 16].unsqueeze(2).broadcast_to([P, 16, 2]), ALU.add).then_inc(mod_ok, 1)
            dve.wait_ge(mod_ok, 1)
            dve.scalar_tensor_tensor(scale_x[:, :, :], mod_a[:, KT:16, :], 1.0,
                                     vec[:, V_GMIX:V_GMIX + KT].unsqueeze(2).broadcast_to([P, KT, 2]),
                                     ALU.add, ALU.mult).then_inc(mod_ok, 1)
            dve.wait_ge(mod_ok, 2)
            dve.wait_ge(z_ok, START + 1)
            dve.wait_ge(sum_mm, 1)
            dve.tensor_tensor(ctx_h[:, 4:8, :], ctx_in[:, 4:8, :], scale_x[:, 4:8, 1:2].broadcast_to([P, 4, CTX]),
                              ALU.mult).then_inc(cb_ok, 1)
            dve.wait_ge(cb_ok, 1)
            dve.tensor_tensor(ctx_h[:, 4:8, :], ctx_h[:, 4:8, :], mod_a[:, 4:8, 1:2].broadcast_to([P, 4, CTX]),
                              ALU.add).then_inc(cb_ok, 1)
            for n in range(2):
                dve.wait_ge(hc_hi_ok, n + 1)
                if n == 1:
                    dve.wait_ge(cb_ok, 2)
                half = slice(4 * n, 4 * n + 4)
                dve.tensor_tensor(hc_lo[:, half, :], ctx_h[:, half, :], hc_hi[:, half, :].bitcast(F32),
                                  ALU.subtract).then_inc(hc_lo_ok, 1)

            for r in range(1, 8):
                ring_lo(R_CTX + r + 1, 0, 8)
            dve.wait_ge(root_ok, 2)
            dve.reciprocal(inv_x[:, :], inv_x[:, :]).then_inc(inv_ok, 1)
            dve.wait_ge(inv_ok, 2)
            with dve.Fori(1, 3) as i:
                for r in range(8):
                    ring_lo(R_CTX + r + 1, i, 8)
                    n = r // 2 - 4
                    k = i * 4 + n
                    if r % 2 == 0:
                        x_tile = x_in[:, bass.ds(k, 1), :].rearrange("p k t -> p (k t)")
                        dve.tensor_tensor(x_tile, x_tile, inv_x[:, :], ALU.mult).then_inc(z_ok, 1)
                    else:
                        dve.wait_ge(h_hi, START + n + 1 + i * 4)
                        dve.tensor_tensor(x0_lo[:, bass.ds(k, 1), :].rearrange("p k t -> p (k t)"), aff[n % 2][:, :],
                                          x0_hi[:, bass.ds(k, 1), :].rearrange("p k t -> p (k t)").bitcast(F32),
                                          ALU.subtract).then_inc(h_lo, 1)

            z = vec[:, V_DEC:V_DEC + 8]
            dve.tensor_scalar(dec[:, DC_T, :], z, -1.0, None, ALU.mult).then_inc(dve0, 1)
            dve.wait_ge(dve0, 1)
            dve.tensor_tensor(dec[:, DC_AZ, :], z, dec[:, DC_T, :], ALU.max).then_inc(dve0, 1)
            dve.wait_ge(act0, 1)
            dve.tensor_scalar(dec[:, DC_W, :], dec[:, DC_U, :], 1.0, None, ALU.add).then_inc(dve0, 1)
            dve.wait_ge(dve0, 3)
            dve.scalar_tensor_tensor(dec[:, DC_CORR, :], dec[:, DC_W, :], 1.0, dec[:, DC_U, :],
                                     ALU.subtract, ALU.subtract).then_inc(dve0, 1)
            dve.reciprocal(dec[:, DC_RW, :], dec[:, DC_W, :]).then_inc(dve0, 1)
            dve.wait_ge(dve0, 5)
            dve.tensor_tensor(dec[:, DC_CORR, :], dec[:, DC_CORR, :], dec[:, DC_RW, :], ALU.mult).then_inc(dve0, 1)
            dve.wait_ge(dve0, 6)
            dve.wait_ge(act0, 2)
            dve.tensor_tensor(dec[:, DC_LN, :], dec[:, DC_LN, :], dec[:, DC_CORR, :], ALU.subtract).then_inc(dve0, 1)
            dve.wait_ge(dve0, 7)
            dve.scalar_tensor_tensor(dec[:, DC_LG, :], z, 0.0, dec[:, DC_LN, :], ALU.min, ALU.subtract).then_inc(dve0, 1)
            dve.wait_ge(act0, 2 + 6 * HEADS)
            mask = head_tab[:, :, H_D:H_D + P]
            dve.tensor_tensor(mask, mask, const[:, C_GE:C_GE + P].unsqueeze(1).broadcast_to([P, HEADS, P]),
                              ALU.mult).then_inc(dve0, 1)
            dve.tensor_tensor(dtmp[:, :, :], dtmp[:, :, :], const[:, C_LT:C_LT + P].unsqueeze(1).broadcast_to([P, HEADS, P]),
                              ALU.mult).then_inc(dve0, 1)
            for col in (H_F, H_B):
                dve.tensor_scalar(head_tab[:, :, col:col + 3], head_tab[:, :, col:col + 3], K_SCALE, None,
                                  ALU.mult).then_inc(dve0, 1)
            dve.wait_ge(dve0, 12)
            dve.tensor_tensor(mask, mask, dtmp[:, :, :], ALU.add).then_inc(dve0, 1)

            dve.wait_ge(trig_in, 32)
            with dve.Fori(0, 4) as i:
                for d in range(2):
                    for m in range(2):
                        u = 2 * d + m
                        ring_lo(R_QK + u + 1, i, 4)
                        dve.wait_ge(pe_done, START + P_QK + u + 1 + i * 4)
                        dve.tensor_tensor(rot_a[d][:, m, :], pair(u), cos[:, :], ALU.mult).then_inc(rot_mul, 1)
                        dve.tensor_tensor(rot_b[d][:, 1 - m, :], pair(u), sin[:, :], ALU.mult).then_inc(rot_mul, 1)
                    dve.wait_ge(rot_mul, START + 4 * (d + 1) + i * 8)
                    dve.wait_ge(qk_st, START + d - 1 + i * 2)
                    dve.tensor_tensor(rot_o[d][:, 0, :], rot_a[d][:, 0, :], rot_b[d][:, 0, :], ALU.subtract).then_inc(rot_add, 1)
                    dve.tensor_tensor(rot_o[d][:, 1, :], rot_a[d][:, 1, :], rot_b[d][:, 1, :], ALU.add).then_inc(rot_add, 1)

            with dve.Fori(0, 8) as b:
                for u in range(4):
                    ring_lo(R_VG + u + 1, b, 4)

            with dve.Fori(0, 4) as i:
                for j in range(2):
                    rows_p = cprod[j][:, :].rearrange("p (r t) -> p r t", t=GRID)
                    rows_y = cy[j][:, :].rearrange("p (r t) -> p r t", t=GRID)
                    for m in range(3):
                        u = 3 * j + m
                        ring_lo(R_CONV + u + 1, i, 6)
                        if m == 1:
                            dve.wait_ge(pe_done, START + P_CONV + u + 1 + i * 6)
                            dve.wait_ge(cv_x, START + j + 1 + i * 2)
                            dve.tensor_tensor(cprod[j][:, :], pair(CONV_PAIR[u]), cx[j][:, :], ALU.mult).then_inc(cv_p, 1)
                            dve.wait_ge(cv_b, START + j + 1 + i * 2)
                            dve.scalar_tensor_tensor(rows_y[:, :, 1:GRID], rows_p[:, :, 0:GRID - 1],
                                                     vec[:, bass.ds(i * 2 + (V_CW + j), 1)], rows_y[:, :, 1:GRID],
                                                     ALU.mult, ALU.add).then_inc(cv_y, 1)
                            dve.wait_ge(cv_y, START + 2 * j + 1 + i * 4)
                            dve.scalar_tensor_tensor(rows_y[:, :, 0:GRID - 1], rows_p[:, :, 1:GRID],
                                                     vec[:, bass.ds(i * 2 + (V_CW + 2 * KT + j), 1)], rows_y[:, :, 0:GRID - 1],
                                                     ALU.mult, ALU.add).then_inc(cv_y, 1)
                        if m == 2:
                            dve.wait_ge(cv_y, START + 2 * j + 2 + i * 4)
                            dve.wait_ge(co_st, START + j - 1 + i * 2)
                            dve.wait_ge(pe_done, START + P_CONV + u + 1 + i * 6)
                            dve.tensor_tensor(co[j][:, :], cy[j][:, :], pair(CONV_PAIR[u]), ALU.mult).then_inc(cv_s, 1)

            with dve.Fori(0, 7) as i:
                for u in range(2):
                    ring_lo(R_GATE + u + 1, i, 2)
            ring_lo(R_GATE + 15, 0, 0)

            with dve.Fori(0, 2) as i:
                for p in range(2):
                    dve.wait_ge(q_ok, START + 2 * (p - 1) + i * 4)
                    dve.wait_ge(kz_ok, START + N_KZ * (p - 1) + i * 2 * N_KZ)
                    dve.wait_ge(ret_in[p], 80 + i * 80)
                    dve.tensor_copy(hd[p][:, :], head_tab[:, bass.ds(i * 2 + p, 1), :].rearrange("p h n -> p (h n)"))\
                       .then_inc(hd_ok, 1)
                    u0 = N_U * p

                    def state(n, dst, old, decay):
                        dve.wait_ge(u_ok, START + u0 + n + 1 + i * 2 * N_U)
                        if old is None:
                            dve.tensor_copy(dst, ps[:, 4 + n % 2, :]).then_inc(st_ok, 1)
                        else:
                            dve.wait_ge(st_ok, START + u0 + n - 1 + i * 2 * N_U)
                            dve.scalar_tensor_tensor(dst, old, decay, ps[:, 4 + n % 2, :], ALU.mult, ALU.add).then_inc(st_ok, 1)

                    dve.wait_ge(o_ok, START + NCH * p + i * 16)
                    for t in range(2):
                        state(t, s_bw[:, NCH - 1, t, :], None, None)
                    for t in range(2):
                        state(2 + t, s_fw[:, 0, t, :], None, None)
                    dve.wait_ge(hd_ok, START + p + 1 + i * 2)
                    for m in range(NCH - 1):
                        c = NCH - 1 - m
                        for t in range(2):
                            state(4 + 2 * m + t, s_bw[:, c - 1, t, :], s_bw[:, c, t, :], hd[p][:, H_B + 3:H_B + 4])

                    def mask_scores(c):
                        n = NCH * p + c
                        dve.wait_ge(o_ok, START + n - 1 + i * 16)
                        dve.wait_ge(sc_ok, START + n + 1 + i * 16)
                        dve.tensor_tensor(s_sc[:, c % 2, :], ps[:, c % 2, 0:P], hd[p][:, H_D:H_D + P], ALU.mult).then_inc(ms_ok, 1)

                    def forward(c, t):
                        if t == 0:
                            dve.wait_ge(o_ok, START + NCH * p + c + i * 16)
                        state(18 + 2 * c + t, s_fw[:, (c + 1) % 2, t, :], s_fw[:, c % 2, t, :], hd[p][:, H_F + 3:H_F + 4])

                    mask_scores(0)
                    for c in range(NCH):
                        n = NCH * p + c
                        if c + 1 < NCH:
                            mask_scores(c + 1)
                            forward(c, 0)
                        dve.wait_ge(ort_ok, START + n + 1 + i * 16)
                        dve.reciprocal(onum[:, c % 2, 2:3], onum[:, c % 2, 1:2]).then_inc(oinv_ok, 1)
                        if c + 1 < NCH:
                            forward(c, 1)
                        dve.wait_ge(adb_in[c % 2], 16 * (NCH // 2 * p + c // 2 + 1) + i * 128)
                        dve.wait_ge(adb_mul, START + n + i * 16)
                        if c == 0:
                            dve.wait_ge(adb_done, START + p + i * 2)
                            dve.tensor_scalar(ada_acc[:, :], ada_ret[0][:, :], silu_c[:, 0, 0:1], None, ALU.mult).then_inc(adb_mul, 1)
                        else:
                            dve.scalar_tensor_tensor(ada_acc[:, :], ada_ret[c % 2][:, :], silu_c[:, c, 0:1], ada_acc[:, :],
                                                     ALU.mult, ALU.add).then_inc(adb_mul, 1)
                        dve.wait_ge(oinv_ok, START + n + 1 + i * 16)
                        dve.wait_ge(g_ld[c % 2], 16 * (NCH // 2 * p + c // 2 + 1) + i * 128)
                        dve.wait_ge(ogt_ok, START + n - 1 + i * 16)
                        dve.scalar_tensor_tensor(og[c % 2][:, :], ps[:, 2 + c % 2, :], onum[:, c % 2, 2:3], g_in[c % 2][:, :],
                                                 ALU.mult, ALU.mult).then_inc(og_ok, 1)
            dve.wait_ge(adb_done, START + HEADS)
            dve.tensor_tensor(mod_b[:, :], ps[:, 7, 0:32], vec[:, V_BADA + 16:V_BADA + 48], ALU.add).then_inc(mod_ok, 1)
            dve.wait_ge(mod_ok, 3)
            dve.scalar_tensor_tensor(scale_h[:, :], mod_b[:, 16:24], 1.0, vec[:, V_GFFN:V_GFFN + KT], ALU.add, ALU.mult).then_inc(mod_ok, 1)
            dve.tensor_tensor(gain_y[:, :], mod_b[:, 0:8], vec[:, V_GPOST:V_GPOST + KT], ALU.mult).then_inc(mod_ok, 1)
            dve.tensor_tensor(gain_f[:, :], mod_b[:, 24:32], vec[:, V_GFPOST:V_GFPOST + KT], ALU.mult).then_inc(mod_ok, 1)

            with dve.Fori(0, 4) as i:
                for j in range(2):
                    split_lo(R_CO + j, i, 2, flat(x1_lo, i, j), flat(x1_hi, i, j))
            ring_lo(R_A, 0, 0)

            def merge(stage, count, i, j):
                dve.wait_ge(gt_in[j], 16 * (4 * stage + 1) + i * 16)
                dve.wait_ge(pe_done, START + count + j + 1 + i * 2)
                for n in range(2):
                    cols = slice(n * HALF, (n + 1) * HALF)
                    out = merged[:, bass.ds(i * 2 + j, 1), cols].rearrange("p k t -> p (k t)")
                    made = START + 16 * stage + 2 * j + n + 1
                    if stage == 0:
                        dve.tensor_tensor(out, ps[:, 2 * j + n, :], gate_in[j][:, cols], ALU.mult).then_inc(mg_mul, 1)
                    else:
                        dve.wait_ge(mg_add, made - 17 + i * 4)
                        dve.tensor_tensor(mtmp[:, :], ps[:, 2 * j + n, :], gate_in[j][:, cols], ALU.mult).then_inc(mg_mul, 1)
                        dve.wait_ge(mg_mul, made + i * 4)
                        dve.tensor_tensor(out, out, mtmp[:, :], ALU.add).then_inc(mg_add, 1)

            for stage, (base, count, hi, lo) in enumerate(((R_A, P_A, x0_hi, x0_lo), (R_B, P_B, x1_hi, x1_lo))):
                with dve.Fori(0, 4) as i:
                    for j in range(2):
                        split_lo(base + 2 * j + 1, i, 4, flat(lo, i, j), flat(hi, i, j))
                        split_lo(base + 2 * j + 2, i, 4, w_lo[(j + 1) % 2][:, :], w_hi[(j + 1) % 2][:, :])
                        merge(stage, count, i, j)

            def last_stage(i, last):
                for j in range(2):
                    if not (last and j == 1):
                        ring_lo(R_C + j + 1, i, 2)
                    merge(2, P_C, i, j)
                    dve.wait_ge(m_hi, START + j + 1 + i * 2)
                    dve.tensor_tensor(flat(x0_lo, i, j), flat(merged, i, j), flat(x0_hi, i, j).bitcast(F32),
                                      ALU.subtract).then_inc(m_lo, 1)

            with dve.Fori(0, 3) as i:
                last_stage(i, False)
            last_stage(3, True)
            with dve.Fori(0, 3) as i:
                for j in range(2):
                    split_lo(R_WO + j, i, 2, flat(x1_lo, i, j), flat(x1_hi, i, j))
            dve.wait_ge(mod_ok, 6)
            dve.wait_ge(m_lo, START + KT)
            dve.tensor_tensor(diag[:, :, :], ident[:, :].unsqueeze(1).broadcast_to([P, KT, P]), by_tile(gain_y[:, :]),
                              ALU.mult).then_inc(dg_ok, 1)
            for k in (6, 7):
                split_lo(R_WO + k, 0, 0, x1_lo[:, k, :], x1_hi[:, k, :])
            ring_lo(R_UP, 0, 0)
            ring_lo(R_UP + 1, 0, 0)

            dve.wait_ge(row_ok, 1)
            dve.tensor_tensor(diag[:, :, :], ident[:, :].unsqueeze(1).broadcast_to([P, KT, P]), by_tile(gain_f[:, :]),
                              ALU.mult).then_inc(dg_ok, 1)
            tile = haff[:, :].rearrange("p (k t) -> p k t", t=P)
            for c in range(NCH + 1):
                if c < NCH:
                    dve.wait_ge(y_act, START + 2 * c + 1)
                    dve.reciprocal(st1[:, c, 2:3], st1[:, c, 1:2]).then_inc(y_dve, 1)
                    dve.wait_ge(y_dve, START + Y_COUNT["inv1", c])
                    dve.wait_ge(y_hn, START + c - 1)
                    dve.wait_ge(y_t, START + c - 1)
                    dve.scalar_tensor_tensor(hn[c % 2][:, :], pair(c % 2), st1[:, c, 2:3], gain_row[:, :],
                                             ALU.mult, ALU.mult).then_inc(y_dve, 1)
                    dve.wait_ge(y_dve, START + Y_COUNT["z", c])
                    dve.wait_ge(xr_in[c % 2], 16 * (c // 2 + 1))
                    dve.wait_ge(x1_st, START + c - 1)
                    dve.tensor_tensor(x1n[c % 2][:, :], hn[c % 2][:, :], xr[c % 2][:, :], ALU.add).then_inc(y_x1, 1)
                if c > 0:
                    dve.wait_ge(y_t, START + c)
                    dve.wait_ge(y_lo, START + c - 1)
                    dve.tensor_tensor(tile, pair(2 + (c - 1) % 2).rearrange("p (k t) -> p k t", t=P), by_tile(scale_h[:, :]),
                                      ALU.mult).then_inc(y_dve, 1)
                    dve.wait_ge(y_dve, START + Y_COUNT["scale", c - 1])
                    dve.tensor_tensor(tile, tile, by_tile(mod_b[:, 8:16]), ALU.add).then_inc(y_dve, 1)
                if c < NCH:
                    dve.wait_ge(y_act, START + 2 * c + 2)
                    dve.reciprocal(st2[:, c, 2:3], st2[:, c, 1:2]).then_inc(y_dve, 1)
                if c > 0:
                    dve.wait_ge(y_hi, START + c)
                    cols = slice((c - 1) * P, c * P)
                    dve.tensor_tensor(x0_lo[:, :, cols], tile, x0_hi[:, :, cols].bitcast(F32), ALU.subtract).then_inc(y_lo, 1)

            def up(i, first, last):
                for j in range(2):
                    for m in range(2):
                        u = 2 * j + m
                        tile = FT * m + j
                        if not (last and u == 3 or first and u == 0):
                            ring_lo(R_UP + u + 1, i, 4)
                        dve.wait_ge(up_b, START + u + 1 + i * 4)
                        y = uy[j][m]
                        dve.scalar_tensor_tensor(y[:, GRID:T], pair(u)[:, 0:T - GRID],
                                                 vec[:, bass.ds(i * 6 + (V_FW + 3 * tile), 1)], y[:, GRID:T],
                                                 ALU.mult, ALU.add).then_inc(up_c, 1)
                        dve.wait_ge(up_c, START + 2 * u + 1 + i * 8)
                        dve.scalar_tensor_tensor(y[:, 0:T - GRID], pair(u)[:, GRID:T],
                                                 vec[:, bass.ds(i * 6 + (V_FW + 3 * tile + 2), 1)], y[:, 0:T - GRID],
                                                 ALU.mult, ALU.add).then_inc(up_c, 1)
                    dve.wait_ge(up_s, START + j + 1 + i * 2)
                    dve.wait_ge(up_c, START + 4 * (j + 1) + i * 8)
                    dve.wait_ge(a_st, START + j - 1 + i * 2)
                    dve.tensor_tensor(ua[j][:, :], uy[j][0][:, :], uy[j][1][:, :], ALU.mult).then_inc(up_a, 1)

            def down_lo(n, i, u):
                dve.wait_ge(dn_hi, START + 2 * (n + 1) + i * 4)
                dve.tensor_tensor(a_lo[u][:, :], a_raw[u][:, :], a_hi[u][:, :].bitcast(F32), ALU.subtract).then_inc(dn_lo, 1)
                dve.tensor_tensor(d_lo[u][:, :], d_raw[u][:, :], d_hi[u][:, :].bitcast(F32), ALU.subtract).then_inc(dn_lo, 1)

            def down(half, i, last):
                for u in range(2):
                    if not (last and half == 1 and u == 1):
                        down_lo(FT * half + u + 1, i, (u + 1) % 2)

            up(0, True, False)
            with dve.Fori(1, FT // 2 - 1) as i:
                up(i, False, False)
            down_lo(0, 0, 0)
            up(FT // 2 - 1, False, True)

            for half in range(2):
                with dve.Fori(0, FT // 2 - 1) as i:
                    down(half, i, False)
                down(half, FT // 2 - 1, True)
                if half == 0:
                    for c in range(NCH):
                        dve.wait_ge(dn_sq, START + c + 1)
                        dve.tensor_copy(f0[:, c, :], ps[:, c, :]).then_inc(dn_ev, 1)
            dve.wait_ge(row_ok, 2)
            dve.wait_ge(dn_ev, START + NCH)
            for c in range(NCH):
                dve.wait_ge(dn_sq, START + NCH + c + 1)
                dve.tensor_tensor(fsum[:, c, 2:3], fsum[:, c, 0:1], fsum[:, c, 1:2], ALU.add).then_inc(dn_add, 1)
                dve.wait_ge(dn_rt, START + c + 1)
                dve.reciprocal(fsum[:, c, 4:5], fsum[:, c, 3:4]).then_inc(dn_dve, 1)
                dve.wait_ge(dn_dve, START + 3 * c + 1)
                if c > 1:
                    dve.wait_ge(out_st[c % 2], 16 * (c // 2))
                for n, part in ((0, f0[:, c, :]), (1, ps[:, c, :])):
                    cols = slice(n * HALF, (n + 1) * HALF)
                    dve.scalar_tensor_tensor(fo[c % 2][:, cols], part, fsum[:, c, 4:5], gain_row[:, cols],
                                             ALU.mult, ALU.mult).then_inc(dn_dve, 1)

        @block.tensor
        def _(pe):
            for s in (pe_done, kt_ok, u_ok, sc_ok, o_ok, ogt_ok, adb_done, y_done, y_t, dn_pe):
                pe.sem_inc(s, START)

            def product(out, a, b, first, last):
                (ah, al), (bh, bl) = a, b
                pe.matmul(out, ah, bh, start=first, stop=False)
                pe.matmul(out, ah, bl, start=False, stop=False)
                return pe.matmul(out, al, bh, start=False, stop=last)

            def by_width(slot, x, out):
                for n in range(2):
                    done = by_width_half(slot, x, out, n)
                return done

            def by_width_half(slot, x, out, n):
                for k in range(KT):
                    w = tuple(t[slot][:, k * P:(k + 1) * P] for t in (w_hi, w_lo))
                    xs = tuple(t[:, k, n * HALF:(n + 1) * HALF] for t in x)
                    done = product(out[:, n * HALF:(n + 1) * HALF], w, xs, k == 0, k == KT - 1)
                return done

            def by_tokens(slot, k, r, x, c, bank, first, last):
                xs = tuple(t[:, k, c * P:(c + 1) * P] for t in x)
                w = tuple(t[slot][:, r * HALF:(r + 1) * HALF] for t in (w_hi, w_lo))
                return product(ps[:, bank, :], xs, w, first, last)

            def transpose(out, tile):
                return pe.transpose(out, tile, ident[:, :])

            pe.wait_ge(vec_in, 16)
            pe.wait_ge(silu_ok, 1)
            pe.wait_ge(setup_ok, 2)
            for k in range(KT):
                pe.wait_ge(ada_in[k], 16)
                for b in range(4):
                    done = pe.matmul(ps[0:2, b, :], silu_c[:, k, :], ada_raw[:, k, b * HALF:(b + 1) * HALF],
                                     start=(k == 0), stop=(k == KT - 1))
                if k == 1:
                    pe.wait_ge(csum_ok, 3)
                    pe.matmul(ps[:, 6, 0:CTX], ones[:, :], ctx_h[:, 0, :], start=True, stop=True).then_inc(sum_mm, 1)
            done.then_inc(row_sum, 1)
            pe.wait_ge(ident_in, 16)
            pe.wait_ge(row_act, 1)
            for n in range(16):
                if n == 8:
                    pe.wait_ge(row_dve, 1)
                done = pe.transpose(ps[:, 7, 2 * n:2 * n + 2], mod_row[:, n // 4, n % 4 * P:(n % 4 + 1) * P], ident[0:2, 0:2])
            done.then_inc(ada_done, 1)

            pe.wait_ge(hc_lo_ok, 2)

            def context_block(e, i, first):
                for u in range(4):
                    pe.wait_ge(lo_done, START + R_CTX + 4 * e + u + 1 + i * 8)
                    for r in range(2):
                        k = 2 * u + r
                        for c in range(NCX):
                            if k == 0 and not first:
                                pe.wait_ge(ctx_ev, START + 2 * (e - 2) + c + 1 + i * 4)
                            done = by_tokens(u % 2, k, r, (hc_hi, hc_lo), c, 2 * e + c, k == 0, k == KT - 1)
                            if k == KT - 1:
                                done.then_inc(pe_done, 1)
                    if u < 3:
                        done.then_inc(pe_done, 1)

            context_block(0, 0, True)
            context_block(1, 0, True)
            pe.wait_ge(xsum_ok, START + KT - 1)
            for n in range(2):
                done = pe.matmul(ps[:, 4 + n, :], ones[:, :], x_sum[:, n * HALF:(n + 1) * HALF], start=True, stop=True)
            done.then_inc(sum_mm, 1)
            with pe.Fori(1, 3) as i:
                for e in range(2):
                    context_block(e, i, False)

            pe.wait_ge(h_lo, START + KT)
            pe.wait_ge(root_ok, 2)
            pe.wait_ge(ctx_ev, START + 12)
            with pe.Fori(0, 4) as i:
                for u in range(4):
                    pe.wait_ge(lo_done, START + R_QK + u + 1 + i * 4)
                    pe.wait_ge(rot_mul, START + 2 * (u + 1) - 8 + i * 8)
                    by_width(u % 2, (x0_hi, x0_lo), pair(u)).then_inc(pe_done, 1)

            pe.wait_ge(rot_mul, START + 32)
            with pe.Fori(0, 8) as b:
                for u in range(4):
                    pe.wait_ge(lo_done, START + R_VG + u + 1 + b * 4)
                    for r in range(2):
                        k = 2 * u + r
                        for c in range(NCH):
                            if k == 0:
                                pe.wait_ge(vg_ev, START + c - 7 + b * 8)
                            done = by_tokens(u % 2, k, r, (x0_hi, x0_lo), c, c, k == 0, k == KT - 1)
                            if k == KT - 1:
                                done.then_inc(pe_done, 1)
                    if u < 3:
                        done.then_inc(pe_done, 1)

            pe.wait_ge(vg_ev, START + 64)
            frees = ((cv_p, 0), (cv_s, 0), (cv_s, -1), (cv_x, 0), (cv_x, 1), (cv_p, 1))
            with pe.Fori(0, 4) as i:
                for u in range(6):
                    freed, n = frees[u]
                    pe.wait_ge(lo_done, START + R_CONV + u + 1 + i * 6)
                    pe.wait_ge(freed, START + n + i * 2)
                    by_width(u % 2, (x0_hi, x0_lo), pair(CONV_PAIR[u])).then_inc(pe_done, 1)

            pe.wait_ge(cv_s, START + 7)
            pe.wait_ge(cv_x, START + 8)
            with pe.Fori(0, 8) as i:
                for u in range(2):
                    pe.wait_ge(lo_done, START + R_GATE + u + 1 + i * 2)
                    pe.wait_ge(gate_ev, START + u - 1 + i * 2)
                    by_width(u % 2, (x0_hi, x0_lo), pair(2 + u)).then_inc(pe_done, 1)

            pe.wait_ge(cv_s, START + 8)
            pe.wait_ge(gate_ev, START + 16)
            with pe.Fori(0, 2) as i:
                for p in range(2):
                    u0 = N_U * p
                    z0 = N_KZ * p

                    def state(n, terms):
                        pe.wait_ge(st_ok, START + u0 + n - 1 + i * 2 * N_U)
                        for m, (a, b) in enumerate(terms):
                            done = pe.matmul(ps[:, 4 + n % 2, :], a, b, start=(m == 0), stop=(m == len(terms) - 1))
                        done.then_inc(u_ok, 1)

                    def transpose_k(m):
                        c = NCH - 1 - m
                        pe.wait_ge(kz_ok, START + z0 + (KZ_END[m - 2] if m > 1 else 0) + i * 2 * N_KZ)
                        if m < 2:
                            pe.wait_ge(ms_ok, START + NCH * p + i * 16)
                        for k in range(2):
                            done = transpose(ps[:, m % 2, k * P:(k + 1) * P], k_t[p][:, k, c * P:(c + 1) * P])
                        done.then_inc(kt_ok, 1)

                    pe.wait_ge(ret_in[p], 80 + i * 80)
                    transpose_k(0)
                    transpose_k(1)
                    for d, kcw in enumerate((kcw_b, kcw_f)):
                        pe.wait_ge(kcw_ok, START + 4 * p + 2 * (d + 1) + i * 8)
                        for t in range(2):
                            state(2 * d + t, [(kcw[:, m, t * P:(t + 1) * P], vc_n[p][:, m, :]) for m in range(NCX)])
                    for m in range(NCH - 1):
                        c = NCH - 1 - m
                        pe.wait_ge(kz_ok, START + z0 + KZ_B[m] + i * 2 * N_KZ)
                        for t in range(2):
                            state(4 + 2 * m + t, [(kz_b[:, m % 2, t * P:(t + 1) * P], v_n[p][:, c, :])])
                        if m + 2 < NCH:
                            transpose_k(m + 2)
                    pe.wait_ge(kz_ok, START + z0 + N_KZ + i * 2 * N_KZ)

                    def scores(c):
                        pe.wait_ge(ms_ok, START + NCH * p + c - 1 + i * 16)
                        for k in range(2):
                            done = pe.matmul(ps[:, c % 2, 0:P], k_t[p][:, k, c * P:(c + 1) * P],
                                             q_t[p][:, k, c * P:(c + 1) * P], start=(k == 0), stop=(k == 1))
                        done.then_inc(sc_ok, 1)

                    def transpose_out(c):
                        n = NCH * p + c
                        pe.wait_ge(og_ok, START + n + 1 + i * 16)
                        pe.wait_ge(ogc_ok, START + n + i * 16)
                        for t in range(4):
                            done = transpose(ps[:, 6, t * P:(t + 1) * P], og[c % 2][:, t * P:(t + 1) * P])
                        done.then_inc(ogt_ok, 1)

                    scores(0)
                    pe.wait_ge(q_ok, START + 2 * (p + 1) + i * 4)
                    for c in range(NCH):
                        n = NCH * p + c
                        if c + 1 < NCH:
                            scores(c + 1)
                        pe.wait_ge(og_ok, START + n - 1 + i * 16)
                        pe.wait_ge(ms_ok, START + n + 1 + i * 16)
                        out = ps[:, 2 + c % 2, :]
                        pe.matmul(out, s_sc[:, c % 2, :], v_n[p][:, c, :], start=True, stop=False)
                        pe.wait_ge(st_ok, START + u0 + 18 + 2 * c + i * 2 * N_U)
                        for k in range(2):
                            pe.matmul(out, q_b[:, k, c * P:(c + 1) * P], s_bw[:, c, k, :], start=False, stop=False)
                        for k in range(2):
                            done = pe.matmul(out, q_f[:, k, c * P:(c + 1) * P], s_fw[:, c % 2, k, :], start=False, stop=(k == 1))
                        done.then_inc(o_ok, 1)
                        if c + 1 < NCH:
                            for t in range(2):
                                state(18 + 2 * c + t, [(kz_f[:, c, t * P:(t + 1) * P], v_n[p][:, c, :])])
                        if c > 0:
                            transpose_out(c - 1)
                    transpose_out(NCH - 1)
                    pe.wait_ge(adb_mul, START + NCH * (p + 1) + i * 16)
                    for k in range(KT):
                        done = pe.matmul(ps[:, 7, bass.ds(i * 16 + 8 * p + k, 1)], ada_acc[:, k * P:(k + 1) * P],
                                         ones[:, 0:1], start=True, stop=True)
                    done.then_inc(adb_done, 1)

            pe.wait_ge(lo_done, START + R_A)
            for stage, (base, count, x, per) in enumerate(((R_A, P_A, (x1_hi, x1_lo), 4), (R_B, P_B, (x0_hi, x0_lo), 4),
                                                           (R_C, P_C, (x1_hi, x1_lo), 2))):
                with pe.Fori(0, 4) as i:
                    for j in range(2):
                        pe.wait_ge(lo_done, START + base + per // 2 * j + 1 + i * per)
                        pe.wait_ge(mg_mul, START + 16 * stage + 2 * j - 2 + i * 4)
                        by_width(j, x, pair(j)).then_inc(pe_done, 1)

            def gain(n):
                pe.wait_ge(dg_ok, n)
                for h in range(2):
                    done = pe.matmul(pair(2)[:, h * HALF:(h + 1) * HALF], ones[:, :],
                                     diag[:, 4 * h:4 * h + 4, :].rearrange("p k t -> p (k t)"), start=True, stop=True)
                done.then_inc(row_mm, 1)

            def w_o_product(c, h, k):
                xs = tuple(t[:, k, c * P:(c + 1) * P] for t in (x0_hi, x0_lo))
                w = tuple(t[:, k, h * HALF:(h + 1) * HALF] for t in (x1_hi, x1_lo))
                return product(pair(c % 2)[:, h * HALF:(h + 1) * HALF], xs, w, k == 0, k == KT - 1)

            pe.wait_ge(mg_mul, START + 48)
            for k in range(KT):
                pe.wait_ge(m_lo, START + k + 1)
                pe.wait_ge(lo_done, START + R_WO + k + 1)
                if k == 6:
                    gain(1)
                for c in range(2):
                    for h in range(2):
                        done = w_o_product(c, h, k)
                    if k == KT - 1:
                        done.then_inc(y_done, 1)
            pe.wait_ge(row_ok, 1)

            def transpose_h(c):
                pe.wait_ge(y_hn, START + c + 1)
                if c > 1:
                    pe.wait_ge(y_dve, START + Y_COUNT["scale", c - 2])
                for k in range(KT):
                    done = transpose(pair(2 + c % 2)[:, k * P:(k + 1) * P], hn[c % 2][:, k * P:(k + 1) * P])
                done.then_inc(y_t, 1)

            for c in range(2, NCH):
                pe.wait_ge(y_dve, START + Y_COUNT["z", c - 2])
                for h in range(2):
                    for k in range(KT):
                        done = w_o_product(c, h, k)
                done.then_inc(y_done, 1)
                transpose_h(c - 2)
            transpose_h(NCH - 2)

            def up_half(u, n):
                return by_width_half(u % 2, (x0_hi, x0_lo), pair(u), n)

            pe.wait_ge(y_lo, START + NCH // 2)
            for u in range(2):
                pe.wait_ge(lo_done, START + R_UP + u + 1)
                pe.wait_ge(y_dve, START + Y_COUNT["z", NCH - 2 + u])
                up_half(u, 0)
            transpose_h(NCH - 1)
            pe.wait_ge(y_dve, START + Y_COUNT["scale", NCH - 2])
            gain(2)
            pe.wait_ge(y_lo, START + NCH)
            for u in range(2):
                up_half(u, 1).then_inc(pe_done, 1)
            pe.wait_ge(row_ok, 2)

            def up(u, i):
                pe.wait_ge(lo_done, START + R_UP + u + 1 + i * 4)
                pe.wait_ge(up_c, START + 2 * (u + 1) - 8 + i * 8)
                by_width(u % 2, (x0_hi, x0_lo), pair(u)).then_inc(pe_done, 1)

            for u in range(2, 4):
                up(u, 0)
            with pe.Fori(1, FT // 2) as i:
                for u in range(4):
                    up(u, i)

            def down(half, i, u, first, last):
                pe.wait_ge(dn_lo, START + 2 * (FT * half + u + 1) + i * 4)
                for c in range(NCH):
                    if first and half == 0:
                        pe.wait_ge(up_c, START + 2 * (2 * FT - 4 + c // 2 + 1))
                    if first and half == 1:
                        pe.wait_ge(dn_ev, START + c + 1)
                    done = product(ps[:, c, :], tuple(t[u][:, c * P:(c + 1) * P] for t in (a_hi, a_lo)),
                                   tuple(t[u][:, :] for t in (d_hi, d_lo)), first, last)
                    if last:
                        done.then_inc(dn_pe, 1)
                if not last:
                    done.then_inc(dn_pe, 1)

            for half in range(2):
                down(half, 0, 0, True, False)
                down(half, 0, 1, False, False)
                with pe.Fori(1, FT // 2 - 1) as i:
                    for u in range(2):
                        down(half, i, u, False, False)
                down(half, FT // 2 - 1, 0, False, False)
                down(half, FT // 2 - 1, 1, False, True)


def kernel(**inputs):
    import concourse.bacc as bacc
    from concourse.bass_utils import run_bass_kernel_spmd

    a = {k: np.asarray(v) for k, v in inputs.items()}

    def cols(v):
        return np.ascontiguousarray(v.reshape(-1, P).T)

    def by_column_tile(w):
        k, n = w.shape
        return np.ascontiguousarray(w.reshape(k // P, P, n // P, P).transpose(2, 1, 0, 3)).reshape(n // P, P, k)

    def by_column_block(w):
        k, n = w.shape
        return np.ascontiguousarray(w.reshape(k // 256, 2, P, n // HALF, HALF).transpose(3, 0, 2, 1, 4))\
            .reshape(n // HALF, k // 256, P, 1024)

    w_in = a["w_in"][0]
    cx_, cb_, cc_, q_, k_, v_, g_, ga_, gb_ = np.split(w_in, np.cumsum([D, D, D, D, D, 2 * D, 2 * D, D]), axis=1)
    conv_tiles = np.stack([by_column_tile(cx_), by_column_tile(cc_), by_column_tile(cb_)], axis=1).reshape(24, P, D)
    ret = a["w_ret_out"][0]
    up = by_column_tile(a["w_ffn_up"][0])
    fw = a["ffn_conv_w"][0].reshape(3, 2 * FT, P).transpose(2, 1, 0).reshape(P, 6 * FT)
    decay = np.concatenate([a["ret_decay_fw"][0], a["ret_decay_bw"][0]])
    vecs = np.concatenate(
        [cols(a["c"][0]), cols(a["c_ctx"]), cols(a["b_ada"][0]), cols(a["norm_mix_pre"][0]), cols(a["norm_mix_post"][0]),
         cols(a["norm_ffn_pre"][0]), cols(a["norm_ffn_post"][0]), cols(a["conv_w"][0]), cols(a["conv_b"][0]), fw,
         cols(a["ffn_conv_b"][0]), np.repeat(decay[None], P, axis=0)], axis=1)
    assert vecs.shape == (P, V_N)

    m, n = np.arange(P)[:, None], np.arange(P)[None, :]
    consts = np.zeros((P, C_N), np.float32)
    consts[:, C_ID:C_ID + P] = np.eye(P)
    consts[:, C_DPOS:C_DPOS + P] = np.maximum(n - m, 0)
    consts[:, C_DNEG:C_DNEG + P] = np.maximum(m - n, 0)
    consts[:, C_GE:C_GE + P] = (n >= m) * K_SCALE
    consts[:, C_LT:C_LT + P] = (n < m) * K_SCALE
    consts[:, C_RF:C_RF + P] = n + 1
    consts[:, C_RB:C_RB + P] = P - n
    consts[:, C_COLF:C_COLF + 4] = np.concatenate([P - 1 - m, CTX - 1 - m, P - 1 - m, 0 * m + P], axis=1)
    consts[:, C_COLB:C_COLB + 4] = np.concatenate([m, m, P + m, 0 * m + P], axis=1)

    pairs = DK // 4
    inv = np.float32(10000.0) ** (-np.arange(pairs, dtype=np.float32) / np.float32(pairs))
    t = np.arange(T)
    ang = np.concatenate([(t // GRID).astype(np.float32)[:, None] * inv, (t % GRID).astype(np.float32)[:, None] * inv], axis=1)
    trig = np.stack([np.cos(ang).T, np.sin(ang).T]).astype(np.float32)

    arrays = {
        "x": a["x"][0],
        "x_t": a["x"][0].T.reshape(KT, P, T),
        "ctx_t": a["ctx"][0].T.reshape(KT, P, CTX).transpose(1, 0, 2),
        "vecs": vecs,
        "consts": consts,
        "trig": np.ascontiguousarray(trig),
        "w_ada_a": a["w_ada"][0][:, :ADA].reshape(KT, P, ADA),
        "w_ada_b": a["w_ada"][0][:, ADA:].reshape(KT, P, HEADS, D).transpose(2, 0, 1, 3),
        "w_n": np.concatenate([by_column_block(k_), by_column_block(v_), by_column_block(g_)]),
        "w_t": np.concatenate([by_column_tile(q_), by_column_tile(k_), conv_tiles, by_column_tile(ga_), by_column_tile(gb_)]),
        "w_m": np.concatenate([by_column_tile(a["w_conv_out"][0]), by_column_tile(ret[:D]), by_column_tile(ret[D:])]),
        "w_o_t": a["w_o"][0].reshape(KT, P, D),
        "w_up_t": np.stack([up[:FT], up[FT:]], axis=1).reshape(2 * FT, P, D),
        "w_dn_t": a["w_ffn_down"][0].reshape(FT, P, D),
    }
    nc = bacc.Bacc("TRN2", target_bir_lowering=False, num_devices=1)
    io = {}
    for name, v in arrays.items():
        arrays[name] = np.ascontiguousarray(v)
        io[name] = nc.dram_tensor(name, arrays[name].shape, mybir.dt.from_np(v.dtype), kind="ExternalInput").ap()
    io["out"] = nc.dram_tensor("out", (T, D), F32, kind="ExternalOutput").ap()
    build(nc, io)
    r = run_bass_kernel_spmd(nc, [arrays], core_ids=[0])
    return r.results[0]["out"].reshape(1, T, D)
```

```python
import math

import numpy as np

import concourse.bass as bass
from concourse import mybir

F32 = mybir.dt.float32
F32R = mybir.dt.float32r
ACT = mybir.ActivationFunctionType
ALU = mybir.AluOpType

START = 256

P = 128
D = 1024
T = 1024
CTX = 256
GRID = 64
KT = D // P
NCH = T // P
NCX = CTX // P
HALF = 512
HEADS = 4
DK, DV = 256, 512
FF = 2816
FT = FF // P
EPS = 1e-6
K_SCALE = 1.0 / math.sqrt(DK)

V_C, V_CC, V_BADA = 0, 8, 16
V_GMIX, V_GPOST, V_GFFN, V_GFPOST = 64, 72, 80, 88
V_CW, V_CB = 96, 120
V_FW, V_FB = 128, 260
V_DEC = 304
V_N = 312

C_ID, C_DPOS, C_DNEG, C_GE, C_LT, C_RF, C_RB = 0, 128, 256, 384, 512, 640, 768
C_COLF, C_COLB = 896, 900
C_N = 904

H_D, H_XF, H_XB, H_F, H_B = 0, 128, 256, 384, 388
H_N = 392

R_CTX = 0
R_QK = R_CTX + 24
R_VG = R_QK + 16
R_CONV = R_VG + 32
R_GATE = R_CONV + 24
R_GB = R_GATE + 16
R_B = R_GB + 8
R_C = R_B + 24
R_WO = R_C + 8
R_UP = R_WO + 8

P_CTX = 0
P_QK = P_CTX + 6 * 5
P_VG = P_QK + 16
P_CONV = P_VG + 8 * 11
P_GATE = P_CONV + 24
P_GB = P_GATE + 16
P_B = P_GB + 8
P_C = P_B + 8
P_UP = P_C + 8

ST_KVC = 0
ST_QK = ST_KVC + 6
ST_VG = ST_QK + 2 * HEADS
ST_MC = ST_VG + 8 * NCH
ST_GATE = ST_MC + KT
ST_GO = ST_GATE + KT
ST_X1 = ST_GO + HEADS * NCH
ST_A = ST_X1 + NCH

ADA = 2 * D
CONV_PAIR = (0, 1, 2, 3, 0, 1)
N_DOWN = FT - 1 + NCH

N_U = 4 + 2 * 2 * (NCH - 1)
KZ_B, KZ_END = [], []
for _m in range(NCH):
    _n = KZ_END[-1] if KZ_END else 0
    KZ_B.append(_n + 1)
    KZ_END.append(_n + (_m < NCH - 1) + (_m > 0))
N_KZ = KZ_END[-1]

Y_COUNT = {}
for _c in range(NCH + 1):
    for _step, _of in (("inv1", _c), ("z", _c), ("inv2", _c), ("scale", _c - 1), ("shift", _c - 1)):
        if 0 <= _of < NCH:
            Y_COUNT[_step, _of] = len(Y_COUNT) + 1

Y_PAIR = (0, 1, 3, 1, 0, 1, 0, 1)
T_PAIR = (2, 2, 3, 2, 3, 2, 3, 2)
Y_FREED = (None, None, None, 1, 0, 3, 4, 5)

DC_T, DC_AZ, DC_U, DC_W, DC_LN, DC_CORR, DC_RW, DC_LG = range(8)


def build(nc, io):
    ps = nc.alloc_psum_tensor("ps", [P, 8, HALF], F32)

    def pair(n):
        return ps[:, 2 * n:2 * n + 2, :].rearrange("p b c -> p (b c)")

    kb = 1024
    PERS = 16640
    RING = PERS + 12 * kb
    X0 = RING + 24 * kb
    X1 = X0 + 64 * kb
    REST = X1 + 64 * kb
    end = nc.sbuf_usable_end
    top = [0]

    def sb(name, shape, at, dt=F32):
        size = 4 * int(np.prod(shape[1:]))
        assert at + size <= end, (name, at + size, end)
        top[0] = at + size
        return nc.alloc_sbuf_tensor_at(name, shape, dt, offset=at)

    def after(align=32):
        return -(-top[0] // align) * align

    vec = sb("vec", [P, V_N], PERS)
    ident = sb("ident", [P, P], after())
    ones = sb("ones", [P, P], after())
    silu_c = sb("silu_c", [P, KT, 2], after())
    mod_a = sb("mod_a", [P, 16, 2], after())
    mod_b = sb("mod_b", [P, 32], after())
    scale_x = sb("scale_x", [P, KT, 2], after())
    scale_h = sb("scale_h", [P, KT], after())
    gain_y = sb("gain_y", [P, KT], after())
    gain_f = sb("gain_f", [P, KT], after())
    head_tab = sb("head_tab", [P, HEADS, H_N], after())
    root = sb("root", [P, NCH], after())
    rinv = sb("rinv", [P, NCH], after())
    dec = sb("dec", [P, 8, 8], after())
    onum = sb("onum", [P, 2, 4], after())
    eps = sb("eps", [P, 1], after())
    st1 = sb("st1", [P, 8, 4], after())
    st2 = sb("st2", [P, 8, 4], after())
    assert top[0] <= RING, top[0] - RING

    raw = [sb(f"raw{n}", [P, 1024], RING + 4096 * n) for n in range(2)]
    w_hi = [sb(f"w_hi{n}", [P, 1024], RING + 8192 + 4096 * n, F32R) for n in range(2)]
    w_lo = [sb(f"w_lo{n}", [P, 1024], RING + 16384 + 4096 * n, F32R) for n in range(2)]

    x0_hi = sb("x0_hi", [P, KT, T], X0, F32R)
    x0_lo = sb("x0_lo", [P, KT, T], X0 + 32 * kb, F32R)
    x1_hi = sb("x1_hi", [P, KT, T], X1, F32R)
    x1_lo = sb("x1_lo", [P, KT, T], X1 + 32 * kb, F32R)

    hc_hi = sb("hc_hi", [P, KT, CTX], X1, F32R)
    hc_lo = sb("hc_lo", [P, KT, CTX], after(), F32R)
    x_in = sb("x_in", [P, KT, T], after())
    ctx_in = sb("ctx_in", [P, KT, CTX], after())
    ctx_h = sb("ctx_h", [P, KT, CTX], after())
    raw_c = raw + [sb(f"raw_c{n}", [P, 1024], X1 + (48 + 4 * n) * kb) for n in range(2)]
    x_sq = [sb(f"x_sq{n}", [P, T], REST + 4096 * n) for n in (4, 1, 0, 3)]
    x_sum = sb("x_sum", [P, T], REST + 8192)
    diag_x = sb("diag_x", [P, NCH, P], REST + 12288)
    aff = [sb(f"aff{n}", [P, T], REST + 16384 + 4096 * n) for n in range(2)]
    ctx_out = [sb(f"ctx_out{n}", [P, NCX, HALF], REST + 24576 + 4096 * n) for n in range(2)]
    const = sb("const", [P, C_N], after())
    dtmp = sb("dtmp", [P, HEADS, P], after())
    inv_c = sb("inv_c", [P, CTX], after())
    ada_raw = sb("ada_raw", [P, KT, ADA], X0)
    mod_row = sb("mod_row", [2, 4, HALF], REST + 16384)

    cos = sb("cos", [P, T], X1)
    sin = sb("sin", [P, T], X1 + 4 * kb)
    rot_a = [sb(f"rot_a{n}", [P, 2, T], X1 + (8 + 8 * n) * kb) for n in range(2)]
    rot_b = [sb(f"rot_b{n}", [P, 2, T], X1 + (24 + 8 * n) * kb) for n in range(2)]
    rot_o = [sb(f"rot_o{n}", [P, 2, T], X1 + (40 + 8 * n) * kb) for n in range(2)]
    vg_out = [sb(f"vg_out{n}", [P, HALF], REST + 2048 * n) for n in range(8)]
    co = [sb(f"co{n}", [P, T], REST + (0 + 4 * n) * kb) for n in range(2)]
    cx = [sb(f"cx{n}", [P, T], REST + (16 + 4 * n) * kb) for n in range(2)]
    cprod = [sb(f"cprod{n}", [P, T], REST + (24 + 4 * n) * kb) for n in range(2)]
    cy = [sb(f"cy{n}", [P, T], REST + (32 + 4 * n) * kb) for n in range(2)]
    gate_o = [sb(f"gate_o{n}", [P, T], REST + 35 * kb + 512 + 4096 * n) for n in range(2)]
    mc_out = [sb(f"mc_out{n}", [P, T], REST + (16 + 4 * n) * kb) for n in range(2)]

    top[0] = X1

    def two(name, shape, starts):
        return [sb(f"{name}{n}", shape, starts[n]) for n in range(2)]

    def place(name, shape, count=None, dt=F32):
        if count is None:
            return sb(name, shape, after(), dt)
        return [sb(f"{name}{n}", shape, after(), dt) for n in range(count)]

    q_t = two("q_t", [P, 2, T], (X1, X0))
    k_t = two("k_t", [P, 2, T], (X1 + 8 * kb, X0 + 8 * kb))
    v_n = two("v_n", [P, NCH, DV], (X1 + 16 * kb, X0 + 16 * kb))
    kc_n = two("kc_n", [P, NCX, DK], (X1 + 32 * kb, X0 + 32 * kb))
    vc_n = two("vc_n", [P, NCX, DV], (X1 + 34 * kb, X0 + 34 * kb))
    kz_f = place("kz_f", [P, NCH, DK])
    kz_b = place("kz_b", [P, 2, DK])
    s_sc = place("s_sc", [P, 2, P])
    g_in = place("g_in", [P, DV], 2)
    og = place("og", [P, DV], 2)
    ada_acc = place("ada_acc", [P, D])
    sq_j = place("sq_j", [P, DV])
    assert top[0] <= X1
    top[0] = X1 + 38 * kb
    kcw_f = place("kcw_f", [P, NCX, DK])
    kcw_b = place("kcw_b", [P, NCX, DK])
    q_f = place("q_f", [P, 2, T])
    q_b = place("q_b", [P, 2, T])
    s_fw = place("s_fw", [P, 2, 2, DV])
    og_t = place("og_t", [P, 4, P], 2)
    s_bw = place("s_bw", [P, NCH, 2, DV])
    ada_ret = [nc.alloc_sbuf_tensor_at(f"ada_ret{n}", [P, D], F32, offset=RING + 12288 + 8192 * n) for n in range(2)]

    merged = sb("merged", [P, KT, T], REST)
    gate_in = [sb(f"gate_in{n}", [P, T], REST + (32 + 4 * n) * kb) for n in range(2)]
    mtmp = sb("mtmp", [P, HALF], REST + 40 * kb)
    gain_row = sb("gain_row", [P, D], REST)
    diag = sb("diag", [P, KT, P], REST + 4 * kb)
    xr = [sb(f"xr{n}", [P, D], REST + (8 + 4 * n) * kb) for n in range(2)]
    x1n = [sb(f"x1n{n}", [P, D], REST + (16 + 4 * n) * kb) for n in range(2)]
    hn = [sb(f"hn{n}", [P, D], REST + (24 + 4 * n) * kb) for n in range(2)]
    haff = sb("haff", [P, D], REST + 32 * kb)
    junk2 = sb("junk2", [P, D], REST + 36 * kb)
    uy = [[sb(f"uy{n}{m}", [P, T], X1 + (12 * n + 4 * m) * kb) for m in range(2)] for n in range(2)]
    ua = [sb(f"ua{n}", [P, T], X1 + (12 * n + 8) * kb) for n in range(2)]
    a_raw = [sb(f"a_raw{n}", [P, T], X1 + (24 + 4 * n) * kb) for n in range(2)]
    d_raw = [sb(f"d_raw{n}", [P, HALF], X1 + (32 + 2 * n) * kb) for n in range(2)]
    d_hi = [sb(f"d_hi{n}", [P, HALF], X1 + (36 + 2 * n) * kb, F32R) for n in range(2)]
    d_lo = [sb(f"d_lo{n}", [P, HALF], X1 + (40 + 2 * n) * kb, F32R) for n in range(2)]
    a_hi = [sb(f"a_hi{n}", [P, T], X1 + (44 + 4 * n) * kb, F32R) for n in range(2)]
    a_lo = [sb(f"a_lo{n}", [P, T], X1 + (52 + 4 * n) * kb, F32R) for n in range(2)]
    f0 = sb("f0", [P, NCH, HALF], X0)
    x1all = sb("x1all", [P, NCH, D], X0 + 16 * kb)
    fo = [sb(f"fo{n}", [P, D], X0 + (48 + 4 * n) * kb if n < 4 else X1 + 4 * (n - 4) * kb) for n in range(NCH)]
    junk3 = sb("junk3", [P, HALF], REST + 4 * kb)
    fsum = sb("fsum", [P, 8, 8], REST + 8 * kb)

    def dram(name, shape):
        return nc.dram_tensor(name, shape, F32).ap()

    kvc_d = dram("kvc_d", [6, P, NCX, HALF])
    qk_d = dram("qk_d", [2 * HEADS, P, 2, T])
    vg_d = dram("vg_d", [2 * HEADS, NCH, P, DV])
    mc_d = dram("mc_d", [KT, P, T])
    gate_d = dram("gate_d", [KT, P, T])
    go_d = dram("go_d", [HEADS * 4, P, T])
    x1_d = dram("x1_d", [NCH, P, D])
    a_d = dram("a_d", [FT, P, T])

    def sem(name):
        return nc.alloc_semaphore(name)

    vec_in, ident_in, const_in, ctx_ready = sem("vec_in"), sem("ident_in"), sem("const_in"), sem("ctx_ready")
    x_ready = [sem(f"x_ready{n}") for n in range(4)]
    ada_in = [sem(f"ada_in{n}") for n in range(KT)]
    inv_mm = sem("inv_mm")
    row_sum, row_act, row_dve = sem("row_sum"), sem("row_act"), sem("row_dve")
    silu_ok, ada_done, mod_ok = sem("silu_ok"), sem("ada_done"), sem("mod_ok")
    act0, dve0 = sem("act0"), sem("dve0")
    csq_ok, xsq_ok, csum_ok, xsum_ok, sum_mm, root_ok, inv_ok, z_ok, ca_ok, cb_ok, aff_ok, hc_hi_ok, hc_lo_ok, h_hi, h_lo = (
        sem(n) for n in ("csq_ok", "xsq_ok", "csum_ok", "xsum_ok", "sum_mm", "root_ok", "inv_ok", "z_ok", "ca_ok", "cb_ok",
                         "aff_ok", "hc_hi_ok", "hc_lo_ok", "h_hi", "h_lo"))
    setup_ok = sem("setup_ok")
    raw_c_in = [sem(f"raw_c_in{n}") for n in range(4)]
    raw_in = [sem("raw_in0"), sem("raw_in1")]
    hi_done, lo_done, pe_done = sem("hi_done"), sem("lo_done"), sem("pe_done")
    kvc_st, qk_st, vg_st, mc_st, gate_st, go_st, x1_st, a_st = (
        sem(n) for n in ("kvc_st", "qk_st", "vg_st", "mc_st", "gate_st", "go_st", "x1_st", "a_st"))
    out_st = sem("out_st")
    landed = sem("landed")
    ctx_ev, trig_in, rot_mul, rot_add, vg_ev = (sem(n) for n in ("ctx_ev", "trig_in", "rot_mul", "rot_add", "vg_ev"))
    cv_x, cv_p, cv_b, cv_y, cv_s, cv_hi, cv_lo = (
        sem(n) for n in ("cv_x", "cv_p", "cv_b", "cv_y", "cv_s", "cv_hi", "cv_lo"))
    gate_ev, mc_ok = sem("gate_ev"), sem("mc_ok")
    ret_in, g_ld = [sem("ret_in0"), sem("ret_in1")], [sem("g_ld0"), sem("g_ld1")]
    (q_ok, kcw_ok, kt_ok, kz_ok, u_ok, st_ok, sc_ok, ms_ok, o_ok, osq_ok, ort_ok,
     oinv_ok, og_ok, ogt_ok, ogc_ok) = (sem(n) for n in (
         "q_ok", "kcw_ok", "kt_ok", "kz_ok", "u_ok", "st_ok", "sc_ok", "ms_ok", "o_ok", "osq_ok",
         "ort_ok", "oinv_ok", "og_ok", "ogt_ok", "ogc_ok"))
    adb_in, adb_mul, adb_done = [sem("adb_in0"), sem("adb_in1")], sem("adb_mul"), sem("adb_done")
    gt_in, mg_mul, mg_add = [sem("gt_in0"), sem("gt_in1")], sem("mg_mul"), sem("mg_add")
    m_hi, m_lo = sem("m_hi"), sem("m_lo")
    wo_hi, wo_lo = sem("wo_hi"), sem("wo_lo")
    dg_ok, row_mm, row_ok = sem("dg_ok"), sem("row_mm"), sem("row_ok")
    xr_in, y_done, y_sq, y_act, y_dve, y_x1, y_hn, y_t, y_hi, y_lo = (
        [sem("xr_in0"), sem("xr_in1")], *(sem(n) for n in (
            "y_done", "y_sq", "y_act", "y_dve", "y_x1", "y_hn", "y_t", "y_hi", "y_lo")))
    up_b, up_c, up_s, up_a = (sem(n) for n in ("up_b", "up_c", "up_s", "up_a"))
    dn_in, dn_hi, dn_lo, dn_pe, dn_ev, dn_sq, dn_add, dn_dve, dn_rt, dn_half, out_ok = (
        [sem("dn_in0"), sem("dn_in1")], *(sem(n) for n in (
            "dn_hi", "dn_lo", "dn_pe", "dn_ev", "dn_sq", "dn_add", "dn_dve", "dn_rt", "dn_half", "out_ok")))
    x1_in, f_row = [sem("x1_in0"), sem("x1_in1")], sem("f_row")

    with nc.Block() as block:

        @block.sync
        def _(sp):
            def context_load(r, i, src):
                sp.wait_ge(lo_done, START + R_CTX + r - 3 + i * 4)
                sp.dma_start(raw_c[r % 4][:, :], src).then_inc(raw_c_in[r % 4], 16)

            def load(base, i, per, src):
                sp.wait_ge(lo_done, START + base - 1 + i * per)
                sp.dma_start(raw[base % 2][:, :], src).then_inc(raw_in[base % 2], 16)

            sp.dma_start(vec[:, :], io["vecs"]).then_inc(vec_in, 16)
            for k in range(KT):
                sp.dma_start(ada_raw[:, k, :], io["w_ada_a"][k]).then_inc(ada_in[k], 16)
                if k == 0:
                    sp.dma_start(ctx_in[:, :, :], io["ctx_t"]).then_inc(ctx_ready, 16)
                    sp.dma_start(ident[:, :], io["consts"][:, C_ID:C_ID + P]).then_inc(ident_in, 16)
                if k == 1:
                    sp.dma_start(const[:, :], io["consts"]).then_inc(const_in, 16)
            for u in range(2):
                context_load(u, 0, io["w_n"][0, u])
            for n in range(4):
                sp.dma_start(x_in[:, 2 * n:2 * n + 2, :],
                             io["x_t"][2 * n:2 * n + 2].rearrange("n p d -> p n d")).then_inc(x_ready[n], 16)
            sp.wait_ge(hc_lo_ok, 3)
            for u in range(2, 4):
                context_load(u, 0, io["w_n"][0, u])
            with sp.Fori(1, 6) as b:
                for u in range(4):
                    context_load(u, b, io["w_n"][b, u])
            for u in range(2):
                load(R_QK + u, 0, 0, io["w_t"][u])
            sp.wait_ge(pe_done, START + P_QK)
            sp.dma_start(cos[:, :], io["trig"][0]).then_inc(trig_in, 16)
            sp.dma_start(sin[:, :], io["trig"][1]).then_inc(trig_in, 16)
            for u in range(2, 4):
                load(R_QK + u, 0, 0, io["w_t"][u])
            with sp.Fori(1, 4) as i:
                for u in range(4):
                    load(R_QK + u, i, 4, io["w_t"][i * 4 + u])
            with sp.Fori(0, 8) as b:
                for u in range(4):
                    load(R_VG + u, b, 4, io["w_n"][b + 2, u])
            with sp.Fori(0, 4) as i:
                for u in range(6):
                    load(R_CONV + u, i, 6, io["w_t"][i * 6 + (16 + u)])
            with sp.Fori(0, 4) as i:
                for u in range(4):
                    load(R_GATE + u, i, 4, io["w_t"][i * 4 + (40 + u)])
            for u in range(2):
                load(R_GB + u, 0, 0, io["w_t"][56 + u])

            sp.wait_ge(pe_done, START + P_GB)
            sp.wait_ge(vg_st, START + 64)
            sp.wait_ge(qk_st, START + 8)

            def head_loads(h):
                p = h % 2
                sp.dma_start(q_t[p][:, :, :], qk_d[h]).then_inc(ret_in[p], 16)
                sp.dma_start(k_t[p][:, :, :], qk_d[h + HEADS]).then_inc(ret_in[p], 16)
                sp.dma_start(v_n[p][:, :, :], vg_d[h].rearrange("c p d -> p c d")).then_inc(ret_in[p], 16)
                sp.dma_start(kc_n[p][:, :, :], kvc_d[h // 2, :, :, p * DK:(p + 1) * DK]).then_inc(ret_in[p], 16)
                sp.dma_start(vc_n[p][:, :, :], kvc_d[h + 2]).then_inc(ret_in[p], 16)

            head_loads(0)
            with sp.Fori(1, 4) as i:
                for u in range(2):
                    load(R_GB + u, i, 2, io["w_t"][i * 2 + (56 + u)])
            sp.wait_ge(pe_done, START + P_B)
            sp.wait_ge(gate_st, START + KT)
            head_loads(1)
            sp.wait_ge(lo_done, START + R_B)
            for h in range(HEADS):
                with sp.Fori(0, NCH // 2) as i:
                    for e in range(2):
                        n = h * NCH + e
                        sp.wait_ge(og_ok, START + n - 1 + i * 2)
                        sp.dma_start(g_in[e][:, :], vg_d[h + HEADS, i * 2 + e]).then_inc(g_ld[e], 16)
                        sp.wait_ge(adb_mul, START + n - 1 + i * 2)
                        sp.dma_start(ada_ret[e][:, :], io["w_ada_b"][h, i * 2 + e]).then_inc(adb_in[e], 16)
                if h == HEADS - 2:
                    load(R_B, 0, 0, io["w_m"][0])
                    load(R_B + 1, 0, 0, go_d[0])
                if h + 2 < HEADS:
                    sp.wait_ge(ogt_ok, START + NCH * (h + 1))
                    sp.wait_ge(q_ok, START + 2 * (h + 1))
                    sp.wait_ge(go_st, START + NCH * (h + 1))
                    head_loads(h + 2)

            load(R_B + 2, 0, 0, io["w_m"][1])

            def gate_load(stage, j, i):
                sp.wait_ge(mg_mul, START + 2 * (8 * stage + j - 1) + i * 4)
                sp.dma_start(gate_in[j][:, :], gate_d[i * 2 + j]).then_inc(gt_in[j], 16)
                if stage == 0:
                    sp.dma_start(merged[:, bass.ds(i * 2 + j, 1), :].rearrange("p k t -> p (k t)"), mc_d[i * 2 + j])\
                      .then_inc(gt_in[j], 16)

            for k in range(1, KT):
                load(R_B + 2 + k, 0, 0, go_d[k])
                if k == 4:
                    sp.wait_ge(go_st, START + HEADS * NCH)
                    gate_load(0, 0, 0)
            load(R_B + 10, 0, 0, io["w_m"][2])
            for j in range(2):
                load(R_B + 11 + j, 0, 0, go_d[8 + j])
            gate_load(0, 1, 0)
            with sp.Fori(1, 4) as i:
                for j in range(2):
                    load(R_B + 9 + 2 * j, i, 4, go_d[i * 2 + (8 + j)])
                    load(R_B + 10 + 2 * j, i, 4, io["w_m"][i * 2 + (j + 1)])
                    gate_load(0, j, i)
            for i in range(4):
                for j in range(2):
                    if i + j > 0:
                        load(R_C + j, i, 2, io["w_m"][i * 2 + (8 + j)])
                    gate_load(1, j, i)
            with sp.Fori(0, 4) as i:
                for j in range(2):
                    load(R_WO + j, i, 2, io["w_o_t"][i * 2 + j])
            load(R_UP, 0, 0, io["w_up_t"][0])
            load(R_UP + 1, 0, 0, io["w_up_t"][1])
            sp.wait_ge(m_lo, START + KT)
            for c in range(NCH):
                sp.wait_ge(y_x1, START + c - 1)
                sp.dma_start(xr[c % 2][:, :], io["x"][c * P:(c + 1) * P, :]).then_inc(xr_in[c % 2], 16)

            for u in range(2, 4):
                load(R_UP + u, 0, 0, io["w_up_t"][u])
            with sp.Fori(1, FT // 2 - 1) as i:
                for u in range(4):
                    load(R_UP + u, i, 4, io["w_up_t"][i * 4 + u])

            def down_load(half, u, i):
                sp.wait_ge(dn_lo, START + 2 * (half * FT + u - 1) + i * 4)
                sp.dma_start(d_raw[u][:, :], io["w_dn_t"][i * 2 + u, :, half * HALF:(half + 1) * HALF])\
                  .then_inc(dn_in[u], 16)
                if half == 0:
                    sp.wait_ge(a_st, START + u + 1 + i * 2)
                sp.dma_start(a_raw[u][:, :], a_d[i * 2 + u]).then_inc(dn_in[u], 16)

            down_load(0, 0, 0)
            down_load(0, 1, 0)
            for u in range(4):
                load(R_UP + 2 * FT - 4 + u, 0, 0, io["w_up_t"][2 * FT - 4 + u])

            with sp.Fori(1, FT // 2) as i:
                for u in range(2):
                    down_load(0, u, i)
            sp.wait_ge(pe_done, START + P_UP + 2 * FT)
            sp.wait_ge(x1_st, START + NCH)
            with sp.Fori(0, NCH // 2) as i:
                for u in range(2):
                    down_load(1, u, i)
                    sp.dma_start(x1all[:, bass.ds(i * 2 + u, 1), :].rearrange("p k t -> p (k t)"), x1_d[i * 2 + u])\
                      .then_inc(x1_in[u], 16)
            with sp.Fori(NCH // 2, FT // 2) as i:
                for u in range(2):
                    down_load(1, u, i)
            for c in range(NCH):
                sp.wait_ge(out_ok, START + c + 1)
                sp.wait_ge(dn_dve, START + 2 * (c + 1))
                sp.dma_start(io["out"][c * P:(c + 1) * P, :], fo[c][:, :]).then_inc(out_st, 16)
            sp.wait_ge(out_st, 16 * NCH)

        @block.gpsimd
        def _(pool):
            for s in (kvc_st, qk_st, vg_st, mc_st, gate_st, go_st, x1_st, a_st, xsum_ok, q_ok, out_ok):
                pool.sem_inc(s, START)

            def store(dst, src, n, stored):
                pool.dma_start(dst, src).then_inc(landed, 16)
                pool.wait_ge(landed, 16 * (n + 1) if isinstance(n, int) else n * 16 + 16)
                pool.sem_inc(stored, 1)

            pool.memset(ones[:, :], 1.0).then_inc(setup_ok, 1)
            pool.memset(eps[:, :], EPS).then_inc(setup_ok, 1)
            for k in range(1, KT):
                pool.wait_ge(xsq_ok, START + k + 1)
                pool.wait_ge(xsum_ok, START + k - 1)
                pool.tensor_tensor(x_sum[:, :], x_sum[:, :], x_sq[k % 4][:, :], ALU.add).then_inc(xsum_ok, 1)
            with pool.Fori(0, 3) as i:
                for e in range(2):
                    pool.wait_ge(ctx_ev, START + 2 * (e + 1) + i * 4)
                    store(kvc_d[i * 2 + e], ctx_out[e][:, :, :], i * 2 + (ST_KVC + e), kvc_st)
            with pool.Fori(0, 4) as i:
                for d in range(2):
                    pool.wait_ge(rot_add, START + 2 * (d + 1) + i * 4)
                    store(qk_d[i * 2 + d], rot_o[d][:, :, :], i * 2 + (ST_QK + d), qk_st)
            with pool.Fori(0, 8) as b:
                for c in range(NCH):
                    pool.wait_ge(vg_ev, START + c + 1 + b * 8)
                    store(vg_d[b, c], vg_out[c][:, :], b * 8 + (ST_VG + c), vg_st)
            with pool.Fori(0, 4) as i:
                for j in range(2):
                    pool.wait_ge(mc_ok, START + j + 1 + i * 2)
                    store(mc_d[i * 2 + j], mc_out[j][:, :], i * 2 + (ST_MC + j), mc_st)
            with pool.Fori(0, 4) as i:
                for j in range(2):
                    pool.wait_ge(gate_ev, START + KT + j + 1 + i * 2)
                    store(gate_d[i * 2 + j], gate_o[j][:, :], i * 2 + (ST_GATE + j), gate_st)

            for i in range(HEADS // 2):
                for p in range(2):
                    pool.wait_ge(ret_in[p], 80 + i * 80)
                    pool.wait_ge(o_ok, START + NCH * p + i * 16)
                    for dst, col in ((q_f, H_XF), (q_b, H_XB)):
                        rows = head_tab[:, 2 * i + p, col:col + P].unsqueeze(1).broadcast_to([P, 2 * NCH, P])
                        pool.tensor_tensor(dst[:, :, :].rearrange("p k (c t) -> p (k c) t", t=P),
                                           q_t[p][:, :, :].rearrange("p k (c t) -> p (k c) t", t=P),
                                           rows, ALU.mult).then_inc(q_ok, 1)
                    for c in range(NCH):
                        pool.wait_ge(ogc_ok, START + NCH * p + c + 1 + i * 16)
                        store(go_d[bass.ds(i * 8 + 4 * p, 4), :, c * P:(c + 1) * P].rearrange("k p t -> p k t"),
                              og_t[c % 2][:, :, :], i * 16 + (ST_GO + NCH * p + c), go_st)
            for c in range(NCH):
                pool.wait_ge(y_x1, START + c + 1)
                store(x1_d[c], x1n[c % 2][:, :], ST_X1 + c, x1_st)
            with pool.Fori(0, FT // 2) as i:
                for j in range(2):
                    pool.wait_ge(up_a, START + j + 1 + i * 2)
                    store(a_d[i * 2 + j], ua[j][:, :], i * 2 + (ST_A + j), a_st)
            for n in range(2):
                pool.wait_ge(x1_in[n], 16 * NCH // 2)
            for c in range(NCH):
                pool.wait_ge(dn_half, START + c + 1)
                pool.tensor_tensor(fo[c][:, 0:HALF], fo[c][:, 0:HALF], x1all[:, c, 0:HALF], ALU.add).then_inc(out_ok, 1)

        @block.scalar
        def _(act):
            for s in (hi_done, xsq_ok, aff_ok, h_hi, ctx_ev, vg_ev, cv_x, cv_b, cv_hi, gate_ev, kcw_ok, kz_ok,
                      osq_ok, ort_ok, ogc_ok, m_hi, y_sq, y_act, y_hn, y_hi, up_b, up_s, dn_hi, dn_sq, dn_rt, dn_half):
                act.sem_inc(s, START)

            def split_hi(base, i, per, dst):
                act.wait_ge(raw_in[base % 2], 16 * ((base - R_QK) // 2 + 1) + i * (8 * per))
                act.activation(dst, raw[base % 2][:, :], ACT.Copy).then_inc(hi_done, 1)

            def context_hi(r, i):
                act.wait_ge(raw_c_in[r % 4], 16 * (r // 4 + 1) + i * 32)
                act.activation(w_hi[r % 2][:, :], raw_c[r % 4][:, :], ACT.Copy).then_inc(hi_done, 1)

            act.wait_ge(vec_in, 16)
            act.activation(silu_c[:, :, :].rearrange("p k v -> p v k"),
                           vec[:, V_C:V_C + 16].rearrange("p (v k) -> p v k", v=2), ACT.Silu).then_inc(silu_ok, 1)
            act.wait_ge(setup_ok, 2)
            act.wait_ge(ctx_ready, 16)
            act.activation(ctx_h[:, :, :], ctx_in[:, :, :], ACT.Square).then_inc(csq_ok, 1)
            act.wait_ge(dve0, 2)
            act.activation(dec[:, DC_U, :], dec[:, DC_AZ, :], ACT.Exp, scale=-1.0).then_inc(act0, 1)
            act.wait_ge(dve0, 3)
            act.activation(dec[:, DC_LN, :], dec[:, DC_W, :], ACT.Ln).then_inc(act0, 1)
            act.wait_ge(dve0, 8)
            act.wait_ge(const_in, 16)
            for h in range(HEADS):
                fw, bw = dec[:, DC_LG, h:h + 1], dec[:, DC_LG, HEADS + h:HEADS + h + 1]
                for dst, src, scale in ((head_tab[:, h, H_D:H_D + P], const[:, C_DPOS:C_DPOS + P], fw),
                                        (dtmp[:, h, :], const[:, C_DNEG:C_DNEG + P], bw),
                                        (head_tab[:, h, H_XF:H_XF + P], const[:, C_RF:C_RF + P], fw),
                                        (head_tab[:, h, H_XB:H_XB + P], const[:, C_RB:C_RB + P], bw),
                                        (head_tab[:, h, H_F:H_F + 4], const[:, C_COLF:C_COLF + 4], fw),
                                        (head_tab[:, h, H_B:H_B + 4], const[:, C_COLB:C_COLB + 4], bw)):
                    act.activation(dst, src, ACT.Exp, scale=scale).then_inc(act0, 1)

            act.wait_ge(sum_mm, 1)
            act.activation(inv_c[:, :], ps[:, 6, 0:CTX], ACT.Sqrt, bias=eps[:, :], scale=1.0 / D).then_inc(root_ok, 1)
            context_hi(0, 0)
            context_hi(1, 0)
            for b in range(2):
                act.wait_ge(row_sum, b + 1)
                act.activation(mod_row[:, b, :], ps[0:2, b, :], ACT.Copy).then_inc(row_act, 1)

            def square_x(k):
                act.wait_ge(x_ready[k // 2], 16)
                act.activation((x_sum if k == 0 else x_sq[k])[:, :], x_in[:, k, :], ACT.Square).then_inc(xsq_ok, 1)

            for k in range(2):
                square_x(k)
            act.wait_ge(mod_ok, 2)
            act.wait_ge(z_ok, START + 1)
            for k in range(KT // 2):
                act.activation(ctx_h[:, k, :], ctx_in[:, k, :], ACT.Identity, scale=scale_x[:, k, 1:2],
                               bias=mod_a[:, k, 1:2]).then_inc(ca_ok, 1)
                if k % 2 == 1:
                    act.wait_ge(ca_ok, k + 1)
                    act.activation(hc_hi[:, k - 1:k + 1, :], ctx_h[:, k - 1:k + 1, :], ACT.Copy).then_inc(hc_hi_ok, 1)
            act.wait_ge(cb_ok, 2)
            act.activation(hc_hi[:, 4:8, :], ctx_h[:, 4:8, :], ACT.Copy).then_inc(hc_hi_ok, 1)
            square_x(2)
            square_x(3)

            def context_unit(e, u, i, last=False):
                act.wait_ge(pe_done, START + 5 * e + u + i * 10)
                if last and (e, u) == (1, 3):
                    split_hi(R_QK, 0, 0, w_hi[0][:, :])
                else:
                    context_hi(4 * e + u + 1, i)

            def context_out(e, i):
                act.wait_ge(kvc_st, START + e - 1 + i * 2)
                for c in range(NCX):
                    act.wait_ge(pe_done, START + 5 * e + 3 + c + 1 + i * 10)
                    act.activation(ctx_out[e % 2][:, c, :], ps[:, 2 * (e % 2) + c, :], ACT.Copy).then_inc(ctx_ev, 1)

            for e in range(2):
                for u in range(4):
                    if e > 0 or u > 0:
                        context_unit(e, u, 0)
                    for k in ((2 * u + 4, 2 * u + 5) if e == 0 and u < 2 else ()):
                        act.wait_ge(x_ready[k // 2], 16)
                        act.wait_ge(ada_done, 1)
                        act.wait_ge(xsum_ok, START + max(k - 4, 0))
                        act.activation(x_sq[k % 4][:, :], x_in[:, k, :], ACT.Square).then_inc(xsq_ok, 1)
                    if (e, u) == (1, 2):
                        act.wait_ge(sum_mm, 2)
                        act.activation(root[:, :], ps[:, 6, 0:NCH], ACT.Sqrt, bias=eps[:, :], scale=1.0 / D).then_inc(root_ok, 1)
                context_out(e, 0)
            for i in (1, 2):
                for e in range(2):
                    for u in range(4):
                        k = 4 * i + 2 * e + u // 2 - 4
                        final = k == KT - 1 and u == 3
                        if not final:
                            context_unit(e, u, i)
                        if u % 2 == 0:
                            act.wait_ge(z_ok, START + k + 2)
                            act.wait_ge(h_lo, START + k - 1)
                            act.activation(aff[k % 2][:, :], x_in[:, k, :], ACT.Identity, scale=scale_x[:, k, 0:1],
                                           bias=mod_a[:, k, 0:1]).then_inc(aff_ok, 1)
                        else:
                            act.wait_ge(aff_ok, START + k + 1)
                            act.activation(x0_hi[:, k, :], aff[k % 2][:, :], ACT.Copy).then_inc(h_hi, 1)
                        if final:
                            context_unit(e, u, i, last=True)
                    context_out(e, i)

            with act.Fori(0, 4) as i:
                for u in range(4):
                    act.wait_ge(pe_done, START + P_QK + u + i * 4)
                    split_hi(R_QK + u + 1, i, 4, w_hi[(u + 1) % 2][:, :])

            for base, func in ((0, ACT.Copy), (4, ACT.Silu)):
                with act.Fori(0, 4) as b:
                    for u in range(4):
                        act.wait_ge(pe_done, START + P_VG + 11 * base + u + b * 11)
                        split_hi(R_VG + 4 * base + u + 1, b, 4, w_hi[(u + 1) % 2][:, :])
                    for c in range(NCH):
                        act.wait_ge(vg_st, START + 8 * base + c - 7 + b * 8)
                        act.wait_ge(pe_done, START + P_VG + 11 * base + 4 + c + b * 11)
                        act.activation(vg_out[c][:, :], ps[:, c, :], func).then_inc(vg_ev, 1)

            act.wait_ge(qk_st, START + 8)
            with act.Fori(0, 4) as i:
                for j in range(2):
                    for m in range(3):
                        u = 3 * j + m
                        act.wait_ge(pe_done, START + P_CONV + u + i * 6)
                        split_hi(R_CONV + u + 1, i, 6, w_hi[(u + 1) % 2][:, :])
                        if m == 0:
                            act.wait_ge(cv_p, START + j - 1 + i * 2)
                            act.wait_ge(pe_done, START + P_CONV + u + 1 + i * 6)
                            act.activation(cx[j][:, :], pair(CONV_PAIR[u]), ACT.Copy).then_inc(cv_x, 1)
                        if m == 1:
                            act.wait_ge(cv_p, START + j + 1 + i * 2)
                            act.wait_ge(cv_s, START + j - 1 + i * 2)
                            act.activation(cy[j][:, :], cprod[j][:, :], ACT.Identity,
                                           scale=vec[:, bass.ds(i * 2 + (V_CW + 8 + j), 1)],
                                           bias=vec[:, bass.ds(i * 2 + (V_CB + j), 1)]).then_inc(cv_b, 1)
                        if m == 2:
                            act.wait_ge(cv_s, START + j + 1 + i * 2)
                            act.activation(x1_hi[:, bass.ds(i * 2 + j, 1), :].rearrange("p k t -> p (k t)"), co[j][:, :],
                                           ACT.Copy).then_inc(cv_hi, 1)

            def gate_out(u, bank):
                act.activation(gate_o[u][:, :], pair(bank), ACT.Sigmoid).then_inc(gate_ev, 1)

            with act.Fori(0, 4) as i:
                for u in range(4):
                    act.wait_ge(pe_done, START + P_GATE + u + i * 4)
                    split_hi(R_GATE + u + 1, i, 4, w_hi[(u + 1) % 2][:, :])
                    if u % 2 == 0:
                        act.wait_ge(mc_ok, START + u // 2 - 1 + i * 2)
                        act.wait_ge(pe_done, START + P_GATE + u + 1 + i * 4)
                        gate_out(u // 2, u)

            def gates(i, last):
                for u in range(2):
                    act.wait_ge(pe_done, START + P_GB + u + i * 2)
                    if not (last and u == 1):
                        split_hi(R_GB + u + 1, i, 2, w_hi[(u + 1) % 2][:, :])
                    act.wait_ge(mc_ok, START + KT)
                    act.wait_ge(gate_st, START + u - 1 + i * 2)
                    act.wait_ge(pe_done, START + P_GB + u + 1 + i * 2)
                    gate_out(u, 1 + 2 * u)

            with act.Fori(0, 3) as i:
                gates(i, False)
            gates(3, True)

            def scale_context(h):
                act.wait_ge(ret_in[h % 2], 80 * (h // 2 + 1))
                act.wait_ge(dve0, 13)
                act.wait_ge(u_ok, START + N_U * (h - 1) + 4)
                for dst, col in ((kcw_b, H_B), (kcw_f, H_F)):
                    for m in range(NCX):
                        act.activation(dst[:, m, :], kc_n[h % 2][:, m, :], ACT.Copy,
                                       scale=head_tab[:, h, col + 1 + m:col + 2 + m]).then_inc(kcw_ok, 1)

            def scale_k(h, m):
                c = NCH - 1 - m
                act.wait_ge(kt_ok, START + NCH * h + m + 1)
                act.wait_ge(u_ok, START + N_U * h + (2 * m + 2 if m > 1 else 0))
                if c > 0:
                    act.activation(kz_b[:, m % 2, :], ps[:, m % 2, 0:DK], ACT.Copy,
                                   scale=head_tab[:, h, H_B:H_B + 1]).then_inc(kz_ok, 1)
                if c < NCH - 1:
                    act.activation(kz_f[:, c, :], ps[:, m % 2, 0:DK], ACT.Copy,
                                   scale=head_tab[:, h, H_F:H_F + 1]).then_inc(kz_ok, 1)

            scale_context(0)
            for i in range(HEADS // 2):
                for p in range(2):
                    for m in range(2 if 2 * i + p > 0 else 0, NCH):
                        scale_k(2 * i + p, m)
                    def gated_out(c):
                        act.wait_ge(go_st, START + NCH * p + c - 1 + i * 16)
                        act.wait_ge(ogt_ok, START + NCH * p + c + 1 + i * 16)
                        act.activation(og_t[c % 2][:, :, :].rearrange("p k t -> p (k t)"), ps[:, 6, :],
                                       ACT.Copy).then_inc(ogc_ok, 1)

                    for c in range(NCH):
                        n = NCH * p + c
                        act.wait_ge(o_ok, START + n + 1 + i * 16)
                        act.wait_ge(osq_ok, START + n + i * 16)
                        act.activation(sq_j[:, :], ps[:, 2 + c % 2, :], ACT.Square,
                                       accum_out=onum[:, c % 2, 0:1]).then_inc(osq_ok, 1)
                        act.wait_ge(osq_ok, START + n + 1 + i * 16)
                        act.wait_ge(oinv_ok, START + n - 1 + i * 16)
                        act.activation(onum[:, c % 2, 1:2], onum[:, c % 2, 0:1], ACT.Sqrt,
                                       bias=eps[:, :], scale=1.0 / DV).then_inc(ort_ok, 1)
                        if c > 0:
                            gated_out(c - 1)
                        if c == 5 and 2 * i + p + 1 < HEADS:
                            scale_context(2 * i + p + 1)
                        if 2 * i + p == HEADS - 1 and c == 2:
                            split_hi(R_B, 0, 0, w_hi[0][:, :])
                        if 2 * i + p == HEADS - 1 and c == NCH - 2:
                            act.wait_ge(sc_ok, START + HEADS * NCH)
                            act.wait_ge(q_ok, START + 2 * HEADS)
                            split_hi(R_B + 1, 0, 0, x0_hi[:, 0, :])
                    if 2 * i + p + 1 < HEADS:
                        scale_k(2 * i + p + 1, 0)
                        scale_k(2 * i + p + 1, 1)
                    else:
                        act.wait_ge(adb_mul, START + HEADS * NCH)
                        split_hi(R_B + 2, 0, 0, w_hi[1][:, :])
                    gated_out(NCH - 1)

            for k in range(1, KT):
                split_hi(R_B + 2 + k, 0, 0, x0_hi[:, k, :])
            act.wait_ge(pe_done, START + P_B + 1)
            split_hi(R_B + 10, 0, 0, w_hi[0][:, :])
            for j in range(2):
                split_hi(R_B + 11 + j, 0, 0, x1_hi[:, j, :])
            with act.Fori(1, 4) as i:
                for j in range(2):
                    act.wait_ge(pe_done, START + P_B + j + i * 2)
                    split_hi(R_B + 8 + 2 * j + 1, i, 4, x1_hi[:, bass.ds(i * 2 + j, 1), :].rearrange("p k t -> p (k t)"))
                    split_hi(R_B + 8 + 2 * j + 2, i, 4, w_hi[(j + 1) % 2][:, :])

            def last_stage(i, last):
                for j in range(2):
                    act.wait_ge(pe_done, START + P_C + j + i * 2)
                    if not (last and j == 1):
                        split_hi(R_C + j + 1, i, 2, w_hi[(j + 1) % 2][:, :])
                    if last and j == 1:
                        act.wait_ge(raw_in[0], 16 * ((R_WO - R_QK) // 2 + 1))
                        act.wait_ge(pe_done, START + P_UP - 1)
                        act.activation(w_hi[0][:, :], raw[0][:, :], ACT.Copy).then_inc(wo_hi, 1)
                        act.wait_ge(pe_done, START + P_UP)
                        for k in range(2):
                            split_hi(R_WO + k, 0, 0, x1_hi[:, k, :])
                    act.wait_ge(mg_add, START + 16 + 2 * (j + 1) + i * 4)
                    act.activation(x0_hi[:, bass.ds(i * 2 + j, 1), :], merged[:, bass.ds(i * 2 + j, 1), :],
                                   ACT.Copy).then_inc(m_hi, 1)

            with act.Fori(0, 3) as i:
                last_stage(i, False)
            last_stage(3, True)
            with act.Fori(1, 4) as i:
                for j in range(2):
                    split_hi(R_WO + j, i, 2, x1_hi[:, bass.ds(i * 2 + j, 1), :].rearrange("p k t -> p (k t)"))
            act.wait_ge(row_mm, 1)
            split_hi(R_UP, 0, 0, w_hi[0][:, :])
            split_hi(R_UP + 1, 0, 0, w_hi[1][:, :])

            act.wait_ge(row_mm, 1)
            act.activation(gain_row[:, :], pair(2), ACT.Copy).then_inc(row_ok, 1)
            for c in range(NCH + 1):
                if c < NCH:
                    act.wait_ge(y_done, START + c + 1)
                    act.wait_ge(y_sq, START + 2 * c)
                    act.activation(junk2[:, :], pair(Y_PAIR[c]), ACT.Square, accum_out=st1[:, c, 0:1]).then_inc(y_sq, 1)
                    act.wait_ge(y_sq, START + 2 * c + 1)
                    act.activation(st1[:, c, 1:2], st1[:, c, 0:1], ACT.Sqrt, bias=eps[:, :], scale=1.0 / D).then_inc(y_act, 1)
                    act.wait_ge(y_x1, START + c + 1)
                    act.wait_ge(y_sq, START + 2 * c + 1)
                    act.activation(junk2[:, :], x1n[c % 2][:, :], ACT.Square, accum_out=st2[:, c, 0:1]).then_inc(y_sq, 1)
                    act.wait_ge(y_sq, START + 2 * c + 2)
                    act.activation(st2[:, c, 1:2], st2[:, c, 0:1], ACT.Sqrt, bias=eps[:, :], scale=1.0 / D).then_inc(y_act, 1)
                if c < NCH:
                    act.wait_ge(y_dve, START + Y_COUNT["inv2", c])
                    act.activation(hn[c % 2][:, :], x1n[c % 2][:, :], ACT.Copy, scale=st2[:, c, 2:3]).then_inc(y_hn, 1)

                if c > 0:
                    act.wait_ge(y_dve, START + Y_COUNT["shift", c - 1])
                    act.activation(x0_hi[:, :, (c - 1) * P:c * P], haff[:, :].rearrange("p (k t) -> p k t", t=P),
                                   ACT.Copy).then_inc(y_hi, 1)
            act.wait_ge(row_mm, 2)
            act.wait_ge(y_dve, START + Y_COUNT["z", NCH - 1])
            act.activation(gain_row[:, :], pair(3), ACT.Copy).then_inc(row_ok, 1)

            def up(i, first, last):
                for j in range(2):
                    for m in range(2):
                        u = 2 * j + m
                        act.wait_ge(pe_done, START + P_UP + u + i * 4)
                        if not (last and u == 3 or first and u == 0):
                            split_hi(R_UP + u + 1, i, 4, w_hi[(u + 1) % 2][:, :])
                        act.wait_ge(up_a, START + j - 1 + i * 2)
                        act.wait_ge(pe_done, START + P_UP + u + 1 + i * 4)
                        tile = FT * m + j
                        act.activation(uy[j][m][:, :], pair(u), ACT.Identity,
                                       scale=vec[:, bass.ds(i * 6 + (V_FW + 3 * tile + 1), 1)],
                                       bias=vec[:, bass.ds(i * 2 + (V_FB + tile), 1)]).then_inc(up_b, 1)
                    act.wait_ge(up_c, START + 4 * j + 2 + i * 8)
                    act.activation(uy[j][0][:, :], uy[j][0][:, :], ACT.Silu).then_inc(up_s, 1)


            def down_hi(n, i, u):
                act.wait_ge(dn_in[u], 32 * (n // 2 + 1) + i * 32)
                act.activation(a_hi[u][:, :], a_raw[u][:, :], ACT.Copy).then_inc(dn_hi, 1)
                act.activation(d_hi[u][:, :], d_raw[u][:, :], ACT.Copy).then_inc(dn_hi, 1)

            def down(half, i, last):
                for u in range(2):
                    act.wait_ge(dn_pe, START + N_DOWN * half + u + i * 2)
                    if not (last and half == 1 and u == 1):
                        down_hi(FT * half + u + 1, i, (u + 1) % 2)

            up(0, True, False)
            with act.Fori(1, FT // 2 - 1) as i:
                up(i, False, False)
            down_hi(0, 0, 0)
            up(FT // 2 - 1, False, True)

            def first_half(c):
                act.wait_ge(f_row, c + 1)
                act.activation(fo[c][:, 0:HALF], f0[:, c, :], ACT.Copy, scale=fsum[:, c, 4:5]).then_inc(dn_half, 1)

            for half in range(2):
                with act.Fori(0, FT // 2 - 1) as i:
                    down(half, i, False)
                down(half, FT // 2 - 1, True)
                for c in range(NCH):
                    act.wait_ge(dn_pe, START + N_DOWN * half + FT + c)
                    act.wait_ge(dn_sq, START + NCH * half + c)
                    act.activation(junk3[:, :], ps[:, c, :], ACT.Square, accum_out=fsum[:, c, half:half + 1]).then_inc(dn_sq, 1)
                    if half == 1:
                        act.wait_ge(dn_add, START + c + 1)
                        act.activation(fsum[:, c, 3:4], fsum[:, c, 2:3], ACT.Sqrt, bias=eps[:, :], scale=1.0 / D).then_inc(dn_rt, 1)
                        if c > 0:
                            first_half(c - 1)
            first_half(NCH - 1)

        @block.vector
        def _(dve):
            for s in (lo_done, z_ok, h_lo, rot_mul, rot_add, cv_p, cv_y, cv_s, cv_lo, mc_ok, st_ok, ms_ok, oinv_ok, og_ok, adb_mul,
                      mg_mul, mg_add, m_lo, y_dve, y_x1, y_lo, up_c, up_a, dn_lo, dn_ev, dn_add, dn_dve):
                dve.sem_inc(s, START)

            def split_lo(base, i, per, dst, hi):
                dve.wait_ge(hi_done, START + base + 1 + i * per)
                dve.tensor_tensor(dst, raw[base % 2][:, :], hi.bitcast(F32), ALU.subtract).then_inc(lo_done, 1)

            def context_lo(r, i):
                dve.wait_ge(hi_done, START + R_CTX + r + 1 + i * 8)
                dve.tensor_tensor(w_lo[r % 2][:, :], raw_c[r % 4][:, :], w_hi[r % 2][:, :].bitcast(F32),
                                  ALU.subtract).then_inc(lo_done, 1)

            def ring_lo(base, i, per):
                split_lo(base, i, per, w_lo[base % 2][:, :], w_hi[base % 2][:, :])

            def flat(t, i, j):
                return t[:, bass.ds(i * 2 + j, 1), :].rearrange("p k t -> p (k t)")

            def by_tile(v):
                return v.unsqueeze(2).broadcast_to([P, KT, P])

            dve.wait_ge(csq_ok, 1)
            for n, k in enumerate((4, 2, 1)):
                if n > 0:
                    dve.wait_ge(csum_ok, n)
                dve.tensor_tensor(ctx_h[:, 0:k, :], ctx_h[:, 0:k, :], ctx_h[:, k:2 * k, :], ALU.add).then_inc(csum_ok, 1)
            z = vec[:, V_DEC:V_DEC + 8]
            dve.tensor_scalar(dec[:, DC_T, :], z, -1.0, None, ALU.mult).then_inc(dve0, 1)
            dve.wait_ge(dve0, 1)
            dve.tensor_tensor(dec[:, DC_AZ, :], z, dec[:, DC_T, :], ALU.max).then_inc(dve0, 1)
            dve.wait_ge(act0, 1)
            dve.tensor_scalar(dec[:, DC_W, :], dec[:, DC_U, :], 1.0, None, ALU.add).then_inc(dve0, 1)
            dve.wait_ge(dve0, 3)
            dve.scalar_tensor_tensor(dec[:, DC_CORR, :], dec[:, DC_W, :], 1.0, dec[:, DC_U, :],
                                     ALU.subtract, ALU.subtract).then_inc(dve0, 1)
            dve.reciprocal(dec[:, DC_RW, :], dec[:, DC_W, :]).then_inc(dve0, 1)
            dve.wait_ge(dve0, 5)
            dve.tensor_tensor(dec[:, DC_CORR, :], dec[:, DC_CORR, :], dec[:, DC_RW, :], ALU.mult).then_inc(dve0, 1)
            dve.wait_ge(dve0, 6)
            dve.wait_ge(act0, 2)
            dve.tensor_tensor(dec[:, DC_LN, :], dec[:, DC_LN, :], dec[:, DC_CORR, :], ALU.subtract).then_inc(dve0, 1)
            dve.wait_ge(dve0, 7)
            dve.scalar_tensor_tensor(dec[:, DC_LG, :], z, 0.0, dec[:, DC_LN, :], ALU.min, ALU.subtract).then_inc(dve0, 1)
            dve.wait_ge(root_ok, 1)
            dve.reciprocal(inv_c[:, :], inv_c[:, :]).then_inc(inv_ok, 1)
            dve.wait_ge(inv_ok, 1)
            dve.tensor_tensor(ctx_in[:, :, :], ctx_in[:, :, :], inv_c[:, :].unsqueeze(1).broadcast_to([P, KT, CTX]),
                              ALU.mult).then_inc(z_ok, 1)
            context_lo(0, 0)
            context_lo(1, 0)
            dve.wait_ge(act0, 2 + 6 * HEADS)
            mask = head_tab[:, :, H_D:H_D + P]
            dve.tensor_tensor(mask, mask, const[:, C_GE:C_GE + P].unsqueeze(1).broadcast_to([P, HEADS, P]),
                              ALU.mult).then_inc(dve0, 1)
            dve.tensor_tensor(dtmp[:, :, :], dtmp[:, :, :], const[:, C_LT:C_LT + P].unsqueeze(1).broadcast_to([P, HEADS, P]),
                              ALU.mult).then_inc(dve0, 1)
            for col in (H_F, H_B):
                dve.tensor_scalar(head_tab[:, :, col:col + 3], head_tab[:, :, col:col + 3], K_SCALE, None,
                                  ALU.mult).then_inc(dve0, 1)
            dve.wait_ge(dve0, 12)
            dve.tensor_tensor(mask, mask, dtmp[:, :, :], ALU.add).then_inc(dve0, 1)
            for b in (2, 3):
                dve.wait_ge(row_sum, b + 1)
                dve.tensor_copy(mod_row[:, b, :], ps[0:2, b, :]).then_inc(row_dve, 1)
            dve.wait_ge(ada_done, 1)
            dve.tensor_tensor(mod_a[:, :, :], ps[:, 7, 0:32].rearrange("p (t v) -> p t v", v=2),
                              vec[:, V_BADA:V_BADA + 16].unsqueeze(2).broadcast_to([P, 16, 2]), ALU.add).then_inc(mod_ok, 1)
            dve.wait_ge(mod_ok, 1)
            dve.scalar_tensor_tensor(scale_x[:, :, :], mod_a[:, KT:16, :], 1.0,
                                     vec[:, V_GMIX:V_GMIX + KT].unsqueeze(2).broadcast_to([P, KT, 2]),
                                     ALU.add, ALU.mult).then_inc(mod_ok, 1)
            dve.wait_ge(mod_ok, 2)
            dve.wait_ge(z_ok, START + 1)
            dve.wait_ge(sum_mm, 1)
            dve.tensor_tensor(ctx_h[:, 4:8, :], ctx_in[:, 4:8, :], scale_x[:, 4:8, 1:2].broadcast_to([P, 4, CTX]),
                              ALU.mult).then_inc(cb_ok, 1)

            def context_low(n, tiles):
                dve.wait_ge(hc_hi_ok, n)
                dve.tensor_tensor(hc_lo[:, tiles, :], ctx_h[:, tiles, :], hc_hi[:, tiles, :].bitcast(F32),
                                  ALU.subtract).then_inc(hc_lo_ok, 1)

            context_low(1, slice(0, 2))
            dve.wait_ge(cb_ok, 1)
            dve.tensor_tensor(ctx_h[:, 4:8, :], ctx_h[:, 4:8, :], mod_a[:, 4:8, 1:2].broadcast_to([P, 4, CTX]),
                              ALU.add).then_inc(cb_ok, 1)
            context_low(2, slice(2, 4))
            dve.wait_ge(cb_ok, 2)
            context_low(3, slice(4, 8))

            for r in range(1, 7):
                context_lo(r + 1, 0)
            dve.wait_ge(root_ok, 2)
            dve.reciprocal(rinv[:, :], root[:, :]).then_inc(inv_ok, 1)
            dve.wait_ge(inv_ok, 2)
            dve.tensor_tensor(diag_x[:, :, :], ident[:, :].unsqueeze(1).broadcast_to([P, NCH, P]), by_tile(rinv[:, :]),
                              ALU.mult).then_inc(inv_ok, 1)
            context_lo(8, 0)
            dve.wait_ge(inv_mm, 1)

            def normed(k):
                dve.tensor_tensor(x_in[:, k, :], x_in[:, k, :], pair(2), ALU.mult).then_inc(z_ok, 1)

            def h_low(k):
                dve.wait_ge(h_hi, START + k + 1)
                dve.tensor_tensor(x0_lo[:, k, :], aff[k % 2][:, :], x0_hi[:, k, :].bitcast(F32), ALU.subtract).then_inc(h_lo, 1)

            normed(0)
            for i in (1, 2):
                for r in range(8):
                    k = 4 * i + r // 2 - 4
                    final = k == KT - 1 and r % 2 == 1
                    if not final:
                        context_lo(r + 1, i)
                    if r % 2 == 0 and k > 0:
                        h_low(k - 1)
                    if r % 2 == 1 and k + 1 < KT:
                        normed(k + 1)
            h_low(KT - 1)
            ring_lo(R_QK, 0, 0)

            dve.wait_ge(trig_in, 32)
            with dve.Fori(0, 4) as i:
                for d in range(2):
                    for m in range(2):
                        u = 2 * d + m
                        ring_lo(R_QK + u + 1, i, 4)
                        dve.wait_ge(pe_done, START + P_QK + u + 1 + i * 4)
                        dve.tensor_tensor(rot_a[d][:, m, :], pair(u), cos[:, :], ALU.mult).then_inc(rot_mul, 1)
                        dve.tensor_tensor(rot_b[d][:, 1 - m, :], pair(u), sin[:, :], ALU.mult).then_inc(rot_mul, 1)
                    dve.wait_ge(rot_mul, START + 4 * (d + 1) + i * 8)
                    dve.wait_ge(qk_st, START + d - 1 + i * 2)
                    dve.tensor_tensor(rot_o[d][:, 0, :], rot_a[d][:, 0, :], rot_b[d][:, 0, :], ALU.subtract).then_inc(rot_add, 1)
                    dve.tensor_tensor(rot_o[d][:, 1, :], rot_a[d][:, 1, :], rot_b[d][:, 1, :], ALU.add).then_inc(rot_add, 1)

            with dve.Fori(0, 8) as b:
                for u in range(4):
                    ring_lo(R_VG + u + 1, b, 4)

            with dve.Fori(0, 4) as i:
                for j in range(2):
                    rows_p = cprod[j][:, :].rearrange("p (r t) -> p r t", t=GRID)
                    rows_y = cy[j][:, :].rearrange("p (r t) -> p r t", t=GRID)
                    for m in range(3):
                        u = 3 * j + m
                        ring_lo(R_CONV + u + 1, i, 6)
                        if m == 1:
                            dve.wait_ge(pe_done, START + P_CONV + u + 1 + i * 6)
                            dve.wait_ge(cv_x, START + j + 1 + i * 2)
                            dve.tensor_tensor(cprod[j][:, :], pair(CONV_PAIR[u]), cx[j][:, :], ALU.mult).then_inc(cv_p, 1)
                            dve.wait_ge(cv_b, START + j + 1 + i * 2)
                            dve.scalar_tensor_tensor(rows_y[:, :, 1:GRID], rows_p[:, :, 0:GRID - 1],
                                                     vec[:, bass.ds(i * 2 + (V_CW + j), 1)], rows_y[:, :, 1:GRID],
                                                     ALU.mult, ALU.add).then_inc(cv_y, 1)
                            dve.wait_ge(cv_y, START + 2 * j + 1 + i * 4)
                            dve.scalar_tensor_tensor(rows_y[:, :, 0:GRID - 1], rows_p[:, :, 1:GRID],
                                                     vec[:, bass.ds(i * 2 + (V_CW + 2 * KT + j), 1)], rows_y[:, :, 0:GRID - 1],
                                                     ALU.mult, ALU.add).then_inc(cv_y, 1)
                        if m == 2:
                            dve.wait_ge(cv_y, START + 2 * j + 2 + i * 4)
                            dve.wait_ge(vg_st, START + 64)
                            dve.wait_ge(cv_hi, START + j - 1 + i * 2)
                            dve.wait_ge(pe_done, START + P_CONV + u + 1 + i * 6)
                            dve.tensor_tensor(co[j][:, :], cy[j][:, :], pair(CONV_PAIR[u]), ALU.mult).then_inc(cv_s, 1)
                            dve.wait_ge(cv_hi, START + j + 1 + i * 2)
                            dve.tensor_tensor(flat(x1_lo, i, j), co[j][:, :], flat(x1_hi, i, j).bitcast(F32),
                                              ALU.subtract).then_inc(cv_lo, 1)

            with dve.Fori(0, 4) as i:
                for u in range(4):
                    ring_lo(R_GATE + u + 1, i, 4)
                    if u % 2 == 1:
                        j = u // 2
                        dve.wait_ge(gate_ev, START + j + 1 + i * 2)
                        dve.wait_ge(mc_st, START + j - 1 + i * 2)
                        dve.wait_ge(pe_done, START + P_GATE + u + 1 + i * 4)
                        dve.tensor_tensor(mc_out[j][:, :], pair(u), gate_o[j][:, :], ALU.mult).then_inc(mc_ok, 1)
            with dve.Fori(0, 3) as i:
                for u in range(2):
                    ring_lo(R_GB + u + 1, i, 2)
            ring_lo(R_GB + 7, 0, 0)

            for i in range(HEADS // 2):
                for p in range(2):
                    u0 = N_U * p

                    def state(n, dst, old, decay):
                        dve.wait_ge(u_ok, START + u0 + n + 1 + i * 2 * N_U)
                        if old is None:
                            dve.tensor_copy(dst, ps[:, 4 + n % 2, :]).then_inc(st_ok, 1)
                        else:
                            dve.wait_ge(st_ok, START + u0 + n - 1 + i * 2 * N_U)
                            dve.scalar_tensor_tensor(dst, old, decay, ps[:, 4 + n % 2, :], ALU.mult, ALU.add).then_inc(st_ok, 1)

                    dve.wait_ge(o_ok, START + NCH * p + i * 16)
                    for t in range(2):
                        state(t, s_bw[:, 0, t, :], None, None)
                    for t in range(2):
                        state(2 + t, s_fw[:, 0, t, :], None, None)
                    for m in range(NCH - 1):
                        c = NCH - 1 - m
                        if p == 0 and m == 4:
                            dve.wait_ge(gate_st, START + KT)
                        for t in range(2):
                            state(4 + 2 * m + t, s_bw[:, m + 1, t, :], s_bw[:, m, t, :], head_tab[:, 2 * i + p, H_B + 3:H_B + 4])

                    def mask_scores(c):
                        n = NCH * p + c
                        dve.wait_ge(o_ok, START + n - 1 + i * 16)
                        dve.wait_ge(sc_ok, START + n + 1 + i * 16)
                        dve.tensor_tensor(s_sc[:, c % 2, :], ps[:, c % 2, 0:P], head_tab[:, 2 * i + p, H_D:H_D + P], ALU.mult).then_inc(ms_ok, 1)

                    def forward(c, t):
                        if t == 0:
                            dve.wait_ge(o_ok, START + NCH * p + c + i * 16)
                        state(18 + 2 * c + t, s_fw[:, (c + 1) % 2, t, :], s_fw[:, c % 2, t, :], head_tab[:, 2 * i + p, H_F + 3:H_F + 4])

                    mask_scores(0)
                    for c in range(NCH):
                        n = NCH * p + c
                        if c + 1 < NCH:
                            mask_scores(c + 1)
                            forward(c, 0)
                        dve.wait_ge(ort_ok, START + n + 1 + i * 16)
                        dve.reciprocal(onum[:, c % 2, 2:3], onum[:, c % 2, 1:2]).then_inc(oinv_ok, 1)
                        if c + 1 < NCH:
                            forward(c, 1)
                        dve.wait_ge(adb_in[c % 2], 16 * (NCH // 2 * p + c // 2 + 1) + i * 128)
                        dve.wait_ge(adb_mul, START + n + i * 16)
                        if c == 0:
                            dve.wait_ge(adb_done, START + p + i * 2)
                            dve.tensor_scalar(ada_acc[:, :], ada_ret[0][:, :], silu_c[:, 0, 0:1], None, ALU.mult).then_inc(adb_mul, 1)
                        else:
                            dve.scalar_tensor_tensor(ada_acc[:, :], ada_ret[c % 2][:, :], silu_c[:, c, 0:1], ada_acc[:, :],
                                                     ALU.mult, ALU.add).then_inc(adb_mul, 1)
                        dve.wait_ge(oinv_ok, START + n + 1 + i * 16)
                        dve.wait_ge(g_ld[c % 2], 16 * (NCH // 2 * p + c // 2 + 1) + i * 128)
                        dve.wait_ge(ogt_ok, START + n - 1 + i * 16)
                        dve.scalar_tensor_tensor(og[c % 2][:, :], ps[:, 2 + c % 2, :], onum[:, c % 2, 2:3], g_in[c % 2][:, :],
                                                 ALU.mult, ALU.mult).then_inc(og_ok, 1)
                        if 2 * i + p == HEADS - 1 and c == 3:
                            ring_lo(R_B, 0, 0)
                        if 2 * i + p == HEADS - 1 and c == NCH - 2:
                            split_lo(R_B + 1, 0, 0, x0_lo[:, 0, :], x0_hi[:, 0, :])
            split_lo(R_B + 2, 0, 0, w_lo[1][:, :], w_hi[1][:, :])
            dve.wait_ge(adb_done, START + HEADS)
            dve.tensor_tensor(mod_b[:, :], ps[:, 7, 0:32], vec[:, V_BADA + 16:V_BADA + 48], ALU.add).then_inc(mod_ok, 1)
            dve.wait_ge(mod_ok, 3)
            dve.scalar_tensor_tensor(scale_h[:, :], mod_b[:, 16:24], 1.0, vec[:, V_GFFN:V_GFFN + KT], ALU.add, ALU.mult).then_inc(mod_ok, 1)
            dve.tensor_tensor(gain_y[:, :], mod_b[:, 0:8], vec[:, V_GPOST:V_GPOST + KT], ALU.mult).then_inc(mod_ok, 1)
            dve.tensor_tensor(gain_f[:, :], mod_b[:, 24:32], vec[:, V_GFPOST:V_GFPOST + KT], ALU.mult).then_inc(mod_ok, 1)

            for k in range(1, KT):
                split_lo(R_B + 2 + k, 0, 0, x0_lo[:, k, :], x0_hi[:, k, :])

            def merge(stage, count, i, j, first=False):
                dve.wait_ge(gt_in[j], 32 + i * 32 if stage == 0 else 16 * 9 + i * 16)
                dve.wait_ge(pe_done, START + count + j + 1 + i * 2)
                for n in range(2):
                    cols = slice(n * HALF, (n + 1) * HALF)
                    out = merged[:, bass.ds(i * 2 + j, 1), cols].rearrange("p k t -> p (k t)")
                    made = START + 16 * stage + 2 * j + n + 1
                    dve.wait_ge(mg_add, made - 1 + i * 4)
                    bank = 2 * j + n + (0 if first else 4)
                    dve.tensor_tensor(mtmp[:, :], ps[:, bank, :], gate_in[j][:, cols], ALU.mult).then_inc(mg_mul, 1)
                    dve.wait_ge(mg_mul, made + i * 4)
                    dve.tensor_tensor(out, out, mtmp[:, :], ALU.add).then_inc(mg_add, 1)

            ring_lo(R_B + 10, 0, 0)
            merge(0, P_B, 0, 0, True)
            for j in range(2):
                split_lo(R_B + 11 + j, 0, 0, x1_lo[:, j, :], x1_hi[:, j, :])
            merge(0, P_B, 0, 1, True)
            with dve.Fori(1, 4) as i:
                for j in range(2):
                    split_lo(R_B + 8 + 2 * j + 1, i, 4, flat(x1_lo, i, j), flat(x1_hi, i, j))
                    split_lo(R_B + 8 + 2 * j + 2, i, 4, w_lo[(j + 1) % 2][:, :], w_hi[(j + 1) % 2][:, :])
                    merge(0, P_B, i, j)

            def last_stage(i, last):
                for j in range(2):
                    if not (last and j == 1):
                        ring_lo(R_C + j + 1, i, 2)
                    if last and j == 1:
                        dve.wait_ge(wo_hi, 1)
                        dve.tensor_tensor(w_lo[0][:, :], raw[0][:, :], w_hi[0][:, :].bitcast(F32), ALU.subtract).then_inc(wo_lo, 1)
                        for k in range(2):
                            split_lo(R_WO + k, 0, 0, x1_lo[:, k, :], x1_hi[:, k, :])
                    merge(1, P_C, i, j)
                    dve.wait_ge(m_hi, START + j + 1 + i * 2)
                    dve.tensor_tensor(flat(x0_lo, i, j), flat(merged, i, j), flat(x0_hi, i, j).bitcast(F32),
                                      ALU.subtract).then_inc(m_lo, 1)

            with dve.Fori(0, 3) as i:
                last_stage(i, False)
            last_stage(3, True)
            with dve.Fori(1, 3) as i:
                for j in range(2):
                    split_lo(R_WO + j, i, 2, flat(x1_lo, i, j), flat(x1_hi, i, j))
            dve.wait_ge(mod_ok, 6)
            dve.wait_ge(m_lo, START + KT)
            dve.tensor_tensor(diag[:, :, :], ident[:, :].unsqueeze(1).broadcast_to([P, KT, P]), by_tile(gain_y[:, :]),
                              ALU.mult).then_inc(dg_ok, 1)
            for k in (6, 7):
                split_lo(R_WO + k, 0, 0, x1_lo[:, k, :], x1_hi[:, k, :])
            ring_lo(R_UP, 0, 0)
            ring_lo(R_UP + 1, 0, 0)

            dve.wait_ge(row_ok, 1)
            dve.tensor_tensor(diag[:, :, :], ident[:, :].unsqueeze(1).broadcast_to([P, KT, P]), by_tile(gain_f[:, :]),
                              ALU.mult).then_inc(dg_ok, 1)
            tile = haff[:, :].rearrange("p (k t) -> p k t", t=P)
            for c in range(NCH + 1):
                if c < NCH:
                    dve.wait_ge(y_act, START + 2 * c + 1)
                    dve.reciprocal(st1[:, c, 2:3], st1[:, c, 1:2]).then_inc(y_dve, 1)
                    dve.wait_ge(y_dve, START + Y_COUNT["inv1", c])
                    dve.wait_ge(y_hn, START + c - 1)
                    dve.wait_ge(y_t, START + c - 1)
                    dve.scalar_tensor_tensor(hn[c % 2][:, :], pair(Y_PAIR[c]), st1[:, c, 2:3], gain_row[:, :],
                                             ALU.mult, ALU.mult).then_inc(y_dve, 1)
                    dve.wait_ge(y_dve, START + Y_COUNT["z", c])
                    dve.wait_ge(xr_in[c % 2], 16 * (c // 2 + 1))
                    dve.wait_ge(x1_st, START + c - 1)
                    dve.tensor_tensor(x1n[c % 2][:, :], hn[c % 2][:, :], xr[c % 2][:, :], ALU.add).then_inc(y_x1, 1)
                    dve.wait_ge(y_act, START + 2 * c + 2)
                    dve.reciprocal(st2[:, c, 2:3], st2[:, c, 1:2]).then_inc(y_dve, 1)
                if c > 0:
                    dve.wait_ge(y_t, START + c)
                    dve.wait_ge(y_lo, START + c - 1)
                    dve.tensor_tensor(tile, pair(T_PAIR[c - 1]).rearrange("p (k t) -> p k t", t=P), by_tile(scale_h[:, :]),
                                      ALU.mult).then_inc(y_dve, 1)
                    dve.wait_ge(y_dve, START + Y_COUNT["scale", c - 1])
                    dve.tensor_tensor(tile, tile, by_tile(mod_b[:, 8:16]), ALU.add).then_inc(y_dve, 1)
                if c > 0:
                    dve.wait_ge(y_hi, START + c)
                    cols = slice((c - 1) * P, c * P)
                    dve.tensor_tensor(x0_lo[:, :, cols], tile, x0_hi[:, :, cols].bitcast(F32), ALU.subtract).then_inc(y_lo, 1)

            def up(i, first, last):
                for j in range(2):
                    for m in range(2):
                        u = 2 * j + m
                        tile = FT * m + j
                        if not (last and u == 3 or first and u == 0):
                            ring_lo(R_UP + u + 1, i, 4)
                        dve.wait_ge(up_b, START + u + 1 + i * 4)
                        y = uy[j][m]
                        dve.scalar_tensor_tensor(y[:, GRID:T], pair(u)[:, 0:T - GRID],
                                                 vec[:, bass.ds(i * 6 + (V_FW + 3 * tile), 1)], y[:, GRID:T],
                                                 ALU.mult, ALU.add).then_inc(up_c, 1)
                        dve.wait_ge(up_c, START + 2 * u + 1 + i * 8)
                        dve.scalar_tensor_tensor(y[:, 0:T - GRID], pair(u)[:, GRID:T],
                                                 vec[:, bass.ds(i * 6 + (V_FW + 3 * tile + 2), 1)], y[:, 0:T - GRID],
                                                 ALU.mult, ALU.add).then_inc(up_c, 1)
                    dve.wait_ge(up_s, START + j + 1 + i * 2)
                    dve.wait_ge(up_c, START + 4 * (j + 1) + i * 8)
                    dve.wait_ge(a_st, START + j - 1 + i * 2)
                    dve.tensor_tensor(ua[j][:, :], uy[j][0][:, :], uy[j][1][:, :], ALU.mult).then_inc(up_a, 1)

            def down_lo(n, i, u):
                dve.wait_ge(dn_hi, START + 2 * (n + 1) + i * 4)
                dve.tensor_tensor(a_lo[u][:, :], a_raw[u][:, :], a_hi[u][:, :].bitcast(F32), ALU.subtract).then_inc(dn_lo, 1)
                dve.tensor_tensor(d_lo[u][:, :], d_raw[u][:, :], d_hi[u][:, :].bitcast(F32), ALU.subtract).then_inc(dn_lo, 1)

            def down(half, i, last):
                for u in range(2):
                    if not (last and half == 1 and u == 1):
                        down_lo(FT * half + u + 1, i, (u + 1) % 2)

            up(0, True, False)
            with dve.Fori(1, FT // 2 - 1) as i:
                up(i, False, False)
            down_lo(0, 0, 0)
            up(FT // 2 - 1, False, True)

            for half in range(2):
                with dve.Fori(0, FT // 2 - 1) as i:
                    down(half, i, False)
                down(half, FT // 2 - 1, True)
                if half == 0:
                    dve.wait_ge(row_ok, 2)
                    for c in range(NCH):
                        dve.wait_ge(dn_sq, START + c + 1)
                        dve.tensor_tensor(f0[:, c, :], ps[:, c, :], gain_row[:, 0:HALF], ALU.mult).then_inc(dn_ev, 1)
            for n in range(2):
                dve.wait_ge(x1_in[n], 16 * NCH // 2)
            for c in range(NCH):
                out = fo[c][:, HALF:D]
                dve.wait_ge(dn_sq, START + NCH + c + 1)
                dve.tensor_tensor(fsum[:, c, 2:3], fsum[:, c, 0:1], fsum[:, c, 1:2], ALU.add).then_inc(dn_add, 1)
                dve.tensor_tensor(out, ps[:, c, :], gain_row[:, HALF:D], ALU.mult).then_inc(dn_dve, 1)
                dve.wait_ge(dn_rt, START + c + 1)
                dve.reciprocal(fsum[:, c, 4:5], fsum[:, c, 3:4]).then_inc(f_row, 1)
                dve.wait_ge(f_row, c + 1)
                dve.wait_ge(dn_dve, START + 2 * c + 1)
                dve.scalar_tensor_tensor(out, out, fsum[:, c, 4:5], x1all[:, c, HALF:D], ALU.mult, ALU.add).then_inc(dn_dve, 1)

        @block.tensor
        def _(pe):
            for s in (pe_done, kt_ok, u_ok, sc_ok, o_ok, ogt_ok, adb_done, y_done, y_t, dn_pe):
                pe.sem_inc(s, START)

            def product(out, a, b, first, last):
                (ah, al), (bh, bl) = a, b
                pe.matmul(out, ah, bh, start=first, stop=False)
                pe.matmul(out, ah, bl, start=False, stop=False)
                return pe.matmul(out, al, bh, start=False, stop=last)

            def by_width(slot, x, out):
                for n in range(2):
                    done = by_width_half(slot, x, out, n)
                return done

            def by_width_half(slot, x, out, n):
                for k in range(KT):
                    w = tuple(t[slot][:, k * P:(k + 1) * P] for t in (w_hi, w_lo))
                    xs = tuple(t[:, k, n * HALF:(n + 1) * HALF] for t in x)
                    done = product(out[:, n * HALF:(n + 1) * HALF], w, xs, k == 0, k == KT - 1)
                return done

            def by_tokens(slot, k, r, x, c, bank, first, last):
                xs = tuple(t[:, k, c * P:(c + 1) * P] for t in x)
                w = tuple(t[slot][:, r * HALF:(r + 1) * HALF] for t in (w_hi, w_lo))
                return product(ps[:, bank, :], xs, w, first, last)

            def transpose(out, tile):
                return pe.transpose(out, tile, ident[:, :])

            pe.wait_ge(vec_in, 16)
            pe.wait_ge(silu_ok, 1)
            pe.wait_ge(setup_ok, 2)
            for k in range(KT):
                pe.wait_ge(ada_in[k], 16)
                for b in range(4):
                    done = pe.matmul(ps[0:2, b, :], silu_c[:, k, :], ada_raw[:, k, b * HALF:(b + 1) * HALF],
                                     start=(k == 0), stop=(k == KT - 1))
                    if k == KT - 1:
                        done.then_inc(row_sum, 1)
                if k == 2:
                    pe.wait_ge(csum_ok, 3)
                    pe.matmul(ps[:, 6, 0:CTX], ones[:, :], ctx_h[:, 0, :], start=True, stop=True).then_inc(sum_mm, 1)
            pe.wait_ge(ident_in, 16)
            for n in range(16):
                if n % 4 == 0:
                    pe.wait_ge(row_act if n < 8 else row_dve, n // 4 % 2 + 1)
                done = pe.transpose(ps[:, 7, 2 * n:2 * n + 2], mod_row[:, n // 4, n % 4 * P:(n % 4 + 1) * P], ident[0:2, 0:2])
            done.then_inc(ada_done, 1)

            pe.wait_ge(hc_lo_ok, 1)

            def context_block(e, i, first):
                for u in range(4):
                    if first and e == 0 and 0 < u < 3:
                        pe.wait_ge(hc_lo_ok, u + 1)
                    if first and e == 1 and u == 2:
                        pe.wait_ge(xsum_ok, START + KT - 1)
                        pe.wait_ge(root_ok, 1)
                        for c in range(NCH):
                            done = pe.matmul(ps[:, 6, c:c + 1], x_sum[:, c * P:(c + 1) * P], ones[:, 0:1],
                                             start=True, stop=True)
                        done.then_inc(sum_mm, 1)
                    pe.wait_ge(lo_done, START + R_CTX + 4 * e + u + 1 + i * 8)
                    for r in range(2):
                        k = 2 * u + r
                        for c in range(NCX):
                            if k == 0 and not first:
                                pe.wait_ge(ctx_ev, START + 2 * (e - 2) + c + 1 + i * 4)
                            done = by_tokens(u % 2, k, r, (hc_hi, hc_lo), c, 2 * e + c, k == 0, k == KT - 1)
                            if k == KT - 1:
                                done.then_inc(pe_done, 1)
                    if u < 3:
                        done.then_inc(pe_done, 1)

            context_block(0, 0, True)
            context_block(1, 0, True)
            pe.wait_ge(inv_ok, 3)
            for n in range(2):
                done = pe.matmul(ps[:, 4 + n, :], ones[:, :], diag_x[:, 4 * n:4 * n + 4, :].rearrange("p k t -> p (k t)"),
                                 start=True, stop=True)
            done.then_inc(inv_mm, 1)
            with pe.Fori(1, 3) as i:
                for e in range(2):
                    context_block(e, i, False)

            pe.wait_ge(h_lo, START + KT)
            pe.wait_ge(root_ok, 2)
            pe.wait_ge(ctx_ev, START + 12)
            with pe.Fori(0, 4) as i:
                for u in range(4):
                    pe.wait_ge(lo_done, START + R_QK + u + 1 + i * 4)
                    pe.wait_ge(rot_mul, START + 2 * (u + 1) - 8 + i * 8)
                    by_width(u % 2, (x0_hi, x0_lo), pair(u)).then_inc(pe_done, 1)

            def vg_block(b, first):
                for u in range(4):
                    pe.wait_ge(lo_done, START + R_VG + u + 1 + b * 4)
                    for r in range(2):
                        k = 2 * u + r
                        for c in range(NCH):
                            if k == 0 and first:
                                pe.wait_ge(rot_mul, START + 26 + 2 * (c // 2))
                            elif k == 0:
                                pe.wait_ge(vg_ev, START + c - 7 + b * 8)
                            done = by_tokens(u % 2, k, r, (x0_hi, x0_lo), c, c, k == 0, k == KT - 1)
                            if k == KT - 1:
                                done.then_inc(pe_done, 1)
                    if u < 3:
                        done.then_inc(pe_done, 1)

            vg_block(0, True)
            with pe.Fori(1, 8) as b:
                vg_block(b, False)

            pe.wait_ge(vg_ev, START + 64)
            frees = ((cv_p, 0), (cv_s, 0), (cv_s, -1), (cv_x, 0), (cv_x, 1), (cv_p, 1))
            with pe.Fori(0, 4) as i:
                for u in range(6):
                    freed, n = frees[u]
                    pe.wait_ge(lo_done, START + R_CONV + u + 1 + i * 6)
                    pe.wait_ge(freed, START + n + i * 2)
                    by_width(u % 2, (x0_hi, x0_lo), pair(CONV_PAIR[u])).then_inc(pe_done, 1)

            pe.wait_ge(cv_s, START + 7)
            pe.wait_ge(cv_x, START + 8)
            with pe.Fori(0, 4) as i:
                for u in range(4):
                    pe.wait_ge(lo_done, START + R_GATE + u + 1 + i * 4)
                    if u % 2 == 0:
                        pe.wait_ge(gate_ev, START + u // 2 - 1 + i * 2)
                        if u == 2:
                            pe.wait_ge(cv_s, START + KT)
                    else:
                        pe.wait_ge(mc_ok, START + u // 2 - 1 + i * 2)
                        pe.wait_ge(cv_lo, START + KT)
                    by_width(u % 2, (x0_hi, x0_lo) if u % 2 == 0 else (x1_hi, x1_lo), pair(u)).then_inc(pe_done, 1)
            pe.wait_ge(mc_ok, START + KT)
            with pe.Fori(0, 4) as i:
                for u in range(2):
                    pe.wait_ge(lo_done, START + R_GB + u + 1 + i * 2)
                    pe.wait_ge(gate_ev, START + KT + u - 1 + i * 2)
                    by_width(u % 2, (x0_hi, x0_lo), pair(1 + 2 * u)).then_inc(pe_done, 1)

            pe.wait_ge(cv_s, START + 8)
            pe.wait_ge(gate_ev, START + 2 * KT)

            def state(h, n, terms):
                pe.wait_ge(st_ok, START + N_U * h + n - 1)
                for m, (a, b) in enumerate(terms):
                    done = pe.matmul(ps[:, 4 + n % 2, :], a, b, start=(m == 0), stop=(m == len(terms) - 1))
                done.then_inc(u_ok, 1)

            def transpose_k(h, m):
                c = NCH - 1 - m
                pe.wait_ge(kz_ok, START + N_KZ * h + (KZ_END[m - 2] if m > 1 else 0))
                if m < 2:
                    pe.wait_ge(ms_ok, START + NCH * h)
                for k in range(2):
                    done = transpose(ps[:, m % 2, k * P:(k + 1) * P], k_t[h % 2][:, k, c * P:(c + 1) * P])
                done.then_inc(kt_ok, 1)

            def head_start(h):
                pe.wait_ge(ret_in[h % 2], 80 * (h // 2 + 1))
                transpose_k(h, 0)
                transpose_k(h, 1)
                for d, kcw in enumerate((kcw_b, kcw_f)):
                    pe.wait_ge(kcw_ok, START + 4 * h + 2 * (d + 1))
                    for t in range(2):
                        state(h, 2 * d + t, [(kcw[:, m, t * P:(t + 1) * P], vc_n[h % 2][:, m, :]) for m in range(NCX)])

            def first_tiles(j, k):
                pe.wait_ge(lo_done, START + R_B + (2 + j if k == 0 else 3 + k))
                w = tuple(t[j][:, k * P:(k + 1) * P] for t in (w_hi, w_lo))
                for n in range(2):
                    xs = tuple(t[:, k, n * HALF:(n + 1) * HALF] for t in (x0_hi, x0_lo))
                    done = product(ps[:, 2 * j + n, :], w, xs, k == 0, k == KT - 1)
                if k == KT - 1:
                    done.then_inc(pe_done, 1)

            head_start(0)
            for i in range(HEADS // 2):
                for p in range(2):
                    h = 2 * i + p
                    u0 = N_U * p
                    z0 = N_KZ * p
                    for m in range(NCH - 1):
                        c = NCH - 1 - m
                        pe.wait_ge(kz_ok, START + z0 + KZ_B[m] + i * 2 * N_KZ)
                        for t in range(2):
                            state(h, 4 + 2 * m + t, [(kz_b[:, m % 2, t * P:(t + 1) * P], v_n[p][:, c, :])])
                        if m + 2 < NCH:
                            transpose_k(h, m + 2)
                    pe.wait_ge(kz_ok, START + z0 + N_KZ + i * 2 * N_KZ)

                    def scores(c):
                        pe.wait_ge(ms_ok, START + NCH * p + c - 1 + i * 16)
                        for k in range(2):
                            done = pe.matmul(ps[:, c % 2, 0:P], k_t[p][:, k, c * P:(c + 1) * P],
                                             q_t[p][:, k, c * P:(c + 1) * P], start=(k == 0), stop=(k == 1))
                        done.then_inc(sc_ok, 1)

                    def transpose_out(c):
                        n = NCH * p + c
                        pe.wait_ge(og_ok, START + n + 1 + i * 16)
                        pe.wait_ge(ogc_ok, START + n + i * 16)
                        for t in range(4):
                            done = transpose(ps[:, 6, t * P:(t + 1) * P], og[c % 2][:, t * P:(t + 1) * P])
                        done.then_inc(ogt_ok, 1)

                    scores(0)
                    pe.wait_ge(q_ok, START + 2 * (p + 1) + i * 4)
                    for c in range(NCH):
                        n = NCH * p + c
                        if c + 1 < NCH:
                            scores(c + 1)
                        pe.wait_ge(og_ok, START + n - 1 + i * 16)
                        pe.wait_ge(ms_ok, START + n + 1 + i * 16)
                        out = ps[:, 2 + c % 2, :]
                        pe.matmul(out, s_sc[:, c % 2, :], v_n[p][:, c, :], start=True, stop=False)
                        pe.wait_ge(st_ok, START + u0 + 18 + 2 * c + i * 2 * N_U)
                        for k in range(2):
                            pe.matmul(out, q_b[:, k, c * P:(c + 1) * P], s_bw[:, NCH - 1 - c, k, :], start=False, stop=False)
                        for k in range(2):
                            done = pe.matmul(out, q_f[:, k, c * P:(c + 1) * P], s_fw[:, c % 2, k, :], start=False, stop=(k == 1))
                        done.then_inc(o_ok, 1)
                        if c + 1 < NCH:
                            for t in range(2):
                                state(h, 18 + 2 * c + t, [(kz_f[:, c, t * P:(t + 1) * P], v_n[p][:, c, :])])
                        if c > 0:
                            transpose_out(c - 1)
                    if h + 1 < HEADS:
                        head_start(h + 1)
                    else:
                        pe.wait_ge(ms_ok, START + HEADS * NCH)
                        first_tiles(0, 0)
                    transpose_out(NCH - 1)
                    pe.wait_ge(adb_mul, START + NCH * (p + 1) + i * 16)
                    for k in range(KT):
                        done = pe.matmul(ps[:, 7, bass.ds(i * 16 + 8 * p + k, 1)], ada_acc[:, k * P:(k + 1) * P],
                                         ones[:, 0:1], start=True, stop=True)
                    done.then_inc(adb_done, 1)

            for k in range(KT):
                for j in range(2):
                    if k + j > 0:
                        first_tiles(j, k)
            for stage, (base, count, x, per) in enumerate(((R_B + 8, P_B, (x0_hi, x0_lo), 4), (R_C, P_C, (x1_hi, x1_lo), 2))):
                if stage == 0:
                    for j in range(2):
                        pe.wait_ge(lo_done, START + (R_B + 11 if j == 0 else base + 2 * j + 1 + per))
                        pe.wait_ge(mod_ok, 3)
                        by_width(j, x, pair(2 + j)).then_inc(pe_done, 1)
                with pe.Fori(2 - 2 * stage, 4) as i:
                    for j in range(2):
                        pe.wait_ge(lo_done, START + base + per // 2 * j + 1 + i * per)
                        pe.wait_ge(mg_mul, START + 16 * stage + 2 * j - 2 + i * 4)
                        by_width(j, x, pair(2 + j)).then_inc(pe_done, 1)

            def gain(n):
                pe.wait_ge(dg_ok, n)
                for h in range(2):
                    done = pe.matmul(pair(1 + n)[:, h * HALF:(h + 1) * HALF], ones[:, :],
                                     diag[:, 4 * h:4 * h + 4, :].rearrange("p k t -> p (k t)"), start=True, stop=True)
                done.then_inc(row_mm, 1)

            def w_o_product(c, h, k):
                xs = tuple(t[:, k, c * P:(c + 1) * P] for t in (x0_hi, x0_lo))
                w = tuple(t[:, k, h * HALF:(h + 1) * HALF] for t in (x1_hi, x1_lo))
                if k == 0 and c < 2:
                    w = tuple(t[0][:, h * HALF:(h + 1) * HALF] for t in (w_hi, w_lo))
                return product(pair(Y_PAIR[c])[:, h * HALF:(h + 1) * HALF], xs, w, k == 0, k == KT - 1)

            for k in range(KT):
                pe.wait_ge(m_lo, START + k + 1)
                if k == 0:
                    pe.wait_ge(wo_lo, 1)
                else:
                    pe.wait_ge(lo_done, START + R_WO + k + 1)
                if k == 6:
                    pe.wait_ge(mg_mul, START + 32)
                    gain(1)
                for c in range(2):
                    for h in range(2):
                        done = w_o_product(c, h, k)
                    if k == KT - 1:
                        done.then_inc(y_done, 1)

            def transpose_h(c):
                pe.wait_ge(y_hn, START + c + 1)
                if c > 0:
                    pe.wait_ge(y_dve, START + (Y_COUNT["z", 2] if c == 2 else Y_COUNT["scale", max(c - 2, 0)]))
                for k in range(KT):
                    done = transpose(pair(T_PAIR[c])[:, k * P:(k + 1) * P], hn[c % 2][:, k * P:(k + 1) * P])
                done.then_inc(y_t, 1)

            for c in range(2, NCH):
                if c > 2:
                    pe.wait_ge(y_dve, START + Y_COUNT["z", Y_FREED[c]])
                for h in range(2):
                    for k in range(KT):
                        done = w_o_product(c, h, k)
                done.then_inc(y_done, 1)
                if c == 2:
                    pe.wait_ge(row_ok, 1)
                    transpose_h(0)
                if c == 3:
                    transpose_h(1)
                if c > 2:
                    transpose_h(c - 1)

            def up_half(u, n):
                return by_width_half(u % 2, (x0_hi, x0_lo), pair(u), n)

            pe.wait_ge(y_lo, START + NCH // 2)
            for u in range(2):
                pe.wait_ge(lo_done, START + R_UP + u + 1)
                pe.wait_ge(y_dve, START + Y_COUNT["z", NCH - 2 + u])
                up_half(u, 0)
                if u == 0:
                    transpose_h(NCH - 1)
            pe.wait_ge(y_dve, START + Y_COUNT["scale", NCH - 2])
            gain(2)
            pe.wait_ge(y_lo, START + NCH)
            for u in range(2):
                up_half(u, 1).then_inc(pe_done, 1)
            pe.wait_ge(row_ok, 2)

            def up(u, i):
                pe.wait_ge(lo_done, START + R_UP + u + 1 + i * 4)
                pe.wait_ge(up_c, START + 2 * (u + 1) - 8 + i * 8)
                by_width(u % 2, (x0_hi, x0_lo), pair(u)).then_inc(pe_done, 1)

            for u in range(2, 4):
                up(u, 0)
            with pe.Fori(1, FT // 2) as i:
                for u in range(4):
                    up(u, i)

            def down(half, i, u, first, last):
                pe.wait_ge(dn_lo, START + 2 * (FT * half + u + 1) + i * 4)
                for c in range(NCH):
                    if first and half == 0:
                        pe.wait_ge(up_c, START + 2 * (2 * FT - 4 + c // 2 + 1))
                    if first and half == 1:
                        pe.wait_ge(dn_ev, START + c + 1)
                    done = product(ps[:, c, :], tuple(t[u][:, c * P:(c + 1) * P] for t in (a_hi, a_lo)),
                                   tuple(t[u][:, :] for t in (d_hi, d_lo)), first, last)
                    if last:
                        done.then_inc(dn_pe, 1)
                if not last:
                    done.then_inc(dn_pe, 1)

            for half in range(2):
                down(half, 0, 0, True, False)
                down(half, 0, 1, False, False)
                with pe.Fori(1, FT // 2 - 1) as i:
                    for u in range(2):
                        down(half, i, u, False, False)
                down(half, FT // 2 - 1, 0, False, False)
                down(half, FT // 2 - 1, 1, False, True)


def kernel(**inputs):
    import concourse.bacc as bacc
    from concourse.bass_utils import run_bass_kernel_spmd

    a = {k: np.asarray(v) for k, v in inputs.items()}

    def cols(v):
        return np.ascontiguousarray(v.reshape(-1, P).T)

    def by_column_tile(w):
        k, n = w.shape
        return np.ascontiguousarray(w.reshape(k // P, P, n // P, P).transpose(2, 1, 0, 3)).reshape(n // P, P, k)

    def by_column_block(w):
        k, n = w.shape
        return np.ascontiguousarray(w.reshape(k // 256, 2, P, n // HALF, HALF).transpose(3, 0, 2, 1, 4))\
            .reshape(n // HALF, k // 256, P, 1024)

    w_in = a["w_in"][0]
    cx_, cb_, cc_, q_, k_, v_, g_, ga_, gb_ = np.split(w_in, np.cumsum([D, D, D, D, D, 2 * D, 2 * D, D]), axis=1)
    conv_tiles = np.stack([by_column_tile(cx_), by_column_tile(cc_), by_column_tile(cb_)], axis=1).reshape(24, P, D)
    gate_tiles = np.stack([by_column_tile(ga_), by_column_tile(a["w_conv_out"][0])], axis=1).reshape(16, P, D)
    ret = a["w_ret_out"][0]
    up = by_column_tile(a["w_ffn_up"][0])
    fw = a["ffn_conv_w"][0].reshape(3, 2 * FT, P).transpose(2, 1, 0).reshape(P, 6 * FT)
    decay = np.concatenate([a["ret_decay_fw"][0], a["ret_decay_bw"][0]])
    vecs = np.concatenate(
        [cols(a["c"][0]), cols(a["c_ctx"]), cols(a["b_ada"][0]), cols(a["norm_mix_pre"][0]), cols(a["norm_mix_post"][0]),
         cols(a["norm_ffn_pre"][0]), cols(a["norm_ffn_post"][0]), cols(a["conv_w"][0]), cols(a["conv_b"][0]), fw,
         cols(a["ffn_conv_b"][0]), np.repeat(decay[None], P, axis=0)], axis=1)
    assert vecs.shape == (P, V_N)

    m, n = np.arange(P)[:, None], np.arange(P)[None, :]
    consts = np.zeros((P, C_N), np.float32)
    consts[:, C_ID:C_ID + P] = np.eye(P)
    consts[:, C_DPOS:C_DPOS + P] = np.maximum(n - m, 0)
    consts[:, C_DNEG:C_DNEG + P] = np.maximum(m - n, 0)
    consts[:, C_GE:C_GE + P] = (n >= m) * K_SCALE
    consts[:, C_LT:C_LT + P] = (n < m) * K_SCALE
    consts[:, C_RF:C_RF + P] = n + 1
    consts[:, C_RB:C_RB + P] = P - n
    consts[:, C_COLF:C_COLF + 4] = np.concatenate([P - 1 - m, CTX - 1 - m, P - 1 - m, 0 * m + P], axis=1)
    consts[:, C_COLB:C_COLB + 4] = np.concatenate([m, m, P + m, 0 * m + P], axis=1)

    pairs = DK // 4
    inv = np.float32(10000.0) ** (-np.arange(pairs, dtype=np.float32) / np.float32(pairs))
    t = np.arange(T)
    ang = np.concatenate([(t // GRID).astype(np.float32)[:, None] * inv, (t % GRID).astype(np.float32)[:, None] * inv], axis=1)
    trig = np.stack([np.cos(ang).T, np.sin(ang).T]).astype(np.float32)

    arrays = {
        "x": a["x"][0],
        "x_t": a["x"][0].T.reshape(KT, P, T),
        "ctx_t": a["ctx"][0].T.reshape(KT, P, CTX).transpose(1, 0, 2),
        "vecs": vecs,
        "consts": consts,
        "trig": np.ascontiguousarray(trig),
        "w_ada_a": a["w_ada"][0][:, :ADA].reshape(KT, P, ADA),
        "w_ada_b": a["w_ada"][0][:, ADA:].reshape(KT, P, HEADS, D).transpose(2, 0, 1, 3),
        "w_n": np.concatenate([by_column_block(k_), by_column_block(v_), by_column_block(g_)]),
        "w_t": np.concatenate([by_column_tile(q_), by_column_tile(k_), conv_tiles, gate_tiles, by_column_tile(gb_)]),
        "w_m": np.concatenate([by_column_tile(ret[:D]), by_column_tile(ret[D:])]),
        "w_o_t": a["w_o"][0].reshape(KT, P, D),
        "w_up_t": np.stack([up[:FT], up[FT:]], axis=1).reshape(2 * FT, P, D),
        "w_dn_t": a["w_ffn_down"][0].reshape(FT, P, D),
    }
    nc = bacc.Bacc("TRN2", target_bir_lowering=False, num_devices=1)
    io = {}
    for name, v in arrays.items():
        arrays[name] = np.ascontiguousarray(v)
        io[name] = nc.dram_tensor(name, arrays[name].shape, mybir.dt.from_np(v.dtype), kind="ExternalInput").ap()
    io["out"] = nc.dram_tensor("out", (T, D), F32, kind="ExternalOutput").ap()
    build(nc, io)
    r = run_bass_kernel_spmd(nc, [arrays], core_ids=[0])
    return r.results[0]["out"].reshape(1, T, D)
```
